# Optimizing a Trainium2 kernel written in Bass

```python
import math
import jax, jax.numpy as jnp
from jax import lax
import numpy as np
import jax
import jax.numpy as jnp

D_MODEL = 1024
BATCH = 1
SEQ = 256
DEPTH = 2

GRID_W = 64
CTX_LEN = 256
EPS = 1e-6
ROPE_THETA = 10000.0
Q_BLOCK = 128
FOURIER_WIDTH = D_MODEL // 4
FOURIER_GROUPS = 4
FOURIER_GROUP_DIM = FOURIER_WIDTH // FOURIER_GROUPS
DIFF_WIDTH = D_MODEL - FOURIER_WIDTH
DIFF_HEAD_DIM = 64
DIFF_V_DIM = 2 * DIFF_HEAD_DIM
DIFF_HEADS = DIFF_WIDTH // DIFF_V_DIM
IN_WIDTH_EVEN = 3 * DIFF_WIDTH + FOURIER_WIDTH
ATTN_SCALE = DIFF_HEAD_DIM ** -0.5
LAMBDA_STD = 0.1
CONV_WIDTH = 31
D_FF = -(-8 * D_MODEL // (3 * 256)) * 256


def rmsnorm(x, g):
    x32 = x.astype(jnp.float32)
    y = x32 * lax.rsqrt(jnp.mean(x32 * x32, axis=-1, keepdims=True) + EPS)
    return (y * g.astype(jnp.float32)).astype(x.dtype)

def layernorm(x, g, b):
    x32 = x.astype(jnp.float32)
    mu = jnp.mean(x32, axis=-1, keepdims=True)
    xc = x32 - mu
    y = xc * lax.rsqrt(jnp.mean(xc * xc, axis=-1, keepdims=True) + EPS)
    return (y * g.astype(jnp.float32) + b.astype(jnp.float32)).astype(x.dtype)

def modulate(h, shift, scale):
    return h * (1 + scale) + shift

def axial_rope_tables(rows_n):
    row = jnp.repeat(jnp.arange(rows_n, dtype=jnp.float32), GRID_W)
    col = jnp.tile(jnp.arange(GRID_W, dtype=jnp.float32), rows_n)
    axis_dim = DIFF_HEAD_DIM // 2
    inv_freq = ROPE_THETA ** (-jnp.arange(0, axis_dim, 2, dtype=jnp.float32) / axis_dim)
    ang = jnp.concatenate([row[:, None] * inv_freq, col[:, None] * inv_freq], axis=-1)
    return jnp.cos(ang), jnp.sin(ang)

def apply_rope(x, cos, sin):
    x1, x2 = jnp.split(x, 2, axis=-1)
    c = cos[:, None, :].astype(x.dtype)
    s = sin[:, None, :].astype(x.dtype)
    return jnp.concatenate([x1 * c - x2 * s, x1 * s + x2 * c], axis=-1)

def rope_heads(q, cos, sin):
    B, S, H, two, d = q.shape
    return apply_rope(q.reshape(B, S, H * two, d), cos, sin).reshape(q.shape)

def diff_attend(q, k, v, lam):
    s = jnp.einsum('bqhcd,bkhcd->bhcqk', q, k, preferred_element_type=jnp.float32) * ATTN_SCALE
    p = jax.nn.softmax(s, axis=-1)
    a = p[:, :, 0] - lam * p[:, :, 1]
    return jnp.einsum('bhqk,bkhe->bqhe', a.astype(v.dtype), v)

def fourier_groups(f, w):
    B, T, _ = f.shape
    fg = f.reshape(B, T, FOURIER_GROUPS, FOURIER_GROUP_DIM).astype(jnp.float32)
    z = jnp.fft.fft2(fg, axes=(1, 3), norm='ortho').real.astype(f.dtype)
    return jnp.einsum('btgc,gce->btge', z, w).reshape(B, T, FOURIER_WIDTH)

def split_proj(u):
    B, T, _ = u.shape
    q, k, v, f = jnp.split(u, [DIFF_WIDTH, 2 * DIFF_WIDTH, 3 * DIFF_WIDTH], axis=-1)
    return (q.reshape(B, T, DIFF_HEADS, 2, DIFF_HEAD_DIM),
            k.reshape(B, T, DIFF_HEADS, 2, DIFF_HEAD_DIM),
            v.reshape(B, T, DIFF_HEADS, DIFF_V_DIM),
            f)

def merge_heads(o, f, subln_g, fourier_w, w_out, lambda_init):
    B, T = o.shape[:2]
    o = (rmsnorm(o, subln_g) * (1.0 - lambda_init)).reshape(B, T, DIFF_WIDTH)
    return jnp.concatenate([o, fourier_groups(f, fourier_w)], axis=-1) @ w_out

def diff_fourier_mixer(h_l, h_c, cos, sin, w_in, lq1, lk1, lq2, lk2, subln_g, fourier_w, w_out,
                       lambda_init, ctx_update):
    B, S, _ = h_l.shape
    q_l, k_l, v_l, f_l = split_proj(h_l @ w_in)
    q_c, k_c, v_c, f_c = split_proj(h_c @ w_in)
    q_l = rope_heads(q_l, cos, sin)
    k_l = rope_heads(k_l, cos, sin)
    lam = (jnp.exp(jnp.sum(lq1.astype(jnp.float32) * lk1.astype(jnp.float32)))
           - jnp.exp(jnp.sum(lq2.astype(jnp.float32) * lk2.astype(jnp.float32))) + lambda_init)
    k_all = jnp.concatenate([k_c, k_l], axis=1)
    v_all = jnp.concatenate([v_c, v_l], axis=1)
    n_blk = S // Q_BLOCK
    q_blocks = jnp.moveaxis(q_l.reshape(B, n_blk, Q_BLOCK, DIFF_HEADS, 2, DIFF_HEAD_DIM), 1, 0)
    o = lax.map(lambda qb: diff_attend(qb, k_all, v_all, lam), q_blocks)
    o_l = jnp.moveaxis(o, 0, 1).reshape(B, S, DIFF_HEADS, DIFF_V_DIM)
    y_l = merge_heads(o_l, f_l, subln_g, fourier_w, w_out, lambda_init)
    y_c = None
    if ctx_update:
        y_c = merge_heads(diff_attend(q_c, k_c, v_c, lam), f_c, subln_g, fourier_w, w_out, lambda_init)
    return y_l, y_c

def depthwise_conv(u, w):
    return lax.conv_general_dilated(
        u, w[:, None, :].astype(u.dtype), window_strides=(1,),
        padding=[(CONV_WIDTH // 2, CONV_WIDTH // 2)],
        dimension_numbers=('NWC', 'WIO', 'NWC'), feature_group_count=u.shape[-1])

def conformer_conv(h, pw1_w, pw1_b, dw_w, dw_b, ln_g, ln_b, pw2_w, pw2_b):
    a, g = jnp.split(h @ pw1_w + pw1_b, 2, axis=-1)
    u = a * jax.nn.sigmoid(g)
    u = depthwise_conv(u, dw_w) + dw_b
    u = jax.nn.silu(layernorm(u, ln_g, ln_b))
    return u @ pw2_w + pw2_b

def swiglu(h, w1, w3, w2):
    return (jax.nn.silu(h @ w1) * (h @ w3)) @ w2

def first_inputs(seed: int = 0) -> dict:
    key = jax.random.key(seed)
    ks = iter(jax.random.split(key, 32))
    n_even = (DEPTH + 1) // 2
    n_odd = DEPTH // 2
    f32 = jnp.float32

    def nrm(shape):
        return jax.random.normal(next(ks), shape, f32)

    def w(shape, fan_in):
        return nrm(shape) * fan_in ** -0.5

    def gain(shape):
        return 1.0 + 0.05 * nrm(shape)

    def bias(shape):
        return 0.02 * nrm(shape)

    D = D_MODEL
    return {
        'x': nrm((BATCH, SEQ, D)),
        'c': nrm((BATCH, D)),
        'ctx': nrm((BATCH, CTX_LEN, D)),
        'c_ctx': nrm((D,)),
        'ada_w': w((DEPTH, D, 6 * D), D),
        'ada_b': bias((DEPTH, 6 * D)),
        'mix_norm_g': gain((DEPTH, D)),
        'ffn_norm_g': gain((DEPTH, D)),
        'ffn_w1': w((DEPTH, D, D_FF), D),
        'ffn_w3': w((DEPTH, D, D_FF), D),
        'ffn_w2': w((DEPTH, D_FF, D), D_FF),
        'ev_w_in': w((n_even, D, IN_WIDTH_EVEN), D),
        'ev_lambda_q1': LAMBDA_STD * nrm((n_even, DIFF_HEAD_DIM)),
        'ev_lambda_k1': LAMBDA_STD * nrm((n_even, DIFF_HEAD_DIM)),
        'ev_lambda_q2': LAMBDA_STD * nrm((n_even, DIFF_HEAD_DIM)),
        'ev_lambda_k2': LAMBDA_STD * nrm((n_even, DIFF_HEAD_DIM)),
        'ev_subln_g': gain((n_even, DIFF_V_DIM)),
        'ev_fourier_w': w((n_even, FOURIER_GROUPS, FOURIER_GROUP_DIM, FOURIER_GROUP_DIM), FOURIER_GROUP_DIM),
        'ev_w_out': w((n_even, D, D), D),
        'od_pw1_w': w((n_odd, D, 2 * D), D),
        'od_pw1_b': bias((n_odd, 2 * D)),
        'od_dw_w': w((n_odd, CONV_WIDTH, D), CONV_WIDTH),
        'od_dw_b': bias((n_odd, D)),
        'od_ln_g': gain((n_odd, D)),
        'od_ln_b': bias((n_odd, D)),
        'od_pw2_w': w((n_odd, D, D), D),
        'od_pw2_b': bias((n_odd, D)),
        'final_g': gain((D,)),
    }

def first_block(x, c, ctx, c_ctx, ada_w, ada_b, mix_norm_g, ffn_norm_g, ffn_w1, ffn_w3, ffn_w2,
              ev_w_in, ev_lambda_q1, ev_lambda_k1, ev_lambda_q2, ev_lambda_k2, ev_subln_g,
              ev_fourier_w, ev_w_out, od_pw1_w, od_pw1_b, od_dw_w, od_dw_b, od_ln_g, od_ln_b,
              od_pw2_w, od_pw2_b, final_g):
    S = x.shape[1]
    ROWS = S // GRID_W
    cos, sin = axial_rope_tables(ROWS)
    silu_c = jax.nn.silu(c)
    silu_cc = jax.nn.silu(c_ctx)
    xc = ctx
    for i in range(DEPTH):
        j = i // 2
        even = i % 2 == 0
        ctx_update = any(k % 2 == 0 for k in range(i + 1, DEPTH))
        read_ctx = even or ctx_update
        mod_l = jnp.split((silu_c @ ada_w[i] + ada_b[i])[:, None, :], 6, axis=-1)
        h_l = modulate(rmsnorm(x, mix_norm_g[i]), mod_l[0], mod_l[1])
        mod_c = None
        h_c = None
        if read_ctx:
            mod_c = jnp.split((silu_cc @ ada_w[i] + ada_b[i])[None, None, :], 6, axis=-1)
            h_c = modulate(rmsnorm(xc, mix_norm_g[i]), mod_c[0], mod_c[1])
        if even:
            lambda_init = 0.8 - 0.6 * math.exp(-0.3 * i)
            y_l, y_c = diff_fourier_mixer(h_l, h_c, cos, sin, ev_w_in[j], ev_lambda_q1[j], ev_lambda_k1[j],
                                          ev_lambda_q2[j], ev_lambda_k2[j], ev_subln_g[j], ev_fourier_w[j],
                                          ev_w_out[j], lambda_init, ctx_update)
        else:
            conv_args = (od_pw1_w[j], od_pw1_b[j], od_dw_w[j], od_dw_b[j], od_ln_g[j], od_ln_b[j],
                         od_pw2_w[j], od_pw2_b[j])
            y_l = conformer_conv(h_l, *conv_args)
            y_c = conformer_conv(h_c, *conv_args) if ctx_update else None
        x = x + mod_l[2] * y_l
        x = x + mod_l[5] * swiglu(modulate(rmsnorm(x, ffn_norm_g[i]), mod_l[3], mod_l[4]),
                                  ffn_w1[i], ffn_w3[i], ffn_w2[i])
        if ctx_update:
            xc = xc + mod_c[2] * y_c
            xc = xc + mod_c[5] * swiglu(modulate(rmsnorm(xc, ffn_norm_g[i]), mod_c[3], mod_c[4]),
                                        ffn_w1[i], ffn_w3[i], ffn_w2[i])
    return rmsnorm(x, final_g)


N_A_LAYERS = DEPTH // 2
N_B_LAYERS = DEPTH - N_A_LAYERS
D_RNN = D_MODEL
RG_HEADS = 4
RG_BLOCK = D_RNN // RG_HEADS
CONV_W = 4
RG_C = 8.0
HEAD_DIM = 128
N_HEADS = D_MODEL // HEAD_DIM
D_ATT = N_HEADS * HEAD_DIM
MOBA_BLOCK = 256
MOBA_TOPK = 3
Q_CHUNK = 16
NEG_INF = -1e30


def _rmsnorm(x, g):
    xf = x.astype(jnp.float32)
    y = xf * lax.rsqrt(jnp.mean(xf * xf, axis=-1, keepdims=True) + EPS)
    return (y * g.astype(jnp.float32)).astype(x.dtype)

def _modulate(h, shift, scale):
    return h * (1.0 + scale[:, None, :]) + shift[:, None, :]

def _lin_combine(left, right):
    a_l, b_l = left
    a_r, b_r = right
    return a_l * a_r, a_r * b_l + b_r

def _block_diag(u, w):
    b, s, _ = u.shape
    ub = u.reshape(b, s, RG_HEADS, RG_BLOCK)
    return jnp.einsum('bshi,hij->bshj', ub, w).reshape(b, s, D_RNN)

def _rglru_mixer(h, w_in, conv_w, conv_b, w_a, b_a, w_x, b_x, lam, w_out):
    u, g = jnp.split(h @ w_in, 2, axis=-1)
    u = lax.conv_general_dilated(
        u, conv_w[:, None, :], window_strides=(1,), padding=[(CONV_W - 1, 0)],
        dimension_numbers=('NWC', 'WIO', 'NWC'), feature_group_count=D_RNN) + conv_b
    r = jax.nn.sigmoid((_block_diag(u, w_a) + b_a).astype(jnp.float32))
    gi = jax.nn.sigmoid((_block_diag(u, w_x) + b_x).astype(jnp.float32))
    log_a = -RG_C * r * jax.nn.softplus(-lam.astype(jnp.float32))
    a = jnp.exp(log_a)
    b_in = jnp.sqrt(-jnp.expm1(2.0 * log_a)) * (gi * u.astype(jnp.float32))
    _, hs = lax.associative_scan(_lin_combine, (a, b_in), axis=1)
    y = hs.astype(h.dtype) * jax.nn.silu(g)
    return y @ w_out

def _shared_kv(x, cs, kv_norm_g, kv_mod_w, kv_mod_b, w_kv):
    b, s, _ = x.shape
    shift, scale = jnp.split(cs @ kv_mod_w + kv_mod_b, 2, axis=-1)
    h = _modulate(_rmsnorm(x, kv_norm_g), shift, scale)
    k, v = jnp.split(h @ w_kv, 2, axis=-1)
    k = k.reshape(b, s, N_HEADS, HEAD_DIM).transpose(0, 2, 1, 3)
    v = v.reshape(b, s, N_HEADS, HEAD_DIM).transpose(0, 2, 1, 3)
    s_pad = -(-s // MOBA_BLOCK) * MOBA_BLOCK
    pad = ((0, 0), (0, 0), (0, s_pad - s), (0, 0))
    k = jnp.pad(k, pad)
    v = jnp.pad(v, pad)
    n_blk = s_pad // MOBA_BLOCK
    k_mean = k.astype(jnp.float32).reshape(b, N_HEADS, n_blk, MOBA_BLOCK, HEAD_DIM).mean(axis=3)
    return k, v, k_mean.astype(k.dtype)

def _moba_attention(q, k, v, k_mean):
    b, nh, s, dh = q.shape
    n = b * nh
    s_pad = k.shape[2]
    n_blk = s_pad // MOBA_BLOCK
    k_sel = min(MOBA_TOPK, n_blk)
    qf = q.reshape(n, s, dh)
    kf = k.reshape(n, s_pad, dh)
    vf = v.reshape(n, s_pad, dh)
    kb = k.reshape(n * n_blk, MOBA_BLOCK, dh)
    vb = v.reshape(n * n_blk, MOBA_BLOCK, dh)
    km = k_mean.reshape(n, n_blk, dh)
    base = (jnp.arange(n, dtype=jnp.int32) * n_blk)[:, None, None]
    blk_ids = jnp.arange(n_blk, dtype=jnp.int32)
    sm_scale = dh ** -0.5

    def one_chunk(ci):
        q0 = ci * Q_CHUNK
        blk = q0 // MOBA_BLOCK
        qc = lax.dynamic_slice_in_dim(qf, q0, Q_CHUNK, axis=1)
        gate = jnp.einsum('nqd,nbd->nqb', qc, km).astype(jnp.float32)
        gate = jnp.where(blk_ids < blk, gate, NEG_INF)
        _, idx = lax.top_k(gate, k_sel)
        valid = idx < blk
        kg = kb[base + idx]
        vg = vb[base + idx]
        s_sel = jnp.einsum('nqd,nqkld->nqkl', qc, kg).astype(jnp.float32) * sm_scale
        s_sel = jnp.where(valid[..., None], s_sel, NEG_INF).reshape(n, Q_CHUNK, k_sel * MOBA_BLOCK)
        k_own = lax.dynamic_slice_in_dim(kf, blk * MOBA_BLOCK, MOBA_BLOCK, axis=1)
        v_own = lax.dynamic_slice_in_dim(vf, blk * MOBA_BLOCK, MOBA_BLOCK, axis=1)
        s_own = jnp.einsum('nqd,nld->nql', qc, k_own).astype(jnp.float32) * sm_scale
        q_pos = q0 + jnp.arange(Q_CHUNK, dtype=jnp.int32)
        k_pos = blk * MOBA_BLOCK + jnp.arange(MOBA_BLOCK, dtype=jnp.int32)
        s_own = jnp.where(k_pos[None, None, :] <= q_pos[None, :, None], s_own, NEG_INF)
        p = jax.nn.softmax(jnp.concatenate([s_sel, s_own], axis=-1), axis=-1).astype(v.dtype)
        p_sel = p[..., :k_sel * MOBA_BLOCK].reshape(n, Q_CHUNK, k_sel, MOBA_BLOCK)
        p_own = p[..., k_sel * MOBA_BLOCK:]
        return (jnp.einsum('nqkl,nqkld->nqd', p_sel, vg)
                + jnp.einsum('nql,nld->nqd', p_own, v_own))

    out = lax.map(one_chunk, jnp.arange(s // Q_CHUNK, dtype=jnp.int32))
    return out.transpose(1, 0, 2, 3).reshape(b, nh, s, dh)

def _moba_mixer(h, k, v, k_mean, w_in, w_out):
    b, s, _ = h.shape
    q, g = jnp.split(h @ w_in, 2, axis=-1)
    q = q.reshape(b, s, N_HEADS, HEAD_DIM).transpose(0, 2, 1, 3)
    o = _moba_attention(q, k, v, k_mean).transpose(0, 2, 1, 3).reshape(b, s, D_ATT)
    return (o * jax.nn.silu(g)) @ w_out

def second_inputs(seed: int = 0) -> dict:
    key = jax.random.key(seed)
    ks = jax.random.split(key, 24)
    f32 = jnp.float32

    def nrm(k, shape, scale):
        return scale * jax.random.normal(k, shape, f32)

    a0 = jax.random.uniform(ks[12], (N_A_LAYERS, D_RNN), f32, 0.9, 0.999)
    s0 = a0 ** (1.0 / RG_C)
    return {
        'x': nrm(ks[0], (BATCH, SEQ, D_MODEL), 1.0),
        'c': nrm(ks[1], (BATCH, D_MODEL), 1.0),
        'mod_w': nrm(ks[2], (DEPTH, D_MODEL, 3 * D_MODEL), 0.5 * D_MODEL ** -0.5),
        'mod_b': nrm(ks[3], (DEPTH, 3 * D_MODEL), 0.02),
        'norm_g': 1.0 + nrm(ks[4], (DEPTH, D_MODEL), 0.02),
        'rg_w_in': nrm(ks[5], (N_A_LAYERS, D_MODEL, 2 * D_RNN), D_MODEL ** -0.5),
        'rg_conv_w': nrm(ks[6], (N_A_LAYERS, CONV_W, D_RNN), CONV_W ** -0.5),
        'rg_conv_b': nrm(ks[7], (N_A_LAYERS, D_RNN), 0.01),
        'rg_w_a': nrm(ks[8], (N_A_LAYERS, RG_HEADS, RG_BLOCK, RG_BLOCK), RG_BLOCK ** -0.5),
        'rg_b_a': nrm(ks[9], (N_A_LAYERS, D_RNN), 0.01),
        'rg_w_x': nrm(ks[10], (N_A_LAYERS, RG_HEADS, RG_BLOCK, RG_BLOCK), RG_BLOCK ** -0.5),
        'rg_b_x': nrm(ks[11], (N_A_LAYERS, D_RNN), 0.01),
        'rg_lambda': jnp.log(s0) - jnp.log1p(-s0),
        'rg_w_out': nrm(ks[13], (N_A_LAYERS, D_RNN, D_MODEL), D_RNN ** -0.5),
        'kv_norm_g': 1.0 + nrm(ks[14], (D_MODEL,), 0.02),
        'kv_mod_w': nrm(ks[15], (D_MODEL, 2 * D_MODEL), 0.5 * D_MODEL ** -0.5),
        'kv_mod_b': nrm(ks[16], (2 * D_MODEL,), 0.02),
        'w_kv': nrm(ks[17], (D_MODEL, 2 * D_ATT), D_MODEL ** -0.5),
        'att_w_in': nrm(ks[18], (N_B_LAYERS, D_MODEL, 2 * D_ATT), D_MODEL ** -0.5),
        'att_w_out': nrm(ks[19], (N_B_LAYERS, D_ATT, D_MODEL), D_ATT ** -0.5),
        'final_norm_g': 1.0 + nrm(ks[20], (D_MODEL,), 0.02),
    }

def second_block(x, c, mod_w, mod_b, norm_g, rg_w_in, rg_conv_w, rg_conv_b, rg_w_a, rg_b_a,
              rg_w_x, rg_b_x, rg_lambda, rg_w_out, kv_norm_g, kv_mod_w, kv_mod_b, w_kv,
              att_w_in, att_w_out, final_norm_g):
    cs = jax.nn.silu(c)
    k_sh = v_sh = km_sh = None
    for layer in range(DEPTH):
        shift, scale, gate = jnp.split(cs @ mod_w[layer] + mod_b[layer], 3, axis=-1)
        h = _modulate(_rmsnorm(x, norm_g[layer]), shift, scale)
        if layer < N_A_LAYERS:
            i = layer
            y = _rglru_mixer(h, rg_w_in[i], rg_conv_w[i], rg_conv_b[i], rg_w_a[i], rg_b_a[i],
                             rg_w_x[i], rg_b_x[i], rg_lambda[i], rg_w_out[i])
        else:
            if layer == N_A_LAYERS:
                k_sh, v_sh, km_sh = _shared_kv(x, cs, kv_norm_g, kv_mod_w, kv_mod_b, w_kv)
            i = layer - N_A_LAYERS
            y = _moba_mixer(h, k_sh, v_sh, km_sh, att_w_in[i], att_w_out[i])
        x = x + gate[:, None, :] * y
    return _rmsnorm(x, final_norm_g)


def setup_inputs(seed=0):
    out = dict(first_inputs(seed))
    for name, value in second_inputs(seed + 1).items():
        if name != "x":
            out[name + "_2"] = value
    return out


def reference(
    x, c, ctx, c_ctx, ada_w, ada_b, mix_norm_g, ffn_norm_g, ffn_w1, ffn_w3, ffn_w2, ev_w_in,
    ev_lambda_q1, ev_lambda_k1, ev_lambda_q2, ev_lambda_k2, ev_subln_g, ev_fourier_w, ev_w_out,
    od_pw1_w, od_pw1_b, od_dw_w, od_dw_b, od_ln_g, od_ln_b, od_pw2_w, od_pw2_b, final_g, c_2,
    mod_w_2, mod_b_2, norm_g_2, rg_w_in_2, rg_conv_w_2, rg_conv_b_2, rg_w_a_2, rg_b_a_2,
    rg_w_x_2, rg_b_x_2, rg_lambda_2, rg_w_out_2, kv_norm_g_2, kv_mod_w_2, kv_mod_b_2, w_kv_2,
    att_w_in_2, att_w_out_2, final_norm_g_2,
):
    x = first_block(
        x, c, ctx, c_ctx, ada_w, ada_b, mix_norm_g, ffn_norm_g, ffn_w1, ffn_w3, ffn_w2, ev_w_in,
        ev_lambda_q1, ev_lambda_k1, ev_lambda_q2, ev_lambda_k2, ev_subln_g, ev_fourier_w,
        ev_w_out, od_pw1_w, od_pw1_b, od_dw_w, od_dw_b, od_ln_g, od_ln_b, od_pw2_w, od_pw2_b,
        final_g,
    )
    return second_block(
        x, c_2, mod_w_2, mod_b_2, norm_g_2, rg_w_in_2, rg_conv_w_2, rg_conv_b_2, rg_w_a_2,
        rg_b_a_2, rg_w_x_2, rg_b_x_2, rg_lambda_2, rg_w_out_2, kv_norm_g_2, kv_mod_w_2,
        kv_mod_b_2, w_kv_2, att_w_in_2, att_w_out_2, final_norm_g_2,
    )


_drawn_inputs = setup_inputs


def setup_inputs(seed=0):
    import zlib

    import numpy as np

    out = dict(_drawn_inputs(seed))
    spreads = {}
    factors = {'ev_lambda_q2': 8.0,
     'od_pw1_b': 8.0,
     'od_dw_b': 6.042,
     'od_ln_g': 3.55,
     'od_ln_b': 7.726,
     'od_pw2_b': 5.187,
     'norm_g_2': 5.685,
     'rg_conv_b_2': 7.574,
     'rg_b_a_2': 8.0,
     'rg_b_x_2': 8.0,
     'kv_norm_g_2': 8.0,
     'kv_mod_b_2': 8.0,
     'final_norm_g_2': 2.795}
    for name, (base, spread) in spreads.items():
        noise = np.random.default_rng([zlib.crc32(name.encode()), seed]).standard_normal(out[name].shape)
        drawn = base * np.exp(spread * noise) if base else spread * noise
        out[name] = jnp.asarray(drawn.astype(out[name].dtype))
    for name, factor in factors.items():
        out[name] = (out[name] * factor).astype(out[name].dtype)
    return out
```

```python
from contextlib import ExitStack

import concourse.bass as bass
from concourse import mybir

F32 = mybir.dt.float32
R32 = mybir.dt.float32r
BF16 = mybir.dt.bfloat16
ALU = mybir.AluOpType
ACT = mybir.ActivationFunctionType
AX_X = mybir.AxisListType.X

P = 128
D = 1024
KT = D // P
S = 256
NT = S // P
EPS = 1e-6
D_FF = 2816
DIFF_W = 768
HEADS = DIFF_W // P
KEYS = 2 * S
SUB_SCALE = 1.0 - 0.2
CONV = 31
PAD = CONV // 2
RG_CONV = 4
RG_C = 8.0
A_HEADS = 8

UNIT = 2048
N_LAND = 6
N_SPLIT = 3
N_ALAND = 2
ADA0 = 8
FCH = D_FF // 256
NEG = -1e30

V_MOD0, V_MOD1, V_KV = 12, 15, 18
JOBS = [2, 3, 4, 5, 11, 6, 7, 8, 9, 10, 12, 13, 14, 15, 16, 17, 18, 19]

STAGES = [("in", 10), ("out", 4), ("ffn0", 3 * FCH), ("pw1", 8), ("pw2", 4), ("ffn1", 3 * FCH),
          ("rg_in", 8), ("rg_out", 4), ("kv", 8), ("att_in", 8), ("att_out", 4)]
BASE = {}
_n = 0
for _name, _count in STAGES:
    BASE[_name] = _n
    _n += _count
UNITS = _n

ROW_GROUPS = [
    [("ada_b", 96), ("c", 8), ("c_ctx", 8), ("c_2", 8), ("final_g", 8)],
    [("mod_b_2", 48), ("kv_mod_b_2", 16), ("mix_norm_g", 16), ("ffn_norm_g", 16), ("norm_g_2", 16),
     ("kv_norm_g_2", 8), ("final_norm_g_2", 8)],
    [("od_pw1_b", 16), ("od_dw_b", 8), ("od_ln_g", 8), ("od_ln_b", 8), ("od_pw2_b", 8),
     ("rg_conv_b_2", 8), ("rg_b_a_2", 8), ("rg_b_x_2", 8), ("rg_lambda_2", 8), ("rg_conv_w_2", 32),
     ("ev_subln_g", 1)],
    [("od_dw_w_a", 16 * 8)],
    [("od_dw_w_b", 15 * 8)],
]
COL = {}
for _g, _rows in enumerate(ROW_GROUPS):
    _r = 0
    for _name, _count in _rows:
        COL[_name] = _g * P + _r
        _r += _count

NORMED = {"ss": NT, "ms": 1, "rstd": 1, "xn": NT, "tr": 2 * KT, "full": KT, "hi": KT, "lo": KT}
SPLIT = {"full": KT, "hi": KT, "lo": KT}
RESCALED = {"ss": NT, "ms": 1, "rstd": 1, "xn": NT}
GATED = {"diag": 1, "gmm": 1, "gate": 2}
STEPS = [("n_x", NORMED), ("n_ctx", NORMED),
         ("sub", {"ss": 12, "ms": 1, "rstd": 1, "xn": NT, "tr": 2 * HEADS, "full": HEADS, "hi": HEADS, "lo": HEADS}),
         ("out", GATED), ("n_ffn0", NORMED), ("ffn0", GATED), ("n_pw1", NORMED), ("ln", SPLIT), ("pw2", GATED),
         ("pw2b", GATED), ("n_ffn1", NORMED), ("ffn1", GATED), ("n_final", RESCALED), ("final", GATED),
         ("n_rg", NORMED), ("rg", SPLIT), ("rg_out", GATED), ("n_kv", NORMED), ("n_att", {"tr": 2 * KT, **SPLIT}),
         ("ao", {"tr": 2 * KT, "hi": KT, "lo": KT}), ("att_out", GATED), ("n_last", RESCALED), ("last", GATED)]
STEPS_BEFORE = {}
_seen = {}
for _stage, _adds in STEPS:
    for _kind, _count in _adds.items():
        STEPS_BEFORE[_kind, _stage] = _seen.get(_kind, 0)
        _seen[_kind] = _seen.get(_kind, 0) + _count


def at(base, i=None, step=0):
    return base if i is None else i * step + base


def build(nc, t_in, out):
    with ExitStack() as ctx:
        sems = {}

        def sem(name):
            if name not in sems:
                sems[name] = ctx.enter_context(nc.semaphore(name))
            return sems[name]

        def seen(kind, stage, n):
            return sem(kind), STEPS_BEFORE[kind, stage] + n

        ARENA = 16512

        def place(name, shape, offset, dtype=F32):
            return nc.alloc_sbuf_tensor_at(name, shape, dtype, offset=ARENA + offset)

        KB = 1024
        w_land = [place(f"w_land{i}", [P, UNIT], 8 * KB * i) for i in range(N_LAND)]
        w_hi = [place(f"w_hi{i}", [P, UNIT], (48 + 8 * i) * KB, R32) for i in range(N_SPLIT)]
        w_lo = [place(f"w_lo{i}", [P, UNIT], (72 + 8 * i) * KB, R32) for i in range(N_SPLIT)]
        a_land = [place(f"a_land{i}", [P, UNIT], (96 + 8 * i) * KB) for i in range(N_ALAND)]
        job_sum = place("job_sum", [P, D], 112 * KB)
        BIG = 116 * KB
        xT_hi = place("xT_hi", [P, KT, S], 164 * KB, R32)
        xT_lo = place("xT_lo", [P, KT, S], 172 * KB, R32)
        x = place("x", [P, NT, D], 180 * KB)
        S1 = 188 * KB
        xn = place("xn", [P, NT, D], S1)
        xfull = place("xfull", [P, KT, S], S1)
        gate = place("gate", [P, D], 196 * KB)
        SMALL = [200 * KB]

        def small(name, shape):
            size = 4
            for n in shape[1:]:
                size *= n
            offset = SMALL[0]
            SMALL[0] += -(-size // 32) * 32
            assert ARENA + SMALL[0] <= 229344
            return place(name, shape, offset)

        ident = small("ident", [P, P])
        ones = small("ones", [P, P])
        pcol = small("pcol", [P, 5 * P])
        mcol = small("mcol", [P, 20 * KT])
        mcol_ctx = small("mcol_ctx", [P, 2 * KT])
        silu_c = small("silu_c", [P, 3, KT])
        mask = small("mask", [P, P])
        rope = small("rope", [P, NT, 2, 32])
        a_col = small("a_col", [P, KT])
        b_col = small("b_col", [P, KT])
        ss = small("ss", [P, 12])
        ms = small("ms", [P, 12])
        rstd = small("rstd", [P, 12])
        neg_half = small("neg_half", [P, 12])
        lam_tmp = small("lam_tmp", [P, 8])
        mx = small("mx", [P, 2, 2])
        nb = small("nb", [P, 2, 2])
        esum = small("esum", [P, 2, 2])
        rsum = small("rsum", [P, 2, 2])
        sp_c = small("sp_c", [P, 8, KT])
        zeros = small("zeros", [P, 256]).bitcast(BF16)
        prow = place("prow", [P, 5, P], 112 * KB)
        ctx_x = place("ctx_x", [P, NT, D], BIG)
        ctx_full = place("ctx_full", [P, KT, S], BIG)
        ada_rows = place("ada_rows", [2, 2 * D], BIG + 8 * KB)
        ctx_junk = place("ctx_junk", [P, NT, D], BIG + 18 * KB)
        lam_in = place("lam_in", [P, 4, 64], BIG + 16 * KB)
        lam_junk = place("lam_junk", [P, 2, 64], BIG + 17 * KB)
        ctxT_hi = place("ctxT_hi", [P, KT, S], BIG + 32 * KB, R32)
        ctxT_lo = place("ctxT_lo", [P, KT, S], BIG + 40 * KB, R32)
        qT = place("qT", [P, HEADS, S], BIG)
        kT = place("kT", [P, HEADS, KEYS], BIG + 6 * KB)
        v_tok = place("v_tok", [P, 4, DIFF_W], BIG + 18 * KB)
        f_tok = place("f_tok", [P, NT, S], BIG + 30 * KB)
        rope_cos = place("rope_cos", [P, 512], 196 * KB)
        rope_sin = place("rope_sin", [P, 512], 198 * KB)
        rot = place("rot", [P, 2, 512], S1)
        k_ctx = place("k_ctx", [P, 2, 512], S1 + 4 * KB)
        prob = place("prob", [P, 2, 2, 512], BIG + 32 * KB)
        diff = place("diff", [P, 2, 512], BIG + 40 * KB)
        diffT = place("diffT", [P, 2, 4, P], BIG + 44 * KB)
        o_tok = place("o_tok", [P, NT, DIFF_W], S1)
        o_full = place("o_full", [P, HEADS, S], S1)
        dft = place("dft", [P, NT, 512], 196 * KB)
        ftT = place("ftT", [P, 2, 512], 112 * KB)
        four_c = place("four_c", [P, 2, P], 96 * KB)
        four_w = place("four_w", [P, 2, P], 97 * KB)
        four_g = place("four_g", [P, 2, 2, P], 98 * KB)
        sq_junk = place("sq_junk", [P, 2, P], S1 + 6 * KB)
        silu_g = place("silu_g", [P, NT, 256], BIG)
        hid = place("hid", [P, NT, 256], BIG + 2 * KB)
        hT_hi = place("hT_hi", [P, 2, S], BIG + 4 * KB, R32)
        hT_lo = place("hT_lo", [P, 2, S], BIG + 6 * KB, R32)
        UP = S + 2 * PAD
        u_pad = place("u_pad", [P, KT, UP], BIG)
        conv = place("conv", [P, KT, S], BIG + 9 * KB)
        ag_tok = place("ag_tok", [P, NT, 512], BIG + 17 * KB)
        sig = place("sig", [P, 2, S], BIG + 21 * KB)
        csq = place("csq", [P, KT, S], BIG + 23 * KB)
        mean = place("mean", [P, S], BIG + 31 * KB)
        rln = place("rln", [P, S], BIG + 32 * KB)
        nhalf_row = place("nhalf_row", [P, S], BIG + 33 * KB)
        bias_gate = place("bias_gate", [P, D], BIG + 34 * KB)
        RUP = S + RG_CONV - 1
        ru_pad = place("ru_pad", [P, KT, RUP], BIG)
        gT = place("gT", [P, KT, S], BIG + 9 * KB)
        rg_tok = place("rg_tok", [P, NT, 512], BIG + 17 * KB)
        uc = place("uc", [P, KT, S], BIG + 21 * KB)
        r_gate = place("r_gate", [P, KT, S], BIG + 29 * KB)
        i_gate = place("i_gate", [P, KT, S], BIG + 37 * KB)
        a_seq = place("a_seq", [P, KT, S], BIG)
        y_full = place("y_full", [P, KT, S], S1)
        akT = place("akT", [P, KT, S], BIG)
        aqT = place("aqT", [P, KT, S], BIG + 8 * KB)
        av = place("av", [P, NT, D], BIG + 16 * KB)
        ag = place("ag", [P, NT, D], BIG + 24 * KB)
        a_tok = place("a_tok", [P, NT, 512], BIG + 32 * KB)
        ap_ = place("ap_", [P, 2, S], BIG + 36 * KB)
        apT = place("apT", [P, 2, NT, P], BIG + 38 * KB)
        ao = place("ao", [P, NT, D], BIG + 40 * KB)
        kv_full = place("kv_full", [P, KT, S], BIG + 40 * KB)
        tmp = place("tmp", [P, 2, 512], S1)

        bank = [ctx.enter_context(nc.psum_tensor(f"bank{i}", [P, 512], F32)) for i in range(8)]
        COLS = bank[7]

        landed = [sem(f"w_landed{i}") for i in range(N_LAND)]
        a_landed = [sem(f"a_landed{i}") for i in range(N_ALAND)]
        s_hi, s_lo, s_used = sem("w_hi"), sem("w_lo"), sem("w_used")
        s_step, s_red, s_cols = sem("job_step"), sem("job_reduced"), sem("job_cols")

        def kview(w, n=None):
            return w.rearrange("(k p) n -> p k n", p=P)

        def pc(name, k=0, n=1):
            return pcol[:, COL[name] + k:COL[name] + k + n]

        def mc(v, k=0, n=KT):
            return mcol[:, v * KT + k:v * KT + k + n]

        block = ctx.enter_context(nc.Block())

        @block.sync
        def _(sp):
            def load_unit(u, parts, i=None):
                n = u + ADA0
                if n >= N_LAND:
                    if n - N_LAND < ADA0:
                        sp.wait_ge(sem("ada0_used"), n - N_LAND + 1)
                    else:
                        sp.wait_ge(s_lo, at(n - N_LAND - ADA0 + 1, i, 6))
                slot = n % N_LAND
                for view, src in parts(w_land[slot]):
                    sp.dma_start(view, src).then_inc(landed[slot], 16)

            def cols_half(w, col, j):
                def parts(land):
                    v = land[:, :].rearrange("p (k n) -> p k n", k=4)
                    return [(v[:, 2 * h:2 * h + 2, :],
                             kview(w)[:, 4 * j + 2 * h:4 * j + 2 * h + 2, bass.ds(col, 512)]) for h in range(2)]
                return parts

            def cols_pair(wa, ca, wb, cb, j):
                def parts(land):
                    v = land[:, :].rearrange("p (k n) -> p k n", k=4)
                    return [(v[:, :, 256 * h:256 * h + 256], kview(w)[:, 4 * j:4 * j + 4, bass.ds(c, 256)])
                            for h, (w, c) in enumerate(((wa, ca), (wb, cb)))]
                return parts

            def rows_pair(w, row, col=0):
                def parts(land):
                    v = land[:, :].rearrange("p (k n) -> p k n", k=2)
                    return [(v[:, h, :], w[bass.ds(row + h * P, P), col:col + D]) for h in range(2)]
                return parts

            ada = t_in["ada_w"]
            w_in = t_in["ev_w_in"][0]

            def rows(name, src, n, g, r):
                sp.dma_start(prow[r:r + n, g, :], src).then_inc(sem(f"prow{g}"), 16)

            def as_rows(name):
                h = t_in[name]
                if len(h.shape) == 1:
                    return h.rearrange("(r p) -> r p", p=P)
                if len(h.shape) == 3:
                    h = h[0]
                return h.rearrange("a (r p) -> (a r) p", p=P)

            def load_rows(g):
                r = 0
                for name, n in ROW_GROUPS[g]:
                    if name == "od_dw_w_a":
                        src = as_rows("od_dw_w")[0:n, :]
                    elif name == "od_dw_w_b":
                        src = as_rows("od_dw_w")[P:P + n, :]
                    else:
                        src = as_rows(name)
                    rows(name, src, n, g, r)
                    r += n

            sp.dma_start(ident[:, :], t_in["k_ident"]).then_inc(sem("ident_in"), 16)
            load_rows(0)
            sp.dma_start(x[:, :, :], t_in["x"][0].rearrange("(t p) d -> p t d", p=P)).then_inc(sem("x_in"), 16)
            for n in range(4):
                load_unit(n - ADA0, rows_pair(ada[0], n * 256))
            load_rows(1)
            for n in range(4, 6):
                load_unit(n - ADA0, rows_pair(ada[0], (n - 4) * 256, D))
            sp.dma_start(ctx_x[:, :, :], t_in["ctx"][0].rearrange("(t p) d -> p t d", p=P)).then_inc(sem("ctx_in"), 16)
            for g in (2, 3, 4):
                load_rows(g)
            sp.dma_start(rope[:, :, :, :], t_in["k_rope"].rearrange("(t p) c d -> p t c d", p=P)).then_inc(sem("rope_in"), 16)
            sp.dma_start(mask[:, :], t_in["k_mask"]).then_inc(sem("mask_in"), 16)
            for n, name in enumerate(("ev_lambda_q1", "ev_lambda_k1", "ev_lambda_q2", "ev_lambda_k2")):
                sp.dma_start(lam_in[:, n, :], t_in[name][0:1, :].broadcast_to([P, 64])).then_inc(sem("lam_in"), 16)
            for n in range(6, ADA0):
                load_unit(n - ADA0, rows_pair(ada[0], (n - 4) * 256, D))

            in_cols = [lambda j: cols_half(w_in, 0, j), lambda j: cols_pair(w_in, 512, w_in, 3 * DIFF_W, j),
                       lambda j: cols_half(w_in, 768, j), lambda j: cols_half(w_in, 1280, j),
                       lambda j: cols_half(w_in, 1792, j)]
            for c in range(5):
                for j in range(2):
                    load_unit(2 * c + j, in_cols[c](j))

            def load_dense(stage, w, n_cols):
                for c in range(n_cols // 512):
                    for j in range(2):
                        load_unit(BASE[stage] + 2 * c + j, cols_half(w, 512 * c, j))

            def load_ffn(layer, loops):
                w1, w3, w2 = (t_in[n][layer] for n in ("ffn_w1", "ffn_w3", "ffn_w2"))
                base = BASE[f"ffn{layer}"]
                for j in range(2):
                    load_unit(base + j, cols_pair(w1, 0, w3, 0, j))
                done = 0
                for n in loops:
                    with sp.Fori(0, n) as i:
                        for b in range(2):
                            u = base + 2 + 6 * done + 3 * b
                            c = 1 + 2 * done + b
                            for j in range(2):
                                load_unit(u + j, cols_pair(w1, i * 512 + 256 * c, w3, i * 512 + 256 * c, j), i)
                            load_unit(u + 2, rows_pair(w2, i * 512 + 256 * (c - 1)), i)
                    done += n
                load_unit(base + 3 * FCH - 1, rows_pair(w2, 256 * (FCH - 1)))

            load_dense("out", t_in["ev_w_out"][0], D)
            load_ffn(0, (5,))

            def load_pairs(stage, w):
                for c in range(4):
                    for j in range(2):
                        load_unit(BASE[stage] + 2 * c + j, cols_pair(w, 256 * c, w, D + 256 * c, j))

            load_pairs("pw1", t_in["od_pw1_w"][0])
            load_dense("pw2", t_in["od_pw2_w"][0], D)
            load_ffn(1, (5,))
            load_pairs("rg_in", t_in["rg_w_in_2"][0])
            load_dense("rg_out", t_in["rg_w_out_2"][0], D)
            load_dense("kv", t_in["w_kv_2"], 2 * D)
            load_dense("att_in", t_in["att_w_in_2"][0], 2 * D)
            load_dense("att_out", t_in["att_w_out_2"][0], D)
            for t in range(NT):
                sp.wait_ge(sem("result"), t + 1)
                sp.dma_start(out[0, t * P:(t + 1) * P, :], xn[:, t, :]).then_inc(sem("stored"), 16)
            sp.wait_ge(sem("stored"), 16 * NT)

        @block.gpsimd
        def _(pool):
            pool.memset(ones[:, :], 1.0).then_inc(sem("ones"), 1)
            pool.memset(neg_half[:, :], -0.5).then_inc(sem("ones"), 1)
            pool.memset(zeros[:, :], 0.0).then_inc(sem("zeros"), 1)
            pool.wait_ge(sem("ones"), 2)

            def pow_half(stage, n):
                pool.wait_ge(*seen("ms", stage, 1))
                pool.tensor_tensor(rstd[:, 0:n], ms[:, 0:n], neg_half[:, 0:n], ALU.pow).then_inc(sem("rstd"), 1)

            def load_job(q, w, col, units=range(4), i=None):
                for j in units:
                    a = 4 * q + j
                    if a >= N_ALAND:
                        pool.wait_ge(s_step, at(2 * (a - N_ALAND) + 2, i, 8))
                    pool.dma_start(a_land[j % 2][:, :].rearrange("p (k n) -> p k n", k=2),
                                   kview(w)[:, 2 * j:2 * j + 2, bass.ds(col, D)]).then_inc(a_landed[j % 2], 16)

            ada = [t_in["ada_w"][n] for n in range(2)]
            mod = [t_in["mod_w_2"][n] for n in range(2)]

            pow_half("n_x", NT)
            pow_half("n_ctx", NT)
            for q in range(3):
                load_job(q, ada[0], (q + 2) * D)
            load_job(3, ada[0], 5 * D, range(2))
            pool.wait_ge(sem("rot"), 16)
            pool.dma_start(dft[:, :, :], t_in["k_dft"].rearrange("(t p) n -> p t n", p=P)).then_inc(sem("dft_in"), 16)
            load_job(3, ada[0], 5 * D, range(2, 4))
            pool.wait_ge(s_step, 8 * 4)
            pool.dma_start(four_c[:, :, :], t_in["k_dft64"].rearrange("c p n -> p c n")).then_inc(sem("four_in"), 16)
            pool.memset(four_w[:, :, :], 0.0).then_inc(sem("four_zero"), 1)
            pool.wait_ge(sem("four_zero"), 1)
            for g in range(4):
                r = 64 * (g % 2)
                pool.dma_start(four_w[r:r + 64, g // 2, r:r + 64], t_in["ev_fourier_w"][0, g]).then_inc(sem("four_in"), 16)
            pow_half("sub", 12)
            pool.wait_ge(sem("four_y"), 1)
            load_job(4, ada[1], 5 * D, range(2))
            pow_half("n_ffn0", NT)
            load_job(4, ada[1], 5 * D, range(2, 4))
            with pool.Fori(0, 5) as i:
                load_job(5, ada[1], i * D, range(4), i)
            load_job(10, mod[0], 0, range(2))
            pow_half("n_pw1", NT)
            pool.wait_ge(sem("xres"), 8)
            pool.memset(u_pad[:, :, 0:PAD], 0.0).then_inc(sem("u_zero"), 1)
            pool.memset(u_pad[:, :, PAD + S:UP], 0.0).then_inc(sem("u_zero"), 1)
            pool.memset(nhalf_row[:, :], -0.5).then_inc(sem("nhalf_row"), 1)
            load_job(10, mod[0], 0, range(2, 4))
            load_job(11, mod[0], D)
            load_job(12, mod[0], 2 * D, range(2))
            pool.wait_ge(sem("nhalf_row"), 1)
            pool.wait_ge(sem("ln_ms"), 1)
            pool.tensor_tensor(rln[:, :], rln[:, :], nhalf_row[:, :], ALU.pow).then_inc(sem("ln_rstd"), 1)
            pow_half("n_ffn1", NT)
            load_job(12, mod[0], 2 * D, range(2, 4))
            with pool.Fori(0, 3) as i:
                load_job(13, mod[1], i * D, range(4), i)
            with pool.Fori(0, 2) as i:
                load_job(16, t_in["kv_mod_w_2"], i * D, range(4), i)
            pool.wait_ge(s_step, 8 * len(JOBS))
            for n, name in enumerate(("rg_w_a_2", "rg_w_x_2")):
                pool.dma_start(a_land[n][:, :].rearrange("p (h k j) -> p h k j", h=4, k=2),
                               t_in[name][0].rearrange("h (k p) j -> p h k j", p=P)).then_inc(a_landed[n], 16)
            pow_half("n_final", NT)
            pow_half("n_rg", NT)
            pool.wait_ge(sem("xres"), 16)
            pool.memset(ru_pad[:, :, 0:RG_CONV - 1], 0.0).then_inc(sem("ru_zero"), 1)
            pow_half("n_kv", NT)
            pow_half("n_last", NT)

        @block.scalar
        def _(act):
            def split_hi(u, i=None):
                if u >= UNITS:
                    return
                n = u + ADA0
                act.wait_ge(landed[n % N_LAND], at(32 * (n // N_LAND + 1), i, 32))
                if u >= N_SPLIT:
                    act.wait_ge(s_used, at(u - N_SPLIT + 1, i, 6))
                act.activation(w_hi[u % N_SPLIT][:, :], w_land[n % N_LAND][:, :], ACT.Copy).then_inc(s_hi, 1)

            def norm_square(stage, src, junk):
                for t in range(NT):
                    act.activation(junk[:, t, :], src[:, t, :], ACT.Square,
                                   accum_out=ss[:, t:t + 1]).then_inc(sem("ss"), 1)

            def full_hi(stage, full, hi, ks=range(KT)):
                for n, k in enumerate(ks):
                    act.wait_ge(*seen("full", stage, n + 1))
                    act.activation(hi[:, k, :], full[:, k, :], ACT.Copy).then_inc(sem("hi"), 1)

            def gate_copy(stage, dst=None):
                dst = gate if dst is None else dst
                act.wait_ge(*seen("gmm", stage, 1))
                for h in range(2):
                    act.activation(dst[:, 512 * h:512 * h + 512], bank[4 + h][:, :], ACT.Copy).then_inc(sem("gate"), 1)

            act.wait_ge(sem("cols_in"), 1)
            act.activation(silu_c[:, :, :], pcol[:, COL["c"]:COL["c"] + 24].rearrange("p (c k) -> p c k", c=3),
                           ACT.Silu).then_inc(sem("silu_c"), 1)
            act.wait_ge(sem("x_in"), 16)
            norm_square("n_x", x, xn)
            act.wait_ge(sem("ctx_in"), 16)
            act.wait_ge(*seen("rstd", "n_x", 1))
            norm_square("n_ctx", ctx_x, ctx_junk)
            act.wait_ge(sem("ada0_used"), ADA0)
            for n in range(4):
                act.activation(ada_rows[:, 512 * n:512 * n + 512], bank[n][0:2, :], ACT.Copy).then_inc(sem("ada0_rows"), 1)
            act.wait_ge(sem("lam_dot"), 2)
            act.activation(lam_tmp[:, 2:4], lam_tmp[:, 0:2], ACT.Exp).then_inc(sem("lam_exp"), 1)
            split_hi(0)
            split_hi(1)
            full_hi("n_x", xfull, xT_hi)
            full_hi("n_ctx", ctx_full, ctxT_hi)

            turned = [0]

            def turn_copy(dst, h0, nh, tok):
                n = turned[0]
                turned[0] += 1
                act.wait_ge(sem("turn"), n + 1)
                act.activation(dst[:, h0:h0 + nh, tok:tok + P],
                               bank[(4, 6)[n % 2]][:, 0:nh * P].rearrange("p (h s) -> p h s", h=nh),
                               ACT.Copy).then_inc(sem("turn_out"), 1)

            def turns(c):
                if c in (0, 1):
                    for t in range(NT):
                        turn_copy(qT, 4 * c, 4 - 2 * c, t * P)
                if c in (2, 3):
                    for src in range(2):
                        for t in range(NT):
                            turn_copy(kT, 4 * (c - 2), 4 - 2 * (c - 2), (S if src == 0 else 0) + t * P)

            for c in range(5):
                split_hi(2 * c + 2)
                split_hi(2 * c + 3)
                if c >= 1:
                    turns(c - 1)
                if c == 2:
                    act.wait_ge(s_used, 6)
                    for t in range(NT):
                        act.activation(k_ctx[:, t, :], bank[2 + t][:, :], ACT.Copy).then_inc(sem("in_act"), 1)
                if c == 3:
                    act.wait_ge(s_used, 8)
                    act.wait_ge(sem("turn"), 8)
                    for t in range(NT):
                        act.activation(k_ctx[:, t, 0:256], bank[2 + t][:, 0:256], ACT.Copy).then_inc(sem("in_act"), 1)
                        act.activation(v_tok[:, t, 0:256], bank[2 + t][:, 256:512], ACT.Copy).then_inc(sem("in_act"), 1)
                if c == 4:
                    for src, tile in ((0, NT), (1, 0)):
                        act.wait_ge(*((sem("in_lat"), 3) if src == 0 else (s_used, 10)))
                        for t in range(NT):
                            act.activation(v_tok[:, tile + t, 256:768], bank[2 * src + t][:, :], ACT.Copy).then_inc(sem("in_act"), 1)

            act.wait_ge(sem("four_gmm"), 1)
            act.activation(four_g[:, :, :, :].rearrange("p c f n -> p (c f n)"), bank[7][:, :], ACT.Copy).then_inc(sem("four_gs"), 1)
            for f in range(2):
                act.wait_ge(sem("four_ft"), f + 1)
                act.activation(ftT[:, f, :], bank[4 + f][:, :], ACT.Copy).then_inc(sem("four_fts"), 1)
            act.wait_ge(sem("four_y"), 1)
            for f in range(2):
                act.activation(xT_hi[:, HEADS + f, :], bank[6][:, 256 * f:256 * f + 256], ACT.Copy).then_inc(sem("four_hi"), 1)

            ITS = [(h, t) for h in range(HEADS) for t in range(NT)]

            def exps(n):
                for c in range(2):
                    act.wait_ge(sem("d_nb"), n + 1)
                    if n >= 2:
                        act.wait_ge(sem("d_diff"), n - 1)
                    act.activation(prob[:, n % 2, c, :], bank[2 * (n % 2) + c][:, :], ACT.Exp, scale=0.125,
                                   bias=nb[:, n % 2, c:c + 1], accum_out=esum[:, n % 2, c:c + 1]).then_inc(sem("d_exp"), 1)

            exps(0)
            for n, (h, t) in enumerate(ITS):
                if n + 1 < len(ITS):
                    exps(n + 1)
                act.wait_ge(sem("d_turn"), n + 1)
                if n >= 2:
                    act.wait_ge(sem("d_pv"), n - 1)
                act.activation(diffT[:, n % 2, :, :].rearrange("p k s -> p (k s)"), bank[4 + n % 2][:, :], ACT.Copy).then_inc(sem("d_diffT"), 1)
                act.wait_ge(sem("d_pv"), n + 1)
                act.activation(o_tok[:, t, h * P:h * P + P], bank[6 + n % 2][:, 0:P], ACT.Copy).then_inc(sem("d_o"), 1)
            full_hi("sub", o_full, xT_hi, range(HEADS))
            gate_copy("out")

            def dense_ahead(stage, n_chunks):
                for c in range(n_chunks):
                    yield c
                    split_hi(BASE[stage] + 2 * c + 2)
                    split_hi(BASE[stage] + 2 * c + 3)

            for _c in dense_ahead("out", 2):
                pass

            def ffn(layer, loops):
                base = BASE[f"ffn{layer}"]
                off = layer * FCH
                act.wait_ge(sem("xres"), {0: 4, 1: 12}[layer])
                norm_square(f"n_ffn{layer}", x, xn)
                full_hi(f"n_ffn{layer}", xfull, xT_hi)
                gate_copy(f"ffn{layer}")

                def silu(c, u, i=None):
                    act.wait_ge(s_used, at(u + 2, i, 6))
                    for t in range(NT):
                        act.activation(silu_g[:, t, :], bank[t][:, 0:256], ACT.Silu).then_inc(sem("silu_g"), 1)

                def hidden_hi(c, i=None):
                    act.wait_ge(sem("h_turn"), at(off + c + 1, i, 2))
                    act.activation(hT_hi[:, :, :].rearrange("p k s -> p (k s)"), bank[6][:, :], ACT.Copy).then_inc(sem("hT_hi"), 1)

                split_hi(base + 2)
                silu(0, base)
                split_hi(base + 3)
                hidden_hi(0)
                done = 0
                for n in loops:
                    with act.Fori(0, n) as i:
                        for b in range(2):
                            u = base + 2 + 6 * done + 3 * b
                            c = 1 + 2 * done + b
                            split_hi(u + 2, i)
                            split_hi(u + 3, i)
                            silu(c, u, i)
                            split_hi(u + 4, i)
                            hidden_hi(c, i)
                    done += n
                split_hi(base + 3 * FCH + 1)

            ffn(0, (5,))

            def rows_out(stage, dst, chunks, n0=0):
                for c in chunks:
                    split_hi(BASE[stage] + 2 * c + 2)
                    split_hi(BASE[stage] + 2 * c + 3)
                    act.wait_ge(s_used, BASE[stage] + 2 * c + 2)
                    if c >= 1:
                        act.wait_ge(sem(f"{stage}_turn"), c)
                    for t in range(NT):
                        act.activation(dst[:, t, :], bank[2 * (c % 2) + t][:, :], ACT.Copy).then_inc(sem(f"{stage}_tok"), 1)
                    yield c

            act.wait_ge(sem("xres"), 8)
            norm_square("n_pw1", x, xn)
            full_hi("n_pw1", xfull, xT_hi)
            for c in rows_out("pw1", ag_tok, range(4)):
                act.wait_ge(sem("pw1_turn"), c + 1)
                if c >= 1:
                    act.wait_ge(sem("pw1_glu"), 2 * c)
                for e in range(2):
                    act.activation(sig[:, e, :], bank[5][:, 256 * e:256 * e + 256], ACT.Sigmoid,
                                   bias=pc("od_pw1_b", KT + 2 * c + e)).then_inc(sem("pw1_sig"), 1)
            act.wait_ge(sem("ln_xc"), 1)
            act.activation(csq[:, :, :], conv[:, :, :], ACT.Square).then_inc(sem("ln_sq"), 1)
            for k in range(KT):
                act.wait_ge(sem("ln_norm"), k + 1)
                act.activation(xfull[:, k, :], csq[:, k, :], ACT.Silu, scale=pc("od_ln_g", k),
                               bias=pc("od_ln_b", k)).then_inc(sem("full"), 1)
                act.wait_ge(*seen("full", "ln", k + 1))
                act.activation(xT_hi[:, k, :], xfull[:, k, :], ACT.Copy).then_inc(sem("hi"), 1)
            gate_copy("pw2")
            gate_copy("pw2b", bias_gate)
            for _c in dense_ahead("pw2", 2):
                pass
            ffn(1, (3, 2))

            act.wait_ge(sem("xres"), 16)
            norm_square("n_final", x, xn)
            gate_copy("final")
            act.wait_ge(sem("x_final"), 2)
            norm_square("n_rg", x, xn)
            full_hi("n_rg", xfull, xT_hi)
            for c in rows_out("rg_in", rg_tok, range(4)):
                act.wait_ge(sem("rg_in_turn"), c + 1)
                for e in range(2):
                    act.activation(gT[:, 2 * c + e, :], bank[5][:, 256 * e:256 * e + 256], ACT.Silu).then_inc(sem("rg_g"), 1)
            for n, (dst, b) in enumerate(((r_gate, "rg_b_a_2"), (i_gate, "rg_b_x_2"))):
                for k in range(KT):
                    act.wait_ge(sem("rg_gates"), n * KT + k + 1)
                    act.activation(dst[:, k, :], bank[k % 4][:, 0:S], ACT.Sigmoid,
                                   bias=pc(b, k)).then_inc(sem("rg_sig"), 1)
            act.wait_ge(sem("sp_abs"), 1)
            act.activation(sp_c[:, 1, :], sp_c[:, 0, :], ACT.Exp, scale=-1.0).then_inc(sem("sp_exp"), 1)
            act.wait_ge(sem("rg_log_a"), 1)
            act.activation(a_seq[:, :, :], r_gate[:, :, :], ACT.Exp).then_inc(sem("rg_a"), 1)
            act.wait_ge(sem("rg_a"), 1)
            act.activation(r_gate[:, :, :], r_gate[:, :, :], ACT.Tanh).then_inc(sem("rg_th"), 1)
            act.wait_ge(sem("rg_m"), 1)
            act.activation(r_gate[:, :, :], r_gate[:, :, :], ACT.Sqrt, scale=-1.0).then_inc(sem("rg_sqrt"), 1)
            full_hi("rg", y_full, xT_hi)
            gate_copy("rg_out")
            for _c in dense_ahead("rg_out", 2):
                pass

            act.wait_ge(sem("xres"), 20)
            norm_square("n_kv", x, xn)
            full_hi("n_kv", kv_full, xT_hi)

            def copies(stage, c, dst):
                split_hi(BASE[stage] + 2 * c + 2)
                split_hi(BASE[stage] + 2 * c + 3)
                act.wait_ge(s_used, BASE[stage] + 2 * c + 2)
                for t in range(NT):
                    if c < 2:
                        if c == 1:
                            act.wait_ge(sem(f"{stage}_turn"), t + 1)
                        act.activation(a_tok[:, t, :], bank[2 * (c % 2) + t][:, :], ACT.Copy).then_inc(sem(f"{stage}_tok"), 1)
                    else:
                        func = ACT.Copy if stage == "kv" else ACT.Silu
                        act.activation(dst[:, t, 512 * (c - 2):512 * (c - 2) + 512], bank[2 * (c % 2) + t][:, :],
                                       func).then_inc(sem(f"{stage}_rows"), 1)

            for stage, dst, turned_dst in (("kv", av, akT), ("att_in", ag, aqT)):
                if stage == "att_in":
                    full_hi("n_att", kv_full, xT_hi)
                for c in range(4):
                    copies(stage, c, dst)
                    if c < 2:
                        for t in range(NT):
                            n = 2 * c + t
                            act.wait_ge(sem(f"{stage}_turn"), n + 1)
                            act.activation(turned_dst[:, 4 * c:4 * c + 4, t * P:t * P + P],
                                           bank[4 + n % 2][:, :].rearrange("p (h s) -> p h s", h=4),
                                           ACT.Copy).then_inc(sem(f"{stage}_turned"), 1)

            A_ITS = [(h, t) for h in range(A_HEADS) for t in range(NT)]

            def a_exp(n):
                h, t = A_ITS[n]
                keys = (t + 1) * P
                act.wait_ge(sem("a_nb"), n + 1)
                act.activation(ap_[:, n % 2, 0:keys], ap_[:, n % 2, 0:keys], ACT.Exp, scale=float(P) ** -0.5,
                               bias=nb[:, n % 2, 0:1], accum_out=esum[:, n % 2, 0:1]).then_inc(sem("a_exp"), 1)

            a_exp(0)
            for n, (h, t) in enumerate(A_ITS):
                if n + 1 < len(A_ITS):
                    a_exp(n + 1)
                act.wait_ge(sem("a_turn"), n + 1)
                if n >= 2:
                    act.wait_ge(sem("a_pv"), n - 1)
                act.activation(apT[:, n % 2, 0:t + 1, :].rearrange("p k s -> p (k s)"),
                               bank[2 + n % 2][:, 0:(t + 1) * P], ACT.Copy).then_inc(sem("a_apT"), 1)
            act.wait_ge(*seen("tr", "ao", 2 * KT))
            for k in range(KT):
                act.activation(xT_hi[:, k, :], bank[k // 2][:, 256 * (k % 2):256 * (k % 2) + 256], ACT.Copy).then_inc(sem("hi"), 1)
                act.wait_ge(*seen("lo", "ao", k + 1))
            gate_copy("att_out")
            for _c in dense_ahead("att_out", 2):
                pass
            act.wait_ge(sem("xres"), 24)
            norm_square("n_last", x, xn)
            gate_copy("last")

        @block.vector
        def _(dve):
            count = [0]

            def link(ins):
                count[0] += 1
                ins.then_inc(sem("dve_chain"), 1)
                dve.wait_ge(sem("dve_chain"), count[0])

            def split_lo(u, i=None):
                if u >= UNITS:
                    return
                n = u + ADA0
                dve.wait_ge(s_hi, at(u + 1, i, 6))
                dve.tensor_tensor(w_lo[u % N_SPLIT][:, :], w_land[n % N_LAND][:, :],
                                  w_hi[u % N_SPLIT][:, :].bitcast(F32), ALU.subtract).then_inc(s_lo, 1)

            def job_units(q, units, i=None):
                c = 0 if JOBS[q] < V_MOD0 else 2
                for j in units:
                    dve.wait_ge(a_landed[j % 2], at(16 * (2 * q + j // 2 + 1), i, 32))
                    for e in range(2):
                        n = 2 * j + e
                        w = a_land[j % 2][:, e * D:e * D + D]
                        if n == 0:
                            if q >= 1:
                                dve.wait_ge(s_red, at(q, i, 1))
                            ins = dve.tensor_scalar(job_sum[:, :], w, silu_c[:, c, n:n + 1], None, ALU.mult)
                        else:
                            dve.wait_ge(s_step, at(8 * q + n, i, 8))
                            ins = dve.scalar_tensor_tensor(out=job_sum[:, :], in0=w, scalar=silu_c[:, c, n:n + 1],
                                                           in1=job_sum[:, :], op0=ALU.mult, op1=ALU.add)
                        ins.then_inc(s_step, 1)

            def job_cols(q, i=None):
                v = JOBS[q]
                dve.wait_ge(s_red, at(q + 1, i, 1))
                if i is None:
                    dst, bias = mcol[:, v * KT:v * KT + KT], pcol[:, v * KT + (32 if v >= V_MOD0 else 0):][:, 0:KT]
                else:
                    dst = mcol[:, bass.ds(i * KT + v * KT, KT)]
                    bias = pcol[:, bass.ds(i * KT + (v * KT + (32 if v >= V_MOD0 else 0)), KT)]
                dve.tensor_tensor(dst, COLS[:, 0:KT], bias, ALU.add).then_inc(s_cols, 1)

            def job(q):
                job_units(q, range(4))

            def norm_stats(stage, src, dst, n=NT, width=D, scale=None):
                dve.wait_ge(*seen("ss", stage, n))
                dve.tensor_scalar(ms[:, 0:n], ss[:, 0:n], 1.0 / width, EPS, ALU.mult, ALU.add).then_inc(sem("ms"), 1)
                dve.wait_ge(*seen("rstd", stage, 1))
                if dst is not None:
                    for t in range(NT):
                        dve.tensor_scalar(dst[:, t, :], src[:, t, :], rstd[:, t:t + 1], None, ALU.mult).then_inc(sem("xn"), 1)

            def mod_cols(g, v_shift, v_scale, scale_cols=None):
                sc = mc(v_scale) if scale_cols is None else scale_cols
                link(dve.scalar_tensor_tensor(out=a_col[:, :], in0=sc, scalar=1.0, in1=g, op0=ALU.add, op1=ALU.mult))

            def full_lo(stage, full, hi, lo, banks, a, b, ks=range(KT), turns=2 * KT):
                dve.wait_ge(*seen("tr", stage, turns))

                def low(n):
                    dve.wait_ge(*seen("hi", stage, n + 1))
                    dve.tensor_tensor(lo[:, ks[n], :], full[:, ks[n], :], hi[:, ks[n], :].bitcast(F32),
                                      ALU.subtract).then_inc(sem("lo"), 1)

                for n, k in enumerate(ks):
                    src = banks[k // 2][:, 256 * (k % 2):256 * (k % 2) + 256]
                    if b is None:
                        ins = dve.tensor_scalar(full[:, k, :], src, a(k), None, ALU.mult)
                    else:
                        ins = dve.tensor_scalar(full[:, k, :], src, a(k), b(k), ALU.mult, ALU.add)
                    ins.then_inc(sem("full"), 1)
                    if n >= 1:
                        low(n - 1)
                low(len(ks) - 1)

            def gate_diag(stage, col):
                g = gate[:, :].rearrange("p (k f) -> p k f", k=KT)
                dve.tensor_tensor(g, ident[:, :].unsqueeze(1).broadcast_to([P, KT, P]),
                                  col.unsqueeze(2).broadcast_to([P, KT, P]), ALU.mult).then_inc(sem("diag"), 1)

            def residual(stage, c, banks, first, bias=None):
                cols = slice(512 * c, 512 * c + 512)
                for t in range(NT):
                    link(dve.tensor_tensor(tmp[:, t, :], banks[t][:, :], gate[:, cols], ALU.mult))
                    if bias is not None:
                        link(dve.tensor_tensor(tmp[:, t, :], tmp[:, t, :], bias[:, cols], ALU.add))
                    dve.tensor_tensor(x[:, t, cols], x[:, t, cols], tmp[:, t, :], ALU.add).then_inc(sem("xres"), 1)

            for g in range(5):
                dve.wait_ge(sem("prow_tr"), g + 1)
                n = sum(k for _, k in ROW_GROUPS[g])
                dve.tensor_copy(pcol[:, g * P:g * P + n], bank[4 + g % 4][:, 0:n]).then_inc(sem("cols_in"), 1)
                if g == 0:
                    norm_stats("n_x", x, xn)
            norm_stats("n_ctx", ctx_x, ctx_x)
            dve.wait_ge(sem("lam_in"), 64)
            for n in range(2):
                dve.tensor_tensor_reduce(lam_junk[:, n, :], lam_in[:, 2 * n, :], lam_in[:, 2 * n + 1, :], 1.0, 0.0,
                                         ALU.mult, ALU.add, lam_tmp[:, n:n + 1]).then_inc(sem("lam_dot"), 1)
            dve.wait_ge(sem("lam_exp"), 1)
            link(dve.tensor_tensor(lam_tmp[:, 4:5], lam_tmp[:, 3:4], lam_tmp[:, 2:3], ALU.subtract))
            link(dve.tensor_scalar(lam_tmp[:, 5:6], lam_tmp[:, 4:5], -(1.0 - SUB_SCALE), None, ALU.add))

            dve.wait_ge(sem("ada0_tr"), 16)
            turned = bank[0][:, 0:32].rearrange("p (v c) -> p v c", c=2)
            dve.tensor_tensor(mcol[:, 0:2 * KT], turned[:, :, 0], pcol[:, 0:2 * KT], ALU.add).then_inc(sem("ada0_cols"), 1)
            dve.tensor_tensor(mcol_ctx[:, :], turned[:, :, 1], pcol[:, 0:2 * KT], ALU.add).then_inc(sem("ada0_cols"), 1)
            dve.wait_ge(sem("ada0_cols"), 2)
            split_lo(0)
            split_lo(1)
            mod_cols(pc("mix_norm_g", 0, KT), 0, 1)
            link(dve.scalar_tensor_tensor(out=b_col[:, :], in0=mcol_ctx[:, KT:2 * KT], scalar=1.0,
                                          in1=pc("mix_norm_g", 0, KT), op0=ALU.add, op1=ALU.mult))
            full_lo("n_x", xfull, xT_hi, xT_lo, bank[4:8], lambda k: a_col[:, k:k + 1], lambda k: mc(0, k, 1))
            full_lo("n_ctx", ctx_full, ctxT_hi, ctxT_lo, bank[4:8], lambda k: b_col[:, k:k + 1],
                    lambda k: mcol_ctx[:, k:k + 1])

            dve.wait_ge(sem("rope_in"), 16)

            def rotate(src, t, n):
                m = n // 64
                v = src[:, 0:n].rearrange("p (m h d) -> p m h d", m=m, h=2)
                c4 = rope_cos[:, 0:n].rearrange("p (m h d) -> p m h d", m=m, h=2)
                s4 = rope_sin[:, 0:n].rearrange("p (m h d) -> p m h d", m=m, h=2)
                v2 = src[:, 0:n].rearrange("p (m d) -> p m d", d=32)
                o4 = rot[:, t, 0:n].rearrange("p (m h d) -> p m h d", m=m, h=2)
                for dst, which in ((rope_cos, 0), (rope_sin, 1)):
                    ins = dve.tensor_tensor(dst[:, 0:n].rearrange("p (m d) -> p m d", d=32), v2,
                                            rope[:, t, which, :].unsqueeze(1).broadcast_to([P, 2 * m, 32]), ALU.mult)
                    link(ins)
                dve.tensor_tensor(o4[:, :, 0, :], c4[:, :, 0, :], s4[:, :, 1, :], ALU.subtract).then_inc(sem("rot"), 1)
                dve.tensor_tensor(o4[:, :, 1, :], s4[:, :, 0, :], c4[:, :, 1, :], ALU.add).then_inc(sem("rot"), 1)

            plan = [((s_used, 2), 0, 512, 0), ((s_used, 4), 2, 256, 2), ((sem("in_lat"), 1), 0, 512, 4),
                    ((sem("in_lat"), 2), 0, 256, 8)]
            for c in range(5):
                split_lo(2 * c + 2)
                split_lo(2 * c + 3)
                if c >= 1:
                    job(c - 1)
                if c < 4:
                    event, b, n, free = plan[c]
                    dve.wait_ge(*event)
                    if free:
                        dve.wait_ge(sem("turn"), free)
                    for t in range(NT):
                        if c or t:
                            dve.wait_ge(sem("rot"), 4 * c + 2 * t)
                        rotate(bank[b + t], t, n)
                        if c == 1:
                            dve.tensor_copy(f_tok[:, t, :], bank[b + t][:, 256:512]).then_inc(sem("f_tok"), 1)
                        if c == 3:
                            dve.tensor_copy(v_tok[:, NT + t, 0:256], bank[b + t][:, 256:512]).then_inc(sem("v_lat"), 1)
                if c >= 1:
                    job_cols(c - 1)
            for f in range(2):
                dve.wait_ge(sem("four_hi"), 2)
                dve.tensor_tensor(xT_lo[:, HEADS + f, :], bank[6][:, 256 * f:256 * f + 256],
                                  xT_hi[:, HEADS + f, :].bitcast(F32), ALU.subtract).then_inc(sem("four_lo"), 1)

            ITS = [(h, t) for h in range(HEADS) for t in range(NT)]

            def row_max(n):
                b = n % 2
                if n >= 2:
                    dve.wait_ge(sem("d_exp"), 2 * (n - 1))
                for c in range(2):
                    dve.wait_ge(sem("d_s"), 2 * n + c + 1)
                    dve.reduce_max(mx[:, b, c:c + 1], bank[2 * b + c][:, :], AX_X).then_inc(sem("d_mx"), 1)
                dve.wait_ge(sem("d_mx"), 2 * n + 2)
                dve.tensor_scalar(nb[:, b, :], mx[:, b, :], -0.125, None, ALU.mult).then_inc(sem("d_nb"), 1)

            row_max(0)
            for n, (h, t) in enumerate(ITS):
                b = n % 2
                if n + 1 < len(ITS):
                    row_max(n + 1)
                dve.wait_ge(sem("d_exp"), 2 * n + 2)
                link(dve.reciprocal(rsum[:, b, :], esum[:, b, :]))
                link(dve.tensor_scalar(rsum[:, b, 1:2], rsum[:, b, 1:2], lam_tmp[:, 5:6], None, ALU.mult))
                link(dve.tensor_scalar(prob[:, b, 1, :], prob[:, b, 1, :], rsum[:, b, 1:2], None, ALU.mult))
                if n >= 2:
                    dve.wait_ge(sem("d_turn"), n - 1)
                dve.scalar_tensor_tensor(out=diff[:, b, :], in0=prob[:, b, 0, :], scalar=rsum[:, b, 0:1],
                                         in1=prob[:, b, 1, :], op0=ALU.mult, op1=ALU.add).then_inc(sem("d_diff"), 1)
            for n, (h, t) in enumerate(ITS):
                dve.wait_ge(sem("d_o"), n + 1)
                o = o_tok[:, t, h * P:h * P + P]
                if n >= 2:
                    dve.wait_ge(*seen("ss", "sub", n - 1))
                dve.tensor_tensor_reduce(sq_junk[:, n % 2, :], o, o, 1.0, 0.0, ALU.mult, ALU.add,
                                         ss[:, t * HEADS + h:t * HEADS + h + 1]).then_inc(sem("ss"), 1)
            norm_stats("sub", None, None, 12, P)
            for t in range(NT):
                o = o_tok[:, t, :].rearrange("p (h e) -> p h e", h=HEADS)
                dve.tensor_tensor(o, o, rstd[:, t * HEADS:t * HEADS + HEADS].unsqueeze(2).broadcast_to([P, HEADS, P]),
                                  ALU.mult).then_inc(sem("xn"), 1)
            link(dve.tensor_scalar(a_col[:, 0:1], pc("ev_subln_g"), SUB_SCALE, None, ALU.mult))
            full_lo("sub", o_full, xT_hi, xT_lo, bank[2:5], lambda k: a_col[:, 0:1], None, range(HEADS), 12)
            gate_diag("out", mc(2))

            def dense_residual(stage, bias=None):
                for c in range(2):
                    split_lo(BASE[stage] + 2 * c + 2)
                    split_lo(BASE[stage] + 2 * c + 3)
                    dve.wait_ge(s_used, BASE[stage] + 2 * c + 2)
                    if c == 0:
                        dve.wait_ge(*seen("gate", stage, 2))
                    residual(stage, c, bank[2 * c:2 * c + 2], 0, bias)

            dense_residual("out")

            def ffn(layer, loops, first_job):
                base = BASE[f"ffn{layer}"]
                off = layer * FCH
                norm_stats(f"n_ffn{layer}", x, xn)
                mod_cols(pc("ffn_norm_g", layer * KT, KT), 0, 6 * layer + 4)
                full_lo(f"n_ffn{layer}", xfull, xT_hi, xT_lo, bank[2:6], lambda k: a_col[:, k:k + 1],
                        lambda k: mc(6 * layer + 3, k, 1))
                gate_diag(f"ffn{layer}", mc(6 * layer + 5))

                def hidden(c, i=None):
                    for t in range(NT):
                        dve.wait_ge(sem("silu_g"), at(2 * (off + c) + t + 1, i, 4))
                        dve.tensor_tensor(hid[:, t, :], silu_g[:, t, :], bank[t][:, 256:512], ALU.mult).then_inc(sem("hid"), 1)

                def hidden_lo(c, i=None):
                    dve.wait_ge(sem("hT_hi"), at(off + c + 1, i, 2))
                    dve.tensor_tensor(hT_lo[:, :, :].rearrange("p k s -> p (k s)"), bank[6][:, :],
                                      hT_hi[:, :, :].rearrange("p k s -> p (k s)").bitcast(F32),
                                      ALU.subtract).then_inc(sem("hT_lo"), 1)

                split_lo(base + 2)
                job(first_job)
                hidden(0)
                split_lo(base + 3)
                hidden_lo(0)
                job_cols(first_job)
                done = 0
                for q, n in loops:
                    with dve.Fori(0, n) as i:
                        for b in range(2):
                            u = base + 2 + 6 * done + 3 * b
                            c = 1 + 2 * done + b
                            split_lo(u + 2, i)
                            split_lo(u + 3, i)
                            job_units(q, range(2 * b, 2 * b + 2), i)
                            hidden(c, i)
                            split_lo(u + 4, i)
                            hidden_lo(c, i)
                        job_cols(q, i)
                    done += n
                split_lo(base + 3 * FCH + 1)
                dve.wait_ge(s_used, base + 3 * FCH)
                dve.wait_ge(*seen("gate", f"ffn{layer}", 2))
                for c in range(2):
                    residual(f"ffn{layer}", c, bank[2 + 2 * c:4 + 2 * c], 0)

            ffn(0, [(5, 5)], 4)

            norm_stats("n_pw1", x, xn)
            mod_cols(pc("mix_norm_g", KT, KT), 0, 7)
            full_lo("n_pw1", xfull, xT_hi, xT_lo, bank[2:6], lambda k: a_col[:, k:k + 1], lambda k: mc(6, k, 1))
            dve.wait_ge(sem("u_zero"), 2)
            for c in range(4):
                split_lo(BASE["pw1"] + 2 * c + 2)
                split_lo(BASE["pw1"] + 2 * c + 3)
                if c < 2:
                    job(10 + c)
                for e in range(2):
                    k = 2 * c + e
                    dve.wait_ge(sem("pw1_sig"), k + 1)
                    dve.scalar_tensor_tensor(out=u_pad[:, k, PAD:PAD + S], in0=bank[4][:, 256 * e:256 * e + 256],
                                             scalar=pc("od_pw1_b", k), in1=sig[:, e, :], op0=ALU.add,
                                             op1=ALU.mult).then_inc(sem("pw1_glu"), 1)
                if c < 2:
                    job_cols(10 + c)
            dve.wait_ge(sem("pw1_glu"), KT)
            for tap in range(CONV):
                w = COL["od_dw_w_a"] + tap * KT
                for k in range(KT):
                    src = u_pad[:, k, tap:tap + S]
                    n = tap * KT + k
                    if tap == 0:
                        ins = dve.tensor_scalar(conv[:, k, :], src, pcol[:, w + k:w + k + 1], pc("od_dw_b", k),
                                                ALU.mult, ALU.add)
                    else:
                        dve.wait_ge(sem("conv"), n - KT + 1)
                        ins = dve.scalar_tensor_tensor(out=conv[:, k, :], in0=src, scalar=pcol[:, w + k:w + k + 1],
                                                       in1=conv[:, k, :], op0=ALU.mult, op1=ALU.add)
                    ins.then_inc(sem("conv"), 1)
            dve.wait_ge(sem("ln_mean_mm"), 1)
            link(dve.tensor_scalar(mean[:, :], bank[4][:, 0:S], 1.0 / D, None, ALU.mult))
            dve.tensor_tensor(conv[:, :, :], conv[:, :, :], mean[:, :].unsqueeze(1).broadcast_to([P, KT, S]),
                              ALU.subtract).then_inc(sem("ln_xc"), 1)
            dve.wait_ge(sem("ln_var_mm"), 1)
            dve.tensor_scalar(rln[:, :], bank[5][:, 0:S], 1.0 / D, EPS, ALU.mult, ALU.add).then_inc(sem("ln_ms"), 1)
            dve.wait_ge(sem("ln_rstd"), 1)
            for k in range(KT):
                dve.tensor_tensor(csq[:, k, :], conv[:, k, :], rln[:, :], ALU.mult).then_inc(sem("ln_norm"), 1)
            for k in range(KT):
                dve.wait_ge(*seen("hi", "ln", k + 1))
                dve.tensor_tensor(xT_lo[:, k, :], xfull[:, k, :], xT_hi[:, k, :].bitcast(F32),
                                  ALU.subtract).then_inc(sem("lo"), 1)
            gate_diag("pw2", mc(8))
            link(dve.tensor_tensor(b_col[:, :], mc(8), pc("od_pw2_b", 0, KT), ALU.mult))
            dve.wait_ge(*seen("gmm", "pw2", 1))
            dve.wait_ge(*seen("gate", "pw2", 2))
            bg = bias_gate[:, :].rearrange("p (k f) -> p k f", k=KT)
            dve.tensor_tensor(bg, ident[:, :].unsqueeze(1).broadcast_to([P, KT, P]),
                              b_col[:, :].unsqueeze(2).broadcast_to([P, KT, P]), ALU.mult).then_inc(sem("diag"), 1)
            dve.wait_ge(*seen("gate", "pw2b", 2))
            dense_residual("pw2", bias_gate)
            ffn(1, [(13, 3), (16, 2)], 12)

            norm_stats("n_final", x, xn)
            gate_diag("final", pc("final_g", 0, KT))
            dve.wait_ge(*seen("gate", "final", 2))
            dve.wait_ge(*seen("xn", "n_final", 2))
            for t in range(NT):
                dve.tensor_tensor(x[:, t, :], xn[:, t, :], gate[:, :], ALU.mult).then_inc(sem("x_final"), 1)

            norm_stats("n_rg", x, xn)
            mod_cols(pc("norm_g_2", 0, KT), 0, V_MOD0 + 1)
            full_lo("n_rg", xfull, xT_hi, xT_lo, bank[2:6], lambda k: a_col[:, k:k + 1], lambda k: mc(V_MOD0, k, 1))
            dve.wait_ge(sem("ru_zero"), 1)
            for c in range(4):
                split_lo(BASE["rg_in"] + 2 * c + 2)
                split_lo(BASE["rg_in"] + 2 * c + 3)
                dve.wait_ge(sem("rg_in_turn"), c + 1)
                dve.tensor_copy(ru_pad[:, 2 * c:2 * c + 2, RG_CONV - 1:RUP],
                                bank[4][:, :].rearrange("p (k s) -> p k s", k=2)).then_inc(sem("rg_u"), 1)
                dve.wait_ge(sem("rg_u"), c + 1)
                for tap in range(RG_CONV):
                    w = COL["rg_conv_w_2"] + tap * KT
                    for k in (2 * c, 2 * c + 1):
                        src = ru_pad[:, k, tap:tap + S]
                        if tap == 0:
                            ins = dve.tensor_scalar(uc[:, k, :], src, pcol[:, w + k:w + k + 1], pc("rg_conv_b_2", k),
                                                    ALU.mult, ALU.add)
                        else:
                            dve.wait_ge(sem("rg_conv"), 8 * c + 2 * (tap - 1) + k - 2 * c + 1)
                            ins = dve.scalar_tensor_tensor(out=uc[:, k, :], in0=src, scalar=pcol[:, w + k:w + k + 1],
                                                           in1=uc[:, k, :], op0=ALU.mult, op1=ALU.add)
                        ins.then_inc(sem("rg_conv"), 1)
            lam = pc("rg_lambda_2", 0, KT)
            link(dve.tensor_scalar(sp_c[:, 2, :], lam, -1.0, 0.0, ALU.mult, ALU.max))
            dve.scalar_tensor_tensor(out=sp_c[:, 0, :], in0=sp_c[:, 2, :], scalar=2.0, in1=lam,
                                     op0=ALU.mult, op1=ALU.add).then_inc(sem("sp_abs"), 1)
            dve.wait_ge(sem("sp_exp"), 1)
            link(dve.tensor_scalar(sp_c[:, 3, :], sp_c[:, 1, :], 2.0, None, ALU.add))
            link(dve.reciprocal(sp_c[:, 4, :], sp_c[:, 3, :]))
            link(dve.tensor_tensor(sp_c[:, 3, :], sp_c[:, 1, :], sp_c[:, 4, :], ALU.mult))
            link(dve.tensor_tensor(sp_c[:, 4, :], sp_c[:, 3, :], sp_c[:, 3, :], ALU.mult))
            link(dve.tensor_scalar(sp_c[:, 5, :], sp_c[:, 4, :], 1.0 / 17, 1.0 / 15, ALU.mult, ALU.add))
            for n in range(13, 0, -2):
                link(dve.tensor_tensor(sp_c[:, 5, :], sp_c[:, 5, :], sp_c[:, 4, :], ALU.mult))
                link(dve.tensor_scalar(sp_c[:, 5, :], sp_c[:, 5, :], 1.0 / n, None, ALU.add))
            link(dve.tensor_tensor(sp_c[:, 5, :], sp_c[:, 5, :], sp_c[:, 3, :], ALU.mult))
            link(dve.scalar_tensor_tensor(out=sp_c[:, 5, :], in0=sp_c[:, 5, :], scalar=2.0, in1=sp_c[:, 2, :],
                                          op0=ALU.mult, op1=ALU.add))
            dve.tensor_scalar(sp_c[:, 7, :], sp_c[:, 5, :], -RG_C, None, ALU.mult).then_inc(sem("sp_done"), 1)
            dve.wait_ge(sem("rg_sig"), 2 * KT)
            dve.wait_ge(sem("sp_done"), 1)
            dve.tensor_tensor(r_gate[:, :, :], r_gate[:, :, :], sp_c[:, 7, :].unsqueeze(2).broadcast_to([P, KT, S]),
                              ALU.mult).then_inc(sem("rg_log_a"), 1)
            link(dve.tensor_tensor(i_gate[:, :, :], i_gate[:, :, :], uc[:, :, :], ALU.mult))
            dve.wait_ge(sem("rg_a"), 1)
            link(dve.tensor_tensor(y_full[:, :, :], a_seq[:, :, :], a_seq[:, :, :], ALU.mult))
            dve.wait_ge(sem("rg_th"), 1)
            dve.scalar_tensor_tensor(out=r_gate[:, :, :], in0=y_full[:, :, :], scalar=1.0, in1=r_gate[:, :, :],
                                     op0=ALU.add, op1=ALU.mult).then_inc(sem("rg_m"), 1)
            dve.wait_ge(sem("rg_sqrt"), 1)
            link(dve.tensor_tensor(i_gate[:, :, :], i_gate[:, :, :], r_gate[:, :, :], ALU.mult))
            for k in range(KT):
                dve.tensor_tensor_scan(uc[:, k, :], a_seq[:, k, :], i_gate[:, k, :], 0.0, ALU.mult, ALU.add).then_inc(sem("rg_scan"), 1)
            for k in range(KT):
                dve.wait_ge(sem("rg_scan"), k + 1)
                dve.tensor_tensor(y_full[:, k, :], uc[:, k, :], gT[:, k, :], ALU.mult).then_inc(sem("full"), 1)
            for k in range(KT):
                dve.wait_ge(*seen("hi", "rg", k + 1))
                dve.tensor_tensor(xT_lo[:, k, :], y_full[:, k, :], xT_hi[:, k, :].bitcast(F32),
                                  ALU.subtract).then_inc(sem("lo"), 1)
            gate_diag("rg_out", mc(V_MOD0 + 2))
            dense_residual("rg_out")

            norm_stats("n_kv", x, xn)
            mod_cols(pc("kv_norm_g_2", 0, KT), 0, V_KV + 1)
            full_lo("n_kv", kv_full, xT_hi, xT_lo, bank[2:6], lambda k: a_col[:, k:k + 1], lambda k: mc(V_KV, k, 1))
            for stage in ("kv", "att_in"):
                if stage == "att_in":
                    mod_cols(pc("norm_g_2", KT, KT), 0, V_MOD1 + 1)
                    dve.wait_ge(s_used, BASE["att_in"])
                    full_lo("n_att", kv_full, xT_hi, xT_lo, bank[2:6], lambda k: a_col[:, k:k + 1],
                            lambda k: mc(V_MOD1, k, 1))
                for c in range(4):
                    split_lo(BASE[stage] + 2 * c + 2)
                    split_lo(BASE[stage] + 2 * c + 3)

            A_ITS = [(h, t) for h in range(A_HEADS) for t in range(NT)]
            dve.wait_ge(sem("mask_in"), 16)

            def a_max(n):
                h, t = A_ITS[n]
                b = n % 2
                keys = (t + 1) * P
                dve.wait_ge(sem("a_s"), n + 1)
                if n >= 2:
                    dve.wait_ge(sem("a_turn"), n - 1)
                if t == 1:
                    link(dve.tensor_copy(ap_[:, b, 0:P], bank[b][:, 0:P]))
                dve.tensor_tensor(ap_[:, b, t * P:keys], bank[b][:, t * P:keys], mask[:, :], ALU.add).then_inc(sem("a_msk"), 1)
                dve.wait_ge(sem("a_msk"), n + 1)
                link(dve.reduce_max(mx[:, b, 0:1], ap_[:, b, 0:keys], AX_X))
                dve.tensor_scalar(nb[:, b, 0:1], mx[:, b, 0:1], -float(P) ** -0.5, None, ALU.mult).then_inc(sem("a_nb"), 1)

            def a_out(n):
                h, t = A_ITS[n]
                b = n % 2
                dve.wait_ge(sem("a_pv"), n + 1)
                dve.scalar_tensor_tensor(out=ao[:, t, h * P:h * P + P], in0=bank[4 + b][:, 0:P],
                                         scalar=rsum[:, b, 0:1], in1=ag[:, t, h * P:h * P + P],
                                         op0=ALU.mult, op1=ALU.mult).then_inc(sem("a_o"), 1)

            a_max(0)
            for n in range(len(A_ITS)):
                if n + 1 < len(A_ITS):
                    a_max(n + 1)
                dve.wait_ge(sem("a_exp"), n + 1)
                if n >= 2:
                    dve.wait_ge(sem("a_o"), n - 1)
                link(dve.reciprocal(rsum[:, n % 2, 0:1], esum[:, n % 2, 0:1]))
                if n >= 1:
                    a_out(n - 1)
            a_out(len(A_ITS) - 1)
            dve.wait_ge(*seen("tr", "ao", 2 * KT))
            for k in range(KT):
                dve.wait_ge(*seen("hi", "ao", k + 1))
                dve.tensor_tensor(xT_lo[:, k, :], bank[k // 2][:, 256 * (k % 2):256 * (k % 2) + 256],
                                  xT_hi[:, k, :].bitcast(F32), ALU.subtract).then_inc(sem("lo"), 1)
            gate_diag("att_out", mc(V_MOD1 + 2))
            dense_residual("att_out")
            norm_stats("n_last", x, xn)
            gate_diag("last", pc("final_norm_g_2", 0, KT))
            dve.wait_ge(*seen("gate", "last", 2))
            dve.wait_ge(*seen("xn", "n_last", 2))
            for t in range(NT):
                dve.tensor_tensor(xn[:, t, :], xn[:, t, :], gate[:, :], ALU.mult).then_inc(sem("result"), 1)

        @block.tensor
        def _(pe):
            def three(dst, hi, lo, whi, wlo, start, stop):
                pe.matmul(dst, hi, whi, start=start, stop=False)
                pe.matmul(dst, hi, wlo, start=False, stop=False)
                return pe.matmul(dst, lo, whi, start=False, stop=stop)

            def unit_wait(u, i=None):
                pe.wait_ge(s_lo, at(u + 1, i, 6))

            def half(u, j, hi, lo, banks, last=None, ready=None):
                wh = w_hi[u % N_SPLIT][:, :].rearrange("p (k n) -> p k n", k=4)
                wl = w_lo[u % N_SPLIT][:, :].rearrange("p (k n) -> p k n", k=4)
                for t in range(NT):
                    for k in range(4):
                        if ready is not None and t == 0:
                            pe.wait_ge(*seen("lo", ready, 4 * j + k + 1))
                        kt = 4 * j + k
                        ins = three(banks[t][:, :], hi[:, kt, t * P:t * P + P], lo[:, kt, t * P:t * P + P],
                                    wh[:, k, :], wl[:, k, :], kt == 0, kt == KT - 1)
                if last is not None:
                    ins.then_inc(last, 1)
                return ins

            def turn_norm(stage, src, banks, wait=None):
                for t in range(NT):
                    pe.wait_ge(*seen("xn", stage, t + 1))
                    for k in range(KT):
                        pe.transpose(banks[k // 2][:, 256 * (k % 2) + t * P:256 * (k % 2) + t * P + P],
                                     src[:, t, k * P:k * P + P], ident[:, :]).then_inc(sem("tr"), 1)

            def gate_mm(stage, src=None):
                src = gate if src is None else src
                pe.wait_ge(*seen("diag", stage, 1))
                for h in range(2):
                    ins = pe.matmul(bank[4 + h][:, :], ones[:, :], src[:, 512 * h:512 * h + 512], start=True, stop=True)
                ins.then_inc(sem("gmm"), 1)

            def job_reduce(q, i=None):
                pe.wait_ge(s_step, at(8 * q + 8, i, 8))
                if q >= 1:
                    pe.wait_ge(s_cols, at(q, i, 1))
                for k in range(KT):
                    ins = pe.matmul(COLS[:, k:k + 1], job_sum[:, k * P:k * P + P], ones[:, 0:1], start=True, stop=True)
                ins.then_inc(s_red, 1)

            pe.wait_ge(sem("ident_in"), 16)
            pe.wait_ge(sem("ones"), 2)

            def turn_rows(g):
                pe.wait_ge(sem(f"prow{g}"), 16 * len(ROW_GROUPS[g]))
                n = sum(k for _, k in ROW_GROUPS[g])
                if g == 4:
                    pe.wait_ge(sem("cols_in"), 1)
                pe.transpose(bank[4 + g % 4][:, 0:n], prow[0:n, g, :], ident[0:n, 0:n]).then_inc(sem("prow_tr"), 1)

            turn_rows(0)
            pe.wait_ge(sem("silu_c"), 1)
            for n in range(ADA0):
                pe.wait_ge(landed[n % N_LAND], 32 * (n // N_LAND + 1))
                w = w_land[n % N_LAND][:, :].rearrange("p (k n) -> p k n", k=2)
                for e in range(2):
                    kt = 2 * (n % 4) + e
                    for h in range(2):
                        ins = pe.matmul(bank[2 * (n // 4) + h][0:2, :], silu_c[:, 0:2, kt],
                                        w[:, e, 512 * h:512 * h + 512], start=kt == 0, stop=kt == KT - 1)
                ins.then_inc(sem("ada0_used"), 1)
            for g in range(1, 5):
                turn_rows(g)
            pe.wait_ge(sem("cols_in"), 5)
            turn_norm("n_x", xn, bank[4:8])
            pe.wait_ge(sem("ada0_rows"), 4)
            for n in range(2 * KT):
                pe.transpose(bank[0][:, 2 * n:2 * n + 2], ada_rows[0:2, n * P:n * P + P], ident[0:2, 0:2]).then_inc(sem("ada0_tr"), 1)
            pe.wait_ge(*seen("full", "n_x", KT))
            turn_norm("n_ctx", ctx_x, bank[4:8])

            def turn_heads(c):
                nh = 4 if c % 2 == 0 else 2
                rot_need = {0: 4, 1: 8, 2: 12, 3: 16}[c]
                for src in range(1 if c < 2 else 2):
                    for t in range(NT):
                        n = turned[0]
                        turned[0] += 1
                        if src == 0:
                            pe.wait_ge(sem("rot"), rot_need - 2 * (1 - t))
                        else:
                            pe.wait_ge(sem("in_act"), {2: t + 1, 3: 2 + 2 * t + 1}[c])
                        if n >= 2:
                            pe.wait_ge(sem("turn_out"), n - 1)
                        buf = rot if src == 0 else k_ctx
                        for h in range(nh):
                            ins = pe.transpose(bank[(4, 6)[n % 2]][:, h * P:h * P + P], buf[:, t, h * P:h * P + P], ident[:, :])
                        ins.then_inc(sem("turn"), 1)

            turned = [0]
            bank_read = [[("ada0_cols", 2)], [], [("rot", 4)], [("rot", 8), ("f_tok", 2)], [("rot", 12)],
                         [("in_act", 2)], [("rot", 16), ("v_lat", 2)], [("in_act", 6)]]
            events = [[(0, 0)], [(1, 2)], [(2, 0), (3, 2)], [(4, 0), (5, 2)], [(6, 0), (7, 2)]]
            for c in range(5):
                for side, (event, b) in enumerate(events[c]):
                    for name, n in bank_read[event]:
                        pe.wait_ge(sem(name), n)
                    for j in range(2):
                        u = 2 * c + j
                        if side == 0:
                            unit_wait(u)
                        hi, lo = (xT_hi, xT_lo) if side == 0 else (ctxT_hi, ctxT_lo)
                        if c == 2 and side == 1 and j == 0:
                            pe.wait_ge(*seen("lo", "n_ctx", KT))
                        last = s_used if side == len(events[c]) - 1 else None
                        ins = half(u, j, hi, lo, bank[b:b + 2], last, "n_x" if c == 0 else None)
                    if last is None:
                        ins.then_inc(sem("in_lat"), 1)
                if c == 1:
                    pe.wait_ge(*seen("full", "n_ctx", KT))
                if c >= 1:
                    job_reduce(c - 1)
                    turn_heads(c - 1)

            pe.wait_ge(sem("four_in"), 16 * 5)
            pe.wait_ge(s_cols, 4)
            for n in range(2):
                for f in range(2):
                    ins = pe.matmul(bank[7][:, 256 * n + P * f:256 * n + P * f + P], four_c[:, n, :], four_w[:, f, :],
                                    start=True, stop=True)
            ins.then_inc(sem("four_gmm"), 1)
            pe.wait_ge(sem("dft_in"), 16)
            pe.wait_ge(sem("f_tok"), 2)
            pe.wait_ge(sem("turn_out"), 12)
            for f in range(2):
                for t in range(NT):
                    ins = pe.matmul(bank[4 + f][:, :], f_tok[:, t, f * P:f * P + P], dft[:, t, :], start=t == 0, stop=t == NT - 1)
                ins.then_inc(sem("four_ft"), 1)

            ITS = [(h, t) for h in range(HEADS) for t in range(NT)]

            def scores(n):
                h, t = ITS[n]
                b = n % 2
                if n >= 2:
                    pe.wait_ge(sem("d_exp"), 2 * (n - 1))
                for c in range(2):
                    pe.matmul(bank[2 * b + c][:, :], qT[64 * c:64 * c + 64, h, t * P:t * P + P],
                              kT[64 * c:64 * c + 64, h, :], start=True, stop=True).then_inc(sem("d_s"), 1)

            def turn_diff(n):
                pe.wait_ge(sem("d_diff"), n + 1)
                if n >= 2:
                    pe.wait_ge(sem("d_diffT"), n - 1)
                for k in range(4):
                    ins = pe.transpose(bank[4 + n % 2][:, k * P:k * P + P], diff[:, n % 2, k * P:k * P + P], ident[:, :])
                ins.then_inc(sem("d_turn"), 1)

            def diff_v(n):
                h, t = ITS[n]
                pe.wait_ge(sem("d_diffT"), n + 1)
                if n >= 2:
                    pe.wait_ge(sem("d_o"), n - 1)
                for k in range(4):
                    ins = pe.matmul(bank[6 + n % 2][:, 0:P], diffT[:, n % 2, k, :], v_tok[:, k, h * P:h * P + P],
                                    start=k == 0, stop=k == 3)
                ins.then_inc(sem("d_pv"), 1)

            pe.wait_ge(sem("in_act"), 10)
            pe.wait_ge(sem("v_lat"), 2)
            scores(0)
            pe.wait_ge(sem("four_fts"), 2)
            pe.wait_ge(sem("four_gs"), 1)
            for f in range(2):
                for n in range(2):
                    ins = pe.matmul(bank[6][:, 256 * f:256 * f + 256], four_g[:, n, f, :],
                                    ftT[:, f, 256 * n:256 * n + 256], start=n == 0, stop=n == 1)
            ins.then_inc(sem("four_y"), 1)
            pe.wait_ge(sem("four_lo"), 2)
            for n in range(len(ITS)):
                if n + 1 < len(ITS):
                    scores(n + 1)
                turn_diff(n)
                if n >= 1:
                    diff_v(n - 1)
            diff_v(len(ITS) - 1)
            for t in range(NT):
                pe.wait_ge(*seen("xn", "sub", t + 1))
                for h in range(HEADS):
                    pe.transpose(bank[2 + h // 2][:, 256 * (h % 2) + t * P:256 * (h % 2) + t * P + P],
                                 o_tok[:, t, h * P:h * P + P], ident[:, :]).then_inc(sem("tr"), 1)
            pe.wait_ge(*seen("lo", "sub", HEADS))

            def dense(stage, n_chunks, ready=None, after=None, before=None):
                for c in range(n_chunks):
                    if before is not None:
                        before(c)
                    for j in range(2):
                        u = BASE[stage] + 2 * c + j
                        unit_wait(u)
                        half(u, j, xT_hi, xT_lo, bank[2 * (c % 2):2 * (c % 2) + 2], s_used,
                             ready if c == 0 else None)
                    if after is not None:
                        after(c)

            gate_mm("out")
            dense("out", 2)

            def ffn(layer, loops, first_job):
                base = BASE[f"ffn{layer}"]
                off = layer * FCH
                turn_norm(f"n_ffn{layer}", xn, bank[2:6])
                gate_mm(f"ffn{layer}")

                def up(c, u, i=None, ready=None):
                    for j in range(2):
                        unit_wait(u + j, i)
                        half(u + j, j, xT_hi, xT_lo, bank[0:2], s_used, ready)

                def down(c, u, i=None, first=False, last=False):
                    unit_wait(u, i)
                    pe.wait_ge(sem("hT_lo"), at(off + c + 1, i, 2))
                    wh = w_hi[u % N_SPLIT][:, :].rearrange("p (k n) -> p k n", k=2)
                    wl = w_lo[u % N_SPLIT][:, :].rearrange("p (k n) -> p k n", k=2)
                    for k in range(2):
                        for t in range(NT):
                            for h in range(2):
                                ins = three(bank[2 + 2 * h + t][:, :], hT_hi[:, k, t * P:t * P + P],
                                            hT_lo[:, k, t * P:t * P + P], wh[:, k, 512 * h:512 * h + 512],
                                            wl[:, k, 512 * h:512 * h + 512], first and k == 0, last and k == 1)
                    ins.then_inc(s_used, 1)

                def turn_hidden(c, i=None):
                    pe.wait_ge(sem("hid"), at(2 * (off + c) + 2, i, 4))
                    if c >= 1 or layer:
                        pe.wait_ge(sem("hT_lo"), at(off + c, i, 2))
                    for t in range(NT):
                        for k in range(2):
                            ins = pe.transpose(bank[6][:, 256 * k + t * P:256 * k + t * P + P],
                                               hid[:, t, k * P:k * P + P], ident[:, :])
                    ins.then_inc(sem("h_turn"), 1)

                up(0, base, None, f"n_ffn{layer}")
                pe.wait_ge(*seen("gate", f"ffn{layer}", 2))
                turn_hidden(0)
                job_reduce(first_job)
                pe.wait_ge(sem("zeros"), 1)
                for n in range(4):
                    pe.matmul(bank[2 + n][:, :], zeros[0:1, 0:P], zeros[0:1, :], start=True, stop=False)
                done = 0
                for q, n in loops:
                    with pe.Fori(0, n) as i:
                        for b in range(2):
                            u = base + 2 + 6 * done + 3 * b
                            c = 1 + 2 * done + b
                            up(c, u, i)
                            down(c - 1, u + 2, i)
                            if b == 1:
                                job_reduce(q, i)
                            turn_hidden(c, i)
                    done += n
                down(FCH - 1, base + 3 * FCH - 1, None, False, True)

            ffn(0, [(5, 5)], 4)
            turn_norm("n_pw1", xn, bank[2:6])

            def turn_pair(stage, src, free):
                def after(c):
                    pe.wait_ge(sem(f"{stage}_tok"), 2 * c + 2)
                    if c >= 1:
                        free(c)
                    for g in range(2):
                        for k in range(2):
                            for t in range(NT):
                                ins = pe.transpose(bank[4 + g][:, 256 * k + t * P:256 * k + t * P + P],
                                                   src[:, t, 256 * g + k * P:256 * g + k * P + P], ident[:, :])
                    ins.then_inc(sem(f"{stage}_turn"), 1)
                return after

            def pw1_free(c):
                pe.wait_ge(sem("pw1_glu"), 2 * c)

            def pw1_after(c):
                if c < 2:
                    job_reduce(10 + c)
                turn_pair("pw1", ag_tok, pw1_free)(c)

            dense("pw1", 4, "n_pw1", pw1_after)
            for k in range(KT):
                pe.wait_ge(sem("conv"), (CONV - 1) * KT + k + 1)
                if k == 0:
                    pe.wait_ge(sem("pw1_glu"), KT)
                ins = pe.matmul(bank[4][:, 0:S], ones[:, :], conv[:, k, :], start=k == 0, stop=k == KT - 1)
            ins.then_inc(sem("ln_mean_mm"), 1)
            pe.wait_ge(sem("ln_sq"), 1)
            for k in range(KT):
                ins = pe.matmul(bank[5][:, 0:S], ones[:, :], csq[:, k, :], start=k == 0, stop=k == KT - 1)
            ins.then_inc(sem("ln_var_mm"), 1)
            pe.wait_ge(*seen("lo", "ln", KT))
            gate_mm("pw2")
            pe.wait_ge(*seen("gate", "pw2", 2))
            gate_mm("pw2b", bias_gate)
            dense("pw2", 2)
            ffn(1, [(13, 3), (16, 2)], 12)

            gate_mm("final")
            pe.wait_ge(*seen("gate", "final", 2))
            turn_norm("n_rg", xn, bank[2:6])

            def rg_free(c):
                pe.wait_ge(sem("rg_u"), c)
                pe.wait_ge(sem("rg_g"), 2 * c)

            dense("rg_in", 4, "n_rg", turn_pair("rg_in", rg_tok, rg_free))
            pe.wait_ge(sem("rg_in_tok"), 8)
            pe.wait_ge(sem("rg_conv"), RG_CONV * KT)
            for n in range(2):
                pe.wait_ge(a_landed[n], 16 * (2 * len(JOBS) + 1))
                w = a_land[n][:, :].rearrange("p (h k j) -> p h k j", h=4, k=2)
                for jt in range(KT):
                    done = n * KT + jt
                    if done >= 4:
                        pe.wait_ge(sem("rg_sig"), done - 3)
                    h = jt // 2
                    for k in range(2):
                        ins = pe.matmul(bank[jt % 4][:, 0:S], w[:, h, k, P * (jt % 2):P * (jt % 2) + P],
                                        uc[:, 2 * h + k, :], start=k == 0, stop=k == 1)
                    ins.then_inc(sem("rg_gates"), 1)
            pe.wait_ge(*seen("lo", "rg", KT))
            gate_mm("rg_out")
            dense("rg_out", 2)

            turn_norm("n_kv", xn, bank[2:6])

            def attn_after(stage):
                def after(c):
                    if c >= 2:
                        return
                    for t in range(NT):
                        n = 2 * c + t
                        pe.wait_ge(sem(f"{stage}_tok"), n + 1)
                        if n >= 2:
                            pe.wait_ge(sem(f"{stage}_turned"), n - 1)
                        for h in range(4):
                            ins = pe.transpose(bank[4 + n % 2][:, h * P:h * P + P], a_tok[:, t, h * P:h * P + P], ident[:, :])
                        ins.then_inc(sem(f"{stage}_turn"), 1)
                return after

            def rows_read(stage):
                def before(c):
                    if c == 2:
                        pe.wait_ge(sem(f"{stage}_tok"), 2)
                    if c == 3:
                        pe.wait_ge(sem(f"{stage}_tok"), 4)
                return before

            dense("kv", 4, "n_kv", attn_after("kv"), rows_read("kv"))
            pe.wait_ge(sem("kv_turned"), 4)
            pe.wait_ge(sem("kv_rows"), 4)
            for t in range(NT):
                for k in range(KT):
                    pe.transpose(bank[2 + k // 2][:, 256 * (k % 2) + t * P:256 * (k % 2) + t * P + P],
                                 xn[:, t, k * P:k * P + P], ident[:, :]).then_inc(sem("tr"), 1)
            dense("att_in", 4, "n_att", attn_after("att_in"), rows_read("att_in"))

            A_ITS = [(h, t) for h in range(A_HEADS) for t in range(NT)]

            def a_scores(n):
                h, t = A_ITS[n]
                if n >= 2:
                    pe.wait_ge(sem("a_msk"), n - 1)
                pe.matmul(bank[n % 2][:, 0:(t + 1) * P], aqT[:, h, t * P:t * P + P], akT[:, h, 0:(t + 1) * P],
                          start=True, stop=True).then_inc(sem("a_s"), 1)

            def a_turn(n):
                h, t = A_ITS[n]
                pe.wait_ge(sem("a_exp"), n + 1)
                if n >= 2:
                    pe.wait_ge(sem("a_apT"), n - 1)
                for k in range(t + 1):
                    ins = pe.transpose(bank[2 + n % 2][:, k * P:k * P + P], ap_[:, n % 2, k * P:k * P + P], ident[:, :])
                ins.then_inc(sem("a_turn"), 1)

            def a_v(n):
                h, t = A_ITS[n]
                pe.wait_ge(sem("a_apT"), n + 1)
                if n >= 2:
                    pe.wait_ge(sem("a_o"), n - 1)
                for k in range(t + 1):
                    ins = pe.matmul(bank[4 + n % 2][:, 0:P], apT[:, n % 2, k, :], av[:, k, h * P:h * P + P],
                                    start=k == 0, stop=k == t)
                ins.then_inc(sem("a_pv"), 1)

            pe.wait_ge(sem("att_in_rows"), 4)
            pe.wait_ge(sem("att_in_turned"), 4)
            a_scores(0)
            for n in range(len(A_ITS)):
                if n + 1 < len(A_ITS):
                    a_scores(n + 1)
                a_turn(n)
                if n >= 1:
                    a_v(n - 1)
            a_v(len(A_ITS) - 1)
            pe.wait_ge(sem("a_o"), len(A_ITS))
            for t in range(NT):
                for k in range(KT):
                    pe.transpose(bank[k // 2][:, 256 * (k % 2) + t * P:256 * (k % 2) + t * P + P],
                                 ao[:, t, k * P:k * P + P], ident[:, :]).then_inc(sem("tr"), 1)
            pe.wait_ge(*seen("lo", "ao", KT))
            gate_mm("att_out")
            dense("att_out", 2)
            gate_mm("last")


CONSTS = ("k_ident", "k_rope", "k_dft", "k_dft64", "k_mask")


def constants():
    import numpy as np

    ident = np.eye(P, dtype=np.float32)
    grid_w = 64
    inv = np.float32(10000.0) ** (-np.arange(0, 32, 2, dtype=np.float32) / np.float32(32))
    row = np.repeat(np.arange(S // grid_w, dtype=np.float32), grid_w)
    col = np.tile(np.arange(grid_w, dtype=np.float32), S // grid_w)
    ang = np.concatenate([row[:, None] * inv, col[:, None] * inv], axis=-1).astype(np.float32)
    rope = np.stack([np.cos(ang), np.sin(ang)], axis=1).astype(np.float32)
    n = np.arange(S)
    a = 2 * np.pi * ((n[:, None] * n[None, :]) % S) / S
    dft = np.concatenate([np.cos(a), np.sin(a)], axis=1).astype(np.float32)
    m = np.arange(64)
    b = 2 * np.pi * ((m[:, None] * m[None, :]) % 64) / 64
    norm = 1.0 / np.sqrt(S * 64)
    d64 = np.zeros((2, P, P), np.float32)
    for g in range(2):
        r = slice(64 * g, 64 * g + 64)
        d64[0, r, r] = np.cos(b) * norm
        d64[1, r, r] = -np.sin(b) * norm
    mask = np.where(np.arange(P)[None, :] <= np.arange(P)[:, None], 0.0, NEG).astype(np.float32)
    return {"k_ident": ident, "k_rope": rope, "k_dft": dft, "k_dft64": d64, "k_mask": mask}


def kernel(**inputs):
    import numpy as np
    import concourse.bacc as bacc
    from concourse.bass_utils import run_bass_kernel_spmd

    nc = bacc.Bacc("TRN2", target_bir_lowering=False, num_devices=1)
    arrays, tensors = {}, {}
    for name, a in {**inputs, **constants()}.items():
        a = np.ascontiguousarray(a)
        arrays[name + "_dram"] = a
        tensors[name] = nc.dram_tensor(name + "_dram", a.shape, mybir.dt.from_np(a.dtype), kind="ExternalInput").ap()
    out = nc.dram_tensor("out_dram", (1, S, D), F32, kind="ExternalOutput").ap()
    build(nc, tensors, out)
    return run_bass_kernel_spmd(nc, [arrays], core_ids=[0]).results[0]["out_dram"]
```

```python
from contextlib import ExitStack

import concourse.bass as bass
from concourse import mybir

F32 = mybir.dt.float32
R32 = mybir.dt.float32r
BF16 = mybir.dt.bfloat16
ALU = mybir.AluOpType
ACT = mybir.ActivationFunctionType
AX_X = mybir.AxisListType.X

P = 128
D = 1024
KT = D // P
S = 256
NT = S // P
EPS = 1e-6
D_FF = 2816
DIFF_W = 768
HEADS = DIFF_W // P
KEYS = 2 * S
SUB_SCALE = 1.0 - 0.2
CONV = 31
PAD = CONV // 2
PE_TAPS = 12
RG_CONV = 4
RG_C = 8.0
A_HEADS = 8

UNIT = 2048
N_LAND = 6
N_SPLIT = 3
N_ALAND = 2
ADA0 = 8
FCH = D_FF // 256
NEG = -1e30

V_MOD0, V_KV, V_MOD1 = 12, 15, 17
JOBS = list(range(2, 20))

STAGES = [("in", 10), ("out", 4), ("ffn0", 3 * FCH), ("pw1", 8), ("pw2", 4), ("ffn1", 3 * FCH),
          ("rg_in", 8), ("rg_out", 4), ("kv", 8), ("att_in", 8), ("att_out", 4)]
BASE = {}
_n = 0
for _name, _count in STAGES:
    BASE[_name] = _n
    _n += _count
UNITS = _n

ROW_GROUPS = [
    [("ada_b", 96), ("c", 8), ("c_ctx", 8), ("c_2", 8), ("final_g", 8)],
    [("mod_b_2_0", 24), ("kv_mod_b_2", 16), ("mod_b_2_1", 24), ("mix_norm_g", 16), ("ffn_norm_g", 16), ("norm_g_2", 16),
     ("kv_norm_g_2", 8), ("final_norm_g_2", 8)],
    [("od_pw1_b", 16), ("od_dw_b", 8), ("od_ln_g", 8), ("od_ln_b", 8), ("od_pw2_b", 8),
     ("rg_conv_b_2", 8), ("rg_b_a_2", 8), ("rg_b_x_2", 8), ("rg_lambda_2", 8), ("rg_conv_w_2", 32),
     ("ev_subln_g", 1)],
    [("od_dw_w_a", 16 * 8)],
    [("od_dw_w_b", 15 * 8)],
]
COL = {}
for _g, _rows in enumerate(ROW_GROUPS):
    _r = 0
    for _name, _count in _rows:
        COL[_name] = _g * P + _r
        _r += _count

NORMED = {"ss": 2 * NT, "ms": 1, "rstd": 1, "xn": NT, "tr": 2 * KT, "full": KT, "hi": KT, "lo": KT}
SPLIT = {"full": KT, "hi": KT, "lo": KT}
WHOLE = {**NORMED, "ss": NT}
RESCALED = {"ss": 2 * NT, "ms": 1, "rstd": 1, "xn": NT}
GATED = {"diag": 1, "gmm": 1, "gate": 2}
PRODUCT = {**GATED, "part": 2}
STEPS = [("n_x", WHOLE), ("n_ctx", WHOLE),
         ("sub", {"ss": 12, "ms": 1, "rstd": 1, "xn": NT, "tr": 2 * HEADS, "full": HEADS, "hi": HEADS, "lo": HEADS}),
         ("out", PRODUCT), ("n_ffn0", NORMED), ("ffn0", {**GATED, "part": 3}), ("n_pw1", NORMED), ("ln", {"ms": 1, "rstd": 1, **SPLIT}), ("pw2", PRODUCT),
         ("pw2b", GATED), ("n_ffn1", NORMED), ("ffn1", {**GATED, "part": 3}), ("n_final", RESCALED), ("final", GATED),
         ("n_rg", WHOLE), ("rg", SPLIT), ("rg_out", PRODUCT), ("n_kv", NORMED), ("n_att", {"tr": 2 * KT, **SPLIT}),
         ("ao", {"tr": 2 * KT, "hi": KT, "lo": KT}), ("att_out", PRODUCT), ("n_last", RESCALED), ("last", GATED)]
STEPS_BEFORE = {}
_seen = {}
for _stage, _adds in STEPS:
    for _kind, _count in _adds.items():
        STEPS_BEFORE[_kind, _stage] = _seen.get(_kind, 0)
        _seen[_kind] = _seen.get(_kind, 0) + _count


RG_GROUPS = [(0, 0), (0, 1), (1, 0), (1, 1), (0, 2), (0, 3), (1, 2), (1, 3)]


def rg_sigs(n, k):
    return 2 * RG_GROUPS.index((n, k // 2)) + k % 2 + 1


def at(base, i=None, step=0):
    return base if i is None else i * step + base


def build(nc, t_in, out):
    with ExitStack() as ctx:
        sems = {}

        def sem(name):
            if name not in sems:
                sems[name] = ctx.enter_context(nc.semaphore(name))
            return sems[name]

        def seen(kind, stage, n):
            return sem(kind), STEPS_BEFORE[kind, stage] + n

        ARENA = 16512

        def place(name, shape, offset, dtype=F32):
            return nc.alloc_sbuf_tensor_at(name, shape, dtype, offset=ARENA + offset)

        KB = 1024
        w_land = [place(f"w_land{i}", [P, UNIT], 8 * KB * i) for i in range(N_LAND)]
        w_hi = [place(f"w_hi{i}", [P, UNIT], (48 + 8 * i) * KB, R32) for i in range(N_SPLIT)]
        w_lo = [place(f"w_lo{i}", [P, UNIT], (72 + 8 * i) * KB, R32) for i in range(N_SPLIT)]
        a_land = [place(f"a_land{i}", [P, UNIT], (96 + 8 * i) * KB) for i in range(N_ALAND)]
        job_sum = place("job_sum", [P, D], 112 * KB)
        BIG = 116 * KB
        xT_hi = place("xT_hi", [P, KT, S], 164 * KB, R32)
        xT_lo = place("xT_lo", [P, KT, S], 172 * KB, R32)
        x = place("x", [P, NT, D], 180 * KB)
        S1 = 188 * KB
        xn = place("xn", [P, NT, D], S1)
        xfull = place("xfull", [P, KT, S], BIG + 40 * KB)
        gate = place("gate", [P, D], 196 * KB)
        SMALL = [200 * KB]

        def small(name, shape):
            size = 4
            for n in shape[1:]:
                size *= n
            offset = SMALL[0]
            SMALL[0] += -(-size // 32) * 32
            assert ARENA + SMALL[0] <= 229344
            return place(name, shape, offset)

        ident = small("ident", [P, P])
        ones = small("ones", [P, P])
        pcol = small("pcol", [P, 5 * P])
        mcol = small("mcol", [P, 20 * KT])
        mcol_ctx = small("mcol_ctx", [P, 2 * KT])
        silu_c = small("silu_c", [P, 3, KT])
        four_g = small("four_g", [P, 2, 2, P])
        rope = small("rope", [P, NT, 2, 32])
        mask = place("mask", [P, P], SMALL[0] - 512)
        a_col = small("a_col", [P, KT])
        b_col = small("b_col", [P, KT])
        ss = small("ss", [P, 12])
        ms = small("ms", [P, 12])
        rstd = small("rstd", [P, 12])
        neg_half = small("neg_half", [P, 12])
        lam_tmp = small("lam_tmp", [P, 8])
        mx = small("mx", [P, 2, 2])
        nb = small("nb", [P, 2, 2])
        esum = small("esum", [P, 2, 2])
        rsum = small("rsum", [P, 2, 2])
        sp_c = small("sp_c", [P, 8, KT])
        prow = place("prow", [P, 5, P], 112 * KB)
        ctx_x = place("ctx_x", [P, NT, D], BIG)
        ctx_full = place("ctx_full", [P, KT, S], BIG)
        ada_rows = place("ada_rows", [2, 2 * D], BIG + 8 * KB)
        ctx_junk = place("ctx_junk", [P, NT, D], BIG + 18 * KB)
        lam_in = place("lam_in", [P, 4, 64], BIG + 16 * KB)
        lam_junk = place("lam_junk", [P, 2, 64], BIG + 17 * KB)
        ctxT_hi = place("ctxT_hi", [P, KT, S], BIG + 32 * KB, R32)
        ctxT_lo = place("ctxT_lo", [P, KT, S], BIG + 40 * KB, R32)
        qT = place("qT", [P, HEADS, S], BIG)
        kT = place("kT", [P, HEADS, KEYS], BIG + 6 * KB)
        v_tok = place("v_tok", [P, 4, DIFF_W], BIG + 18 * KB)
        f_tok = place("f_tok", [P, NT, S], BIG + 30 * KB)
        rope_cos = place("rope_cos", [P, 512], 196 * KB)
        rope_sin = place("rope_sin", [P, 512], 198 * KB)
        rot = place("rot", [P, 2, 512], S1)
        k_ctx = place("k_ctx", [P, 2, 512], S1 + 4 * KB)
        prob = place("prob", [P, 2, 2, 512], BIG + 32 * KB)
        diff = place("diff", [P, 2, 512], BIG + 40 * KB)
        diffT = place("diffT", [P, 2, 4, P], BIG + 44 * KB)
        o_tok = place("o_tok", [P, NT, DIFF_W], S1)
        o_full = place("o_full", [P, HEADS, S], BIG + 40 * KB)
        dft = place("dft", [P, NT, 512], 196 * KB)
        ftT = place("ftT", [P, 2, 512], S1 + 4 * KB)
        four_c = place("four_c", [P, 2, P], BIG + 26 * KB)
        four_w = place("four_w", [P, 2, P], BIG + 27 * KB)
        sq_junk = place("sq_junk", [P, 2, P], S1 + 6 * KB)
        silu_g = place("silu_g", [P, NT, 256], BIG)
        hid = place("hid", [P, NT, 256], BIG + 2 * KB)
        hT_hi = place("hT_hi", [P, 2, S], BIG + 4 * KB, R32)
        hT_lo = place("hT_lo", [P, 2, S], BIG + 6 * KB, R32)
        zeros = place("zeros", [P, 512], BIG + 8 * KB, BF16)
        UP = S + 2 * PAD
        u_pad = place("u_pad", [P, KT, UP], BIG)
        conv = place("conv", [P, KT, S], BIG + 9 * KB)
        ag_tok = place("ag_tok", [P, NT, 512], BIG + 17 * KB)
        sig = place("sig", [P, 2, S], BIG + 21 * KB)
        csq = place("csq", [P, KT, S], BIG + 23 * KB)
        mean = place("mean", [P, S], BIG + 31 * KB)
        rln = place("rln", [P, S], BIG + 32 * KB)
        tap_diag = [place("tap_diag0", [P, PE_TAPS, P], BIG + 23 * KB), place("tap_diag1", [P, PE_TAPS, P], BIG + 38 * KB)]
        bias_gate = place("bias_gate", [P, D], BIG + 34 * KB)
        RUP = S + RG_CONV - 1
        ru_pad = place("ru_pad", [P, KT, RUP], BIG)
        gT = place("gT", [P, KT, S], BIG + 9 * KB)
        rg_tok = place("rg_tok", [P, NT, 512], BIG + 17 * KB)
        uc = place("uc", [P, KT, S], BIG + 21 * KB)
        r_gate = place("r_gate", [P, KT, S], BIG + 29 * KB)
        i_gate = place("i_gate", [P, KT, S], BIG + 37 * KB)
        b_seq = place("b_seq", [P, KT, S], BIG)
        y_full = place("y_full", [P, KT, S], S1)
        rg_w = [place(f"rg_w{n}", [P, 4, 2, S], (96 + 8 * n) * KB) for n in range(2)]
        akT = place("akT", [P, KT, S], BIG)
        aqT = place("aqT", [P, KT, S], BIG + 8 * KB)
        av = place("av", [P, NT, D], BIG + 16 * KB)
        ag = place("ag", [P, NT, D], BIG + 24 * KB)
        a_tok = place("a_tok", [P, NT, 512], BIG + 32 * KB)
        ap_ = place("ap_", [P, 2, S], BIG + 36 * KB)
        apT = place("apT", [P, 2, NT, P], BIG + 38 * KB)
        ao = place("ao", [P, NT, D], BIG + 40 * KB)
        kv_full = place("kv_full", [P, KT, S], BIG + 40 * KB)
        last_gate = place("last_gate", [P, D], BIG)
        tmp = place("tmp", [P, 2, 512], S1)
        sq_half = place("sq_half", [P, 2, 512], S1 + 4 * KB)

        bank = [ctx.enter_context(nc.psum_tensor(f"bank{i}", [P, 512], F32)) for i in range(8)]
        COLS = bank[7]

        landed = [sem(f"w_landed{i}") for i in range(N_LAND)]
        a_landed = [sem(f"a_landed{i}") for i in range(N_ALAND)]
        s_hi, s_lo, s_used = sem("w_hi"), sem("w_lo"), sem("w_used")
        s_step, s_red, s_cols = sem("job_step"), sem("job_reduced"), sem("job_cols")

        def kview(w, n=None):
            return w.rearrange("(k p) n -> p k n", p=P)

        def pc(name, k=0, n=1):
            return pcol[:, COL[name] + k:COL[name] + k + n]

        def mc(v, k=0, n=KT):
            return mcol[:, v * KT + k:v * KT + k + n]

        block = ctx.enter_context(nc.Block())

        @block.sync
        def _(sp):
            def load_unit(u, parts, i=None):
                n = u + ADA0
                if n >= N_LAND:
                    if n - N_LAND < ADA0:
                        sp.wait_ge(sem("ada0_used"), n - N_LAND + 1)
                    else:
                        sp.wait_ge(s_lo, at(n - N_LAND - ADA0 + 1, i, 6))
                slot = n % N_LAND
                for view, src in parts(w_land[slot]):
                    sp.dma_start(view, src).then_inc(landed[slot], 16)

            def cols_half(w, col, j):
                def parts(land):
                    v = land[:, :].rearrange("p (k n) -> p k n", k=4)
                    return [(v[:, 2 * h:2 * h + 2, :],
                             kview(w)[:, 4 * j + 2 * h:4 * j + 2 * h + 2, bass.ds(col, 512)]) for h in range(2)]
                return parts

            def cols_pair(wa, ca, wb, cb, j):
                def parts(land):
                    v = land[:, :].rearrange("p (k n) -> p k n", k=4)
                    return [(v[:, :, 256 * h:256 * h + 256], kview(w)[:, 4 * j:4 * j + 4, bass.ds(c, 256)])
                            for h, (w, c) in enumerate(((wa, ca), (wb, cb)))]
                return parts

            def rows_pair(w, row, col=0):
                def parts(land):
                    v = land[:, :].rearrange("p (k n) -> p k n", k=2)
                    return [(v[:, h, :], w[bass.ds(row + h * P, P), col:col + D]) for h in range(2)]
                return parts

            ada = t_in["ada_w"]
            w_in = t_in["ev_w_in"][0]

            def rows(name, src, n, g, r):
                sp.dma_start(prow[r:r + n, g, :], src).then_inc(sem(f"prow{g}"), 16)

            def as_rows(name):
                h = t_in[name]
                if len(h.shape) == 1:
                    return h.rearrange("(r p) -> r p", p=P)
                if len(h.shape) == 3:
                    h = h[0]
                return h.rearrange("a (r p) -> (a r) p", p=P)

            def load_rows(g):
                r = 0
                for name, n in ROW_GROUPS[g]:
                    if name == "od_dw_w_a":
                        src = as_rows("od_dw_w")[0:n, :]
                    elif name == "od_dw_w_b":
                        src = as_rows("od_dw_w")[P:P + n, :]
                    elif name in ("mod_b_2_0", "mod_b_2_1"):
                        layer = int(name[-1])
                        src = as_rows("mod_b_2")[n * layer:n * layer + n, :]
                    else:
                        src = as_rows(name)
                    rows(name, src, n, g, r)
                    r += n

            sp.dma_start(ident[:, :], t_in["k_ident"]).then_inc(sem("ident_in"), 16)
            load_rows(0)
            sp.dma_start(x[:, :, :], t_in["x"][0].rearrange("(t p) d -> p t d", p=P)).then_inc(sem("x_in"), 16)
            for n in range(4):
                load_unit(n - ADA0, rows_pair(ada[0], n * 256))
            load_rows(1)
            for n in range(4, 6):
                load_unit(n - ADA0, rows_pair(ada[0], (n - 4) * 256, D))
            for g in (2, 3, 4):
                load_rows(g)
            sp.dma_start(rope[:, :, :, :], t_in["k_rope"].rearrange("(t p) c d -> p t c d", p=P)).then_inc(sem("rope_in"), 16)
            for n, name in enumerate(("ev_lambda_q1", "ev_lambda_k1", "ev_lambda_q2", "ev_lambda_k2")):
                sp.dma_start(lam_in[:, n, :], t_in[name][0:1, :].broadcast_to([P, 64])).then_inc(sem("lam_in"), 16)
            for n in range(6, ADA0):
                load_unit(n - ADA0, rows_pair(ada[0], (n - 4) * 256, D))

            in_cols = [lambda j: cols_half(w_in, 0, j), lambda j: cols_pair(w_in, 512, w_in, 3 * DIFF_W, j),
                       lambda j: cols_half(w_in, 768, j), lambda j: cols_half(w_in, 1280, j),
                       lambda j: cols_half(w_in, 1792, j)]
            for c in range(5):
                for j in range(2):
                    load_unit(2 * c + j, in_cols[c](j))
                if c == 0:
                    sp.dma_start(ctx_x[:, :, :], t_in["ctx"][0].rearrange("(t p) d -> p t d", p=P)).then_inc(sem("ctx_in"), 16)
                    sp.dma_start(four_c[:, :, :], t_in["k_dft64"].rearrange("c p n -> p c n")).then_inc(sem("four_in"), 16)
                    sp.wait_ge(sem("four_zero"), 1)
                    for g in range(4):
                        r = 64 * (g % 2)
                        sp.dma_start(four_w[r:r + 64, g // 2, r:r + 64], t_in["ev_fourier_w"][0, g]).then_inc(sem("four_in"), 16)

            def load_dense(stage, w, n_cols):
                for c in range(n_cols // 512):
                    for j in range(2):
                        load_unit(BASE[stage] + 2 * c + j, cols_half(w, 512 * c, j))

            def load_ffn(layer, loops):
                w1, w3, w2 = (t_in[n][layer] for n in ("ffn_w1", "ffn_w3", "ffn_w2"))
                base = BASE[f"ffn{layer}"]
                for j in range(2):
                    load_unit(base + j, cols_pair(w1, 0, w3, 0, j))
                done = 0
                for n in loops:
                    with sp.Fori(0, n) as i:
                        for b in range(2):
                            u = base + 2 + 6 * done + 3 * b
                            c = 1 + 2 * done + b
                            for j in range(2):
                                load_unit(u + j, cols_pair(w1, i * 512 + 256 * c, w3, i * 512 + 256 * c, j), i)
                            load_unit(u + 2, rows_pair(w2, i * 512 + 256 * (c - 1)), i)
                    done += n
                load_unit(base + 3 * FCH - 1, rows_pair(w2, 256 * (FCH - 1)))

            load_dense("out", t_in["ev_w_out"][0], D)
            load_ffn(0, (5,))

            def load_pairs(stage, w):
                for c in range(4):
                    for j in range(2):
                        load_unit(BASE[stage] + 2 * c + j, cols_pair(w, 256 * c, w, D + 256 * c, j))

            load_pairs("pw1", t_in["od_pw1_w"][0])
            load_dense("pw2", t_in["od_pw2_w"][0], D)
            load_ffn(1, (5,))
            load_dense("rg_in", t_in["rg_w_in_2"][0], 2 * D)
            load_dense("rg_out", t_in["rg_w_out_2"][0], D)
            load_dense("kv", t_in["w_kv_2"], 2 * D)
            load_dense("att_in", t_in["att_w_in_2"][0], 2 * D)
            load_dense("att_out", t_in["att_w_out_2"][0], D)
            for t in range(NT):
                sp.wait_ge(sem("result"), t + 1)
                sp.dma_start(out[0, t * P:(t + 1) * P, :], xn[:, t, :]).then_inc(sem("stored"), 16)
            sp.wait_ge(sem("stored"), 16 * NT)

        @block.gpsimd
        def _(pool):
            pool.memset(ones[:, :], 1.0).then_inc(sem("ones"), 1)
            pool.memset(neg_half[:, :], -0.5).then_inc(sem("ones"), 1)
            pool.memset(four_w[:, :, :], 0.0).then_inc(sem("four_zero"), 1)
            pool.wait_ge(sem("ones"), 2)

            def pow_half(stage, n):
                pool.wait_ge(*seen("ms", stage, 1))
                pool.tensor_tensor(rstd[:, 0:n], ms[:, 0:n], neg_half[:, 0:n], ALU.pow).then_inc(sem("rstd"), 1)

            def load_job(q, w, col, units=range(4), i=None):
                for j in units:
                    a = 4 * q + j
                    if a >= N_ALAND:
                        pool.wait_ge(s_step, at(2 * (a - N_ALAND) + 2, i, 8))
                    pool.dma_start(a_land[j % 2][:, :].rearrange("p (k n) -> p k n", k=2),
                                   kview(w)[:, 2 * j:2 * j + 2, bass.ds(col, D)]).then_inc(a_landed[j % 2], 16)

            ada = [t_in["ada_w"][n] for n in range(2)]
            mod = [t_in["mod_w_2"][n] for n in range(2)]

            pow_half("n_x", NT)
            pow_half("n_ctx", NT)
            for q in range(3):
                load_job(q, ada[0], (q + 2) * D, range(2))
                if q == 2:
                    pool.wait_ge(sem("rot"), 16)
                    pool.dma_start(dft[:, :, :], t_in["k_dft"].rearrange("(t p) n -> p t n", p=P)).then_inc(sem("dft_in"), 16)
                load_job(q, ada[0], (q + 2) * D, range(2, 4))
            load_job(3, ada[0], 5 * D, range(2))
            pool.wait_ge(sem("rot"), 16)
            pool.dma_start(mask[:, :], t_in["k_mask"]).then_inc(sem("mask_in"), 16)
            pow_half("sub", 12)
            load_job(3, ada[0], 5 * D, range(2, 4))
            load_job(4, ada[1], 0, (0,))

            def zero_ffn(n):
                pool.memset(zeros[:, :], 0.0).then_inc(sem("zeros"), 1)

            pow_half("n_ffn0", NT)
            load_job(4, ada[1], 0, (1,))
            zero_ffn(0)
            with pool.Fori(0, 5) as i:
                load_job(4, ada[1], i * D, range(2, 4), i)
                load_job(5, ada[1], i * D + D, range(2), i)
            load_job(9, ada[1], 5 * D, range(2, 4))
            load_job(10, mod[0], 0, range(2))
            pow_half("n_pw1", NT)
            pool.wait_ge(sem("xres"), 8)
            pool.memset(u_pad[:, :, 0:PAD], 0.0).then_inc(sem("u_zero"), 1)
            pool.memset(u_pad[:, :, PAD + S:UP], 0.0).then_inc(sem("u_zero"), 1)
            pow_half("ln", NT)
            pow_half("n_ffn1", NT)
            zero_ffn(1)
            with pool.Fori(0, 2) as i:
                load_job(10, mod[0], i * D, range(2, 4), i)
                load_job(11, mod[0], i * D + D, range(2), i)
            load_job(12, mod[0], 2 * D, range(2, 4))
            for q in (13, 14):
                load_job(q, t_in["kv_mod_w_2"], (q - 13) * D)
            load_job(15, mod[1], 0)
            pool.wait_ge(s_step, 8 * 16)
            for n, name in enumerate(("rg_w_a_2", "rg_w_x_2")):
                pool.dma_start(rg_w[n][:, :, :, :], t_in[name][0].rearrange("h (k p) j -> p h k j", p=P)).then_inc(sem(f"rg_w{n}"), 16)
            pow_half("n_final", NT)
            pow_half("n_rg", NT)
            pool.wait_ge(sem("xres"), 16)
            pool.memset(ru_pad[:, :, 0:RG_CONV - 1], 0.0).then_inc(sem("ru_zero"), 1)
            for k in range(KT):
                pool.wait_ge(sem("rg_sig"), rg_sigs(1, k))
                pool.tensor_tensor(i_gate[:, k, :], i_gate[:, k, :], uc[:, k, :], ALU.mult).then_inc(sem("rg_iu"), 1)
            for k in range(0, KT, 2):
                pool.wait_ge(sem("rg_a"), k + 1)
                pool.tensor_tensor(y_full[:, k, :], r_gate[:, k, :], r_gate[:, k, :], ALU.mult).then_inc(sem("rg_a2"), 1)
            pool.wait_ge(sem("rg_gates"), len(RG_GROUPS))
            load_job(16, mod[1], D, range(2))
            pow_half("n_kv", NT)
            load_job(16, mod[1], D, range(2, 4))
            load_job(17, mod[1], 2 * D)
            pow_half("n_last", NT)

        @block.scalar
        def _(act):
            def split_hi(u, i=None):
                if u >= UNITS:
                    return
                n = u + ADA0
                act.wait_ge(landed[n % N_LAND], at(32 * (n // N_LAND + 1), i, 32))
                if u >= N_SPLIT:
                    act.wait_ge(s_used, at(u - N_SPLIT + 1, i, 6))
                act.activation(w_hi[u % N_SPLIT][:, :], w_land[n % N_LAND][:, :], ACT.Copy).then_inc(s_hi, 1)

            def norm_square(stage, src, junk):
                for t in range(NT):
                    act.activation(junk[:, t, :], src[:, t, :], ACT.Square,
                                   accum_out=ss[:, t:t + 1]).then_inc(sem("ss"), 1)

            def half_squares(stage, residual_steps, ns=range(2 * NT)):
                for n in ns:
                    c, t = n // NT, n % NT
                    act.wait_ge(sem("xres"), residual_steps + n + 1)
                    if n >= 2:
                        act.wait_ge(*seen("ss", stage, n - 1))
                    act.activation(sq_half[:, n % 2, :], x[:, t, 512 * c:512 * c + 512], ACT.Square,
                                   accum_out=ss[:, 2 * t + c:2 * t + c + 1]).then_inc(sem("ss"), 1)

            def full_hi(stage, full, hi, ks=range(KT)):
                for n, k in enumerate(ks):
                    act.wait_ge(*seen("full", stage, n + 1))
                    act.activation(hi[:, k, :], full[:, k, :], ACT.Copy).then_inc(sem("hi"), 1)

            def gate_copy(stage, dst=None, b=4):
                dst = gate if dst is None else dst
                act.wait_ge(*seen("gmm", stage, 1))
                for h in range(2):
                    act.activation(dst[:, 512 * h:512 * h + 512], bank[b + h][:, :], ACT.Copy).then_inc(sem("gate"), 1)

            act.wait_ge(sem("cols_in"), 1)
            act.activation(silu_c[:, :, :], pcol[:, COL["c"]:COL["c"] + 24].rearrange("p (c k) -> p c k", c=3),
                           ACT.Silu).then_inc(sem("silu_c"), 1)
            act.wait_ge(sem("x_in"), 16)
            norm_square("n_x", x, xn)
            split_hi(0)
            split_hi(1)
            act.wait_ge(sem("ada0_used"), ADA0)
            for n in range(4):
                act.activation(ada_rows[:, 512 * n:512 * n + 512], bank[n][0:2, :], ACT.Copy).then_inc(sem("ada0_rows"), 1)
            act.wait_ge(sem("lam_dot"), 2)
            act.activation(lam_tmp[:, 2:4], lam_tmp[:, 0:2], ACT.Exp).then_inc(sem("lam_exp"), 1)
            act.wait_ge(sem("sp_abs"), 1)
            act.activation(sp_c[:, 1, :], sp_c[:, 0, :], ACT.Exp, scale=-1.0).then_inc(sem("sp_exp"), 1)
            full_hi("n_x", xfull, xT_hi)

            turned = [0]

            def turn_copy(dst, h0, nh, tok):
                n = turned[0]
                turned[0] += 1
                act.wait_ge(sem("turn"), n + 1)
                act.activation(dst[:, h0:h0 + nh, tok:tok + P],
                               bank[(4, 6)[n % 2]][:, 0:nh * P].rearrange("p (h s) -> p h s", h=nh),
                               ACT.Copy).then_inc(sem("turn_out"), 1)

            def turns(c):
                if c in (0, 1):
                    for t in range(NT):
                        turn_copy(qT, 4 * c, 4 - 2 * c, t * P)
                if c in (2, 3):
                    for src in range(2):
                        for t in range(NT):
                            turn_copy(kT, 4 * (c - 2), 4 - 2 * (c - 2), (S if src == 0 else 0) + t * P)

            for c in range(5):
                split_hi(2 * c + 2)
                if c == 0:
                    act.wait_ge(sem("ctx_in"), 16)
                    act.wait_ge(*seen("rstd", "n_x", 1))
                    norm_square("n_ctx", ctx_x, ctx_junk)
                if c == 1:
                    act.wait_ge(sem("four_gmm"), 1)
                    act.activation(four_g[:, :, :, :].rearrange("p c f n -> p (c f n)"), bank[2][:, :], ACT.Copy).then_inc(sem("four_gs"), 1)
                    full_hi("n_ctx", ctx_full, ctxT_hi)
                if c < 2:
                    split_hi(2 * c + 3)
                if c == 1:
                    act.wait_ge(*seen("lo", "n_ctx", KT))
                if c >= 1:
                    turns(c - 1)
                if c >= 2:
                    split_hi(2 * c + 3)
                if c == 2:
                    act.wait_ge(s_used, 6)
                    for t in range(NT):
                        act.activation(k_ctx[:, t, :], bank[2 + t][:, :], ACT.Copy).then_inc(sem("in_act"), 1)
                if c == 3:
                    act.wait_ge(s_used, 8)
                    act.wait_ge(sem("turn"), 8)
                    for t in range(NT):
                        act.activation(k_ctx[:, t, 0:256], bank[2 + t][:, 0:256], ACT.Copy).then_inc(sem("in_act"), 1)
                        act.activation(v_tok[:, t, 0:256], bank[2 + t][:, 256:512], ACT.Copy).then_inc(sem("in_act"), 1)
                if c == 4:
                    for src, tile in ((0, NT), (1, 0)):
                        act.wait_ge(*((sem("in_lat"), 3) if src == 0 else (s_used, 10)))
                        for t in range(NT):
                            act.activation(v_tok[:, tile + t, 256:768], bank[2 * src + t][:, :], ACT.Copy).then_inc(sem("in_act"), 1)

            for f in range(2):
                act.wait_ge(sem("four_ft"), f + 1)
                act.activation(ftT[:, f, :], bank[4 + f][:, :], ACT.Copy).then_inc(sem("four_fts"), 1)
            ITS = [(h, t) for h in range(HEADS) for t in range(NT)]

            def exps(n):
                for c in range(2):
                    act.wait_ge(sem("d_nb"), n + 1)
                    if n >= 2:
                        act.wait_ge(sem("d_diff"), n - 1)
                    act.activation(prob[:, n % 2, c, :], bank[2 * (n % 2) + c][:, :], ACT.Exp, scale=0.125,
                                   bias=nb[:, n % 2, c:c + 1], accum_out=esum[:, n % 2, c:c + 1]).then_inc(sem("d_exp"), 1)

            def head_out(n):
                h, t = ITS[n]
                act.wait_ge(sem("d_pv"), n + 1)
                act.activation(o_tok[:, t, h * P:h * P + P], bank[6 + n % 2][:, 0:P], ACT.Copy,
                               scale=rsum[:, n % 2, 0:1]).then_inc(sem("d_o"), 1)

            exps(0)
            act.wait_ge(sem("four_y"), 1)
            for f in range(2):
                act.activation(xT_hi[:, HEADS + f, :], bank[6][:, 256 * f:256 * f + 256], ACT.Copy).then_inc(sem("four_hi"), 1)

            for n in range(len(ITS)):
                if n + 1 < len(ITS):
                    exps(n + 1)
                act.wait_ge(sem("d_turn"), n + 1)
                if n >= 2:
                    act.wait_ge(sem("d_pv"), n - 1)
                act.activation(diffT[:, n % 2, :, :].rearrange("p k s -> p (k s)"), bank[4 + n % 2][:, :], ACT.Copy).then_inc(sem("d_diffT"), 1)
                if n >= 1:
                    head_out(n - 1)
            head_out(len(ITS) - 1)
            full_hi("sub", o_full, xT_hi, range(HEADS))

            def dense_out(stage, after, residual_steps):
                split_hi(BASE[stage] + 2)
                split_hi(BASE[stage] + 3)
                gate_copy(stage)
                if stage == "pw2":
                    gate_copy("pw2b", bias_gate, 6)
                if stage == "att_out":
                    gate_copy("last", last_gate, 6)
                half_squares(after, residual_steps, (0, 1))
                split_hi(BASE[stage] + 4)
                split_hi(BASE[stage] + 5)
                half_squares(after, residual_steps, (2, 3))

            dense_out("out", "n_ffn0", 0)

            def ffn(layer, loops):
                base = BASE[f"ffn{layer}"]
                off = layer * FCH
                full_hi(f"n_ffn{layer}", xfull, xT_hi)

                def silu(c, u, i=None):
                    act.wait_ge(s_used, at(u + 2, i, 6))
                    for t in range(NT):
                        act.activation(silu_g[:, t, :], bank[t][:, 0:256], ACT.Silu).then_inc(sem("silu_g"), 1)

                def hidden_hi(c, i=None):
                    act.wait_ge(sem("h_turn"), at(off + c + 1, i, 2))
                    act.activation(hT_hi[:, :, :].rearrange("p k s -> p (k s)"), bank[6][:, :], ACT.Copy).then_inc(sem("hT_hi"), 1)

                split_hi(base + 2)
                silu(0, base)
                split_hi(base + 3)
                hidden_hi(0)
                gate_copy(f"ffn{layer}")
                if layer == 1:
                    gate_copy("final", bias_gate)
                done = 0
                for n in loops:
                    with act.Fori(0, n) as i:
                        for b in range(2):
                            u = base + 2 + 6 * done + 3 * b
                            c = 1 + 2 * done + b
                            split_hi(u + 2, i)
                            split_hi(u + 3, i)
                            silu(c, u, i)
                            split_hi(u + 4, i)
                            hidden_hi(c, i)
                    done += n
                split_hi(base + 3 * FCH + 1)
                half_squares(("n_pw1", "n_final")[layer], 4 + 8 * layer)

            ffn(0, (5,))

            def rows_out(stage, dst, chunks, n0=0):
                for c in chunks:
                    split_hi(BASE[stage] + 2 * c + 2)
                    split_hi(BASE[stage] + 2 * c + 3)
                    act.wait_ge(s_used, BASE[stage] + 2 * c + 2)
                    if c >= 1:
                        act.wait_ge(sem(f"{stage}_turn"), c)
                    for t in range(NT):
                        act.activation(dst[:, t, :], bank[2 * (c % 2) + t][:, :], ACT.Copy).then_inc(sem(f"{stage}_tok"), 1)
                    yield c

            full_hi("n_pw1", xfull, xT_hi)
            for c in rows_out("pw1", ag_tok, range(4)):
                act.wait_ge(sem("pw1_turn"), c + 1)
                if c >= 1:
                    act.wait_ge(sem("pw1_glu"), 2 * c)
                for e in range(2):
                    act.activation(sig[:, e, :], bank[5][:, 256 * e:256 * e + 256], ACT.Sigmoid,
                                   bias=pc("od_pw1_b", KT + 2 * c + e)).then_inc(sem("pw1_sig"), 1)
                if c >= 1:
                    act.wait_ge(sem("conv_pe"), c)
                for e in range(2):
                    for n in range(PE_TAPS):
                        w = COL["od_dw_w_a"] + (CONV - PE_TAPS + n) * KT + 2 * c + e
                        act.activation(tap_diag[e][:, n, :], ident[:, :], ACT.Copy, scale=pcol[:, w:w + 1]).then_inc(sem("tap_diag"), 1)
            for k in range(KT):
                act.wait_ge(sem("ln_xc"), k + 1)
                act.activation(csq[:, k, :], conv[:, k, :], ACT.Square).then_inc(sem("ln_sq"), 1)
            for k in range(KT):
                act.wait_ge(sem("ln_norm"), k + 1)
                act.activation(xfull[:, k, :], csq[:, k, :], ACT.Silu, scale=pc("od_ln_g", k),
                               bias=pc("od_ln_b", k)).then_inc(sem("full"), 1)
                act.wait_ge(*seen("full", "ln", k + 1))
                act.activation(xT_hi[:, k, :], xfull[:, k, :], ACT.Copy).then_inc(sem("hi"), 1)
            dense_out("pw2", "n_ffn1", 8)
            ffn(1, (3, 2))

            act.wait_ge(sem("x_final"), 2)
            norm_square("n_rg", x, xn)
            full_hi("n_rg", xfull, xT_hi)
            base = BASE["rg_in"]

            def rg_rows(c):
                act.wait_ge(s_used, base + 2 * c + 2)
                if c >= 1:
                    act.wait_ge(sem("rg_in_turn"), c)
                for t in range(NT):
                    act.activation(rg_tok[:, t, :], bank[2 * (c % 2) + t][:, :], ACT.Copy).then_inc(sem("rg_in_tok"), 1)

            def rg_turned(c, func=ACT.Copy):
                act.wait_ge(sem("rg_in_turn"), c + 1)
                for g in range(2):
                    k = 4 * (c % 2) + 2 * g
                    dst = ru_pad[:, k:k + 2, RG_CONV - 1:RUP] if c < 2 else gT[:, k:k + 2, :]
                    act.activation(dst, bank[4 + g][:, :].rearrange("p (k s) -> p k s", k=2), func).then_inc(sem("rg_turned"), 1)

            def rg_sigmoids(g):
                n, h = RG_GROUPS[g]
                act.wait_ge(sem("rg_gates"), g + 1)
                for e in range(2):
                    k = 2 * h + e
                    dst, b = ((r_gate, "rg_b_a_2"), (i_gate, "rg_b_x_2"))[n]
                    act.activation(dst[:, k, :], bank[6 + g % 2][:, 256 * e:256 * e + 256], ACT.Sigmoid,
                                   bias=pc(b, k)).then_inc(sem("rg_sig"), 1)
                if n == 0:
                    act.wait_ge(sem("rg_conv"), RG_CONV * 4 * (h // 2 + 1))
                    for k in (2 * h, 2 * h + 1):
                        act.wait_ge(sem("rg_sig"), rg_sigs(0, k))
                        act.activation(b_seq[:, k, :], r_gate[:, k, :], ACT.Tanh, scale=sp_c[:, 7, k:k + 1]).then_inc(sem("rg_th"), 1)

            split_hi(base + 2)
            split_hi(base + 3)
            rg_rows(0)
            act.wait_ge(sem("ru_zero"), 1)
            rg_turned(0)
            split_hi(base + 4)
            split_hi(base + 5)
            rg_rows(1)
            rg_turned(1)
            split_hi(base + 6)
            act.wait_ge(sem("sp_done"), 1)
            rg_sigmoids(0)
            rg_sigmoids(1)
            split_hi(base + 7)
            for g in range(2, 6):
                rg_sigmoids(g)
            rg_rows(2)
            rg_sigmoids(6)
            rg_sigmoids(7)
            rg_turned(2)
            for k in range(KT):
                act.wait_ge(sem("rg_th"), k + 1)
                act.activation(r_gate[:, k, :], r_gate[:, k, :], ACT.Exp, scale=sp_c[:, 7, k:k + 1]).then_inc(sem("rg_a"), 1)
            split_hi(base + 8)
            for k in range(KT):
                act.wait_ge(sem("rg_m"), k + 1)
                act.activation(b_seq[:, k, :], b_seq[:, k, :], ACT.Sqrt, scale=-1.0).then_inc(sem("rg_sqrt"), 1)
            rg_rows(3)
            act.wait_ge(sem("rg_turned"), 6)
            for k in range(0, 4, 2):
                act.activation(gT[:, k:k + 2, :], gT[:, k:k + 2, :], ACT.Silu).then_inc(sem("rg_g"), 1)
            rg_turned(3, ACT.Silu)
            split_hi(base + 9)
            full_hi("rg", y_full, xT_hi)
            dense_out("rg_out", "n_kv", 16)

            full_hi("n_kv", kv_full, xT_hi)

            def copies(stage, c, dst):
                split_hi(BASE[stage] + 2 * c + 2)
                split_hi(BASE[stage] + 2 * c + 3)
                act.wait_ge(s_used, BASE[stage] + 2 * c + 2)
                for t in range(NT):
                    if c < 2:
                        if c == 1:
                            act.wait_ge(sem(f"{stage}_turn"), t + 1)
                        act.activation(a_tok[:, t, :], bank[2 * (c % 2) + t][:, :], ACT.Copy).then_inc(sem(f"{stage}_tok"), 1)
                    else:
                        func = ACT.Copy if stage == "kv" else ACT.Silu
                        act.activation(dst[:, t, 512 * (c - 2):512 * (c - 2) + 512], bank[2 * (c % 2) + t][:, :],
                                       func).then_inc(sem(f"{stage}_rows"), 1)

            for stage, dst, turned_dst in (("kv", av, akT), ("att_in", ag, aqT)):
                if stage == "att_in":
                    full_hi("n_att", kv_full, xT_hi)
                for c in range(4 if stage == "kv" else 2):
                    copies(stage, c, dst)
                    if c < 2:
                        for t in range(NT):
                            n = 2 * c + t
                            act.wait_ge(sem(f"{stage}_turn"), n + 1)
                            act.activation(turned_dst[:, 4 * c:4 * c + 4, t * P:t * P + P],
                                           bank[4 + n % 2][:, :].rearrange("p (h s) -> p h s", h=4),
                                           ACT.Copy).then_inc(sem(f"{stage}_turned"), 1)

            A_ITS = [(h, t) for h in range(A_HEADS) for t in range(NT)]
            base = BASE["att_in"]

            def a_exp(n):
                h, t = A_ITS[n]
                keys = (t + 1) * P
                act.wait_ge(sem("a_nb"), n + 1)
                if n >= 2:
                    act.wait_ge(sem("a_turn"), n - 1)
                act.activation(ap_[:, n % 2, 0:keys], bank[2 + n % 2][:, 0:keys], ACT.Exp, scale=float(P) ** -0.5,
                               bias=nb[:, n % 2, 0:1], accum_out=esum[:, n % 2, 0:1]).then_inc(sem("a_exp"), 1)

            def gate_rows(c):
                act.wait_ge(s_used, base + 2 * c + 2)
                for t in range(NT):
                    act.activation(ag[:, t, 512 * (c - 2):512 * (c - 2) + 512], bank[t][:, :], ACT.Copy).then_inc(sem("att_in_rows"), 1)

            split_hi(base + 6)
            a_exp(0)
            for n, (h, t) in enumerate(A_ITS):
                if n + 1 < len(A_ITS):
                    a_exp(n + 1)
                act.wait_ge(sem("a_turn"), n + 1)
                if n >= 2:
                    act.wait_ge(sem("a_pv"), n - 1)
                act.activation(apT[:, n % 2, 0:t + 1, :].rearrange("p k s -> p (k s)"),
                               bank[4 + n % 2][:, 0:(t + 1) * P], ACT.Copy).then_inc(sem("a_apT"), 1)
                if n == 2:
                    split_hi(base + 7)
                if n == 4:
                    gate_rows(2)
                if n == 6:
                    split_hi(base + 8)
                if n == 10:
                    split_hi(base + 9)
                if n == 13:
                    gate_rows(3)
            act.wait_ge(sem("att_in_rows"), 4)
            for c in range(2):
                for t in range(NT):
                    part = ag[:, t, 512 * c:512 * c + 512]
                    act.activation(part, part, ACT.Silu).then_inc(sem("ag_silu"), 1)
            for k in range(KT):
                act.wait_ge(*seen("tr", "ao", 4 * (k // 2) + 4))
                act.activation(xT_hi[:, k, :], bank[4 + k // 2][:, 256 * (k % 2):256 * (k % 2) + 256], ACT.Copy).then_inc(sem("hi"), 1)
                act.wait_ge(*seen("lo", "ao", k + 1))
            dense_out("att_out", "n_last", 20)

        @block.vector
        def _(dve):
            count = [0]

            def link(ins):
                count[0] += 1
                ins.then_inc(sem("dve_chain"), 1)
                dve.wait_ge(sem("dve_chain"), count[0])

            def split_lo(u, i=None):
                if u >= UNITS:
                    return
                n = u + ADA0
                dve.wait_ge(s_hi, at(u + 1, i, 6))
                dve.tensor_tensor(w_lo[u % N_SPLIT][:, :], w_land[n % N_LAND][:, :],
                                  w_hi[u % N_SPLIT][:, :].bitcast(F32), ALU.subtract).then_inc(s_lo, 1)

            def job_units(q, units, i=None):
                c = 0 if JOBS[q] < V_MOD0 else 2
                for j in units:
                    dve.wait_ge(a_landed[j % 2], at(16 * (2 * q + j // 2 + 1), i, 32))
                    for e in range(2):
                        n = 2 * j + e
                        w = a_land[j % 2][:, e * D:e * D + D]
                        if n == 0:
                            if q >= 1:
                                dve.wait_ge(s_red, at(q, i, 1))
                            ins = dve.tensor_scalar(job_sum[:, :], w, silu_c[:, c, n:n + 1], None, ALU.mult)
                        else:
                            dve.wait_ge(s_step, at(8 * q + n, i, 8))
                            ins = dve.scalar_tensor_tensor(out=job_sum[:, :], in0=w, scalar=silu_c[:, c, n:n + 1],
                                                           in1=job_sum[:, :], op0=ALU.mult, op1=ALU.add)
                        ins.then_inc(s_step, 1)

            def job_cols(q, i=None):
                v = JOBS[q]
                dve.wait_ge(s_red, at(q + 1, i, 1))
                if i is None:
                    dst, bias = mcol[:, v * KT:v * KT + KT], pcol[:, v * KT + (32 if v >= V_MOD0 else 0):][:, 0:KT]
                else:
                    dst = mcol[:, bass.ds(i * KT + v * KT, KT)]
                    bias = pcol[:, bass.ds(i * KT + (v * KT + (32 if v >= V_MOD0 else 0)), KT)]
                dve.tensor_tensor(dst, COLS[:, 0:KT], bias, ALU.add).then_inc(s_cols, 1)

            def norm_stats(stage, src, dst, n=NT, width=D, scale=None):
                halves = NORMED["ss"] if dict(STEPS)[stage]["ss"] == 2 * NT else 0
                dve.wait_ge(*seen("ss", stage, halves or n))
                if halves:
                    link(dve.tensor_tensor(ms[:, 0:n], ss[:, 0:halves].rearrange("p (t c) -> p t c", c=2)[:, :, 0],
                                           ss[:, 0:halves].rearrange("p (t c) -> p t c", c=2)[:, :, 1], ALU.add))
                dve.tensor_scalar(ms[:, 0:n], ms[:, 0:n] if halves else ss[:, 0:n], 1.0 / width, EPS, ALU.mult, ALU.add).then_inc(sem("ms"), 1)
                dve.wait_ge(*seen("rstd", stage, 1))
                if dst is not None:
                    for t in range(NT):
                        dve.tensor_scalar(dst[:, t, :], src[:, t, :], rstd[:, t:t + 1], None, ALU.mult).then_inc(sem("xn"), 1)

            def mod_cols(g, v_shift, v_scale, scale_cols=None):
                sc = mc(v_scale) if scale_cols is None else scale_cols
                link(dve.scalar_tensor_tensor(out=a_col[:, :], in0=sc, scalar=1.0, in1=g, op0=ALU.add, op1=ALU.mult))

            def full_lo(stage, full, hi, lo, banks, a, b, ks=range(KT), turns=2 * KT, whole=False):
                if whole:
                    dve.wait_ge(*seen("tr", stage, turns))

                def low(n):
                    dve.wait_ge(*seen("hi", stage, n + 1))
                    dve.tensor_tensor(lo[:, ks[n], :], full[:, ks[n], :], hi[:, ks[n], :].bitcast(F32),
                                      ALU.subtract).then_inc(sem("lo"), 1)

                for n, k in enumerate(ks):
                    if not whole and k % 2 == 0:
                        dve.wait_ge(*seen("tr", stage, 2 * k + 4))
                    src = banks[k // 2][:, 256 * (k % 2):256 * (k % 2) + 256]
                    if b is None:
                        ins = dve.tensor_scalar(full[:, k, :], src, a(k), None, ALU.mult)
                    else:
                        ins = dve.tensor_scalar(full[:, k, :], src, a(k), b(k), ALU.mult, ALU.add)
                    ins.then_inc(sem("full"), 1)
                    if n >= 1:
                        low(n - 1)
                low(len(ks) - 1)

            def gate_diag(stage, col, dst=None):
                g = (gate if dst is None else dst)[:, :].rearrange("p (k f) -> p k f", k=KT)
                dve.tensor_tensor(g, ident[:, :].unsqueeze(1).broadcast_to([P, KT, P]),
                                  col.unsqueeze(2).broadcast_to([P, KT, P]), ALU.mult).then_inc(sem("diag"), 1)

            def residual(stage, c, banks, waits):
                cols = slice(512 * c, 512 * c + 512)
                for t in range(NT):
                    dve.wait_ge(*waits[t])
                    link(dve.tensor_tensor(tmp[:, t, :], banks[t][:, :], gate[:, cols], ALU.mult))
                    dve.tensor_tensor(x[:, t, cols], x[:, t, cols], tmp[:, t, :], ALU.add).then_inc(sem("xres"), 1)

            for g in range(5):
                dve.wait_ge(sem("prow_tr"), g + 1)
                n = sum(k for _, k in ROW_GROUPS[g])
                dve.tensor_copy(pcol[:, g * P:g * P + n], bank[4 + g % 4][:, 0:n]).then_inc(sem("cols_in"), 1)
                if g == 0:
                    norm_stats("n_x", x, xn)
            split_lo(0)
            split_lo(1)
            dve.wait_ge(sem("lam_in"), 64)
            dve.wait_ge(sem("cols_in"), 5)
            for n in range(2):
                dve.tensor_tensor_reduce(lam_junk[:, n, :], lam_in[:, 2 * n, :], lam_in[:, 2 * n + 1, :], 1.0, 0.0,
                                         ALU.mult, ALU.add, lam_tmp[:, n:n + 1]).then_inc(sem("lam_dot"), 1)
            lam = pc("rg_lambda_2", 0, KT)
            link(dve.tensor_scalar(sp_c[:, 2, :], lam, -1.0, 0.0, ALU.mult, ALU.max))
            dve.scalar_tensor_tensor(out=sp_c[:, 0, :], in0=sp_c[:, 2, :], scalar=2.0, in1=lam,
                                     op0=ALU.mult, op1=ALU.add).then_inc(sem("sp_abs"), 1)
            dve.wait_ge(sem("lam_exp"), 1)
            link(dve.tensor_tensor(lam_tmp[:, 4:5], lam_tmp[:, 3:4], lam_tmp[:, 2:3], ALU.subtract))
            link(dve.tensor_scalar(lam_tmp[:, 5:6], lam_tmp[:, 4:5], -(1.0 - SUB_SCALE), None, ALU.add))

            dve.wait_ge(sem("ada0_tr"), 16)
            turned = bank[0][:, 0:32].rearrange("p (v c) -> p v c", c=2)
            dve.tensor_tensor(mcol[:, 0:2 * KT], turned[:, :, 0], pcol[:, 0:2 * KT], ALU.add).then_inc(sem("ada0_cols"), 1)
            dve.tensor_tensor(mcol_ctx[:, :], turned[:, :, 1], pcol[:, 0:2 * KT], ALU.add).then_inc(sem("ada0_cols"), 1)
            dve.wait_ge(sem("ada0_cols"), 2)
            mod_cols(pc("mix_norm_g", 0, KT), 0, 1)
            link(dve.scalar_tensor_tensor(out=b_col[:, :], in0=mcol_ctx[:, KT:2 * KT], scalar=1.0,
                                          in1=pc("mix_norm_g", 0, KT), op0=ALU.add, op1=ALU.mult))
            full_lo("n_x", xfull, xT_hi, xT_lo, bank[4:8], lambda k: a_col[:, k:k + 1], lambda k: mc(0, k, 1))

            def softplus_lambda():
                dve.wait_ge(sem("sp_exp"), 1)
                link(dve.tensor_scalar(sp_c[:, 3, :], sp_c[:, 1, :], 2.0, None, ALU.add))
                link(dve.reciprocal(sp_c[:, 4, :], sp_c[:, 3, :]))
                link(dve.tensor_tensor(sp_c[:, 3, :], sp_c[:, 1, :], sp_c[:, 4, :], ALU.mult))
                link(dve.tensor_tensor(sp_c[:, 4, :], sp_c[:, 3, :], sp_c[:, 3, :], ALU.mult))
                link(dve.tensor_scalar(sp_c[:, 5, :], sp_c[:, 4, :], 1.0 / 17, 1.0 / 15, ALU.mult, ALU.add))
                for n in range(13, 0, -2):
                    link(dve.tensor_tensor(sp_c[:, 5, :], sp_c[:, 5, :], sp_c[:, 4, :], ALU.mult))
                    link(dve.tensor_scalar(sp_c[:, 5, :], sp_c[:, 5, :], 1.0 / n, None, ALU.add))
                link(dve.tensor_tensor(sp_c[:, 5, :], sp_c[:, 5, :], sp_c[:, 3, :], ALU.mult))
                link(dve.scalar_tensor_tensor(out=sp_c[:, 5, :], in0=sp_c[:, 5, :], scalar=2.0, in1=sp_c[:, 2, :],
                                              op0=ALU.mult, op1=ALU.add))
                dve.tensor_scalar(sp_c[:, 7, :], sp_c[:, 5, :], -RG_C, None, ALU.mult).then_inc(sem("sp_done"), 1)

            ITS = [(h, t) for h in range(HEADS) for t in range(NT)]

            def row_max(n):
                b = n % 2
                if n >= 2:
                    dve.wait_ge(sem("d_exp"), 2 * (n - 1))
                for c in range(2):
                    dve.wait_ge(sem("d_s"), 2 * n + c + 1)
                    dve.reduce_max(mx[:, b, c:c + 1], bank[2 * b + c][:, :], AX_X).then_inc(sem("d_mx"), 1)
                dve.wait_ge(sem("d_mx"), 2 * n + 2)
                dve.tensor_scalar(nb[:, b, :], mx[:, b, :], -0.125, None, ALU.mult).then_inc(sem("d_nb"), 1)

            dve.wait_ge(sem("rope_in"), 16)

            def rotate(src, t, n):
                m = n // 64
                v = src[:, 0:n].rearrange("p (m h d) -> p m h d", m=m, h=2)
                c4 = rope_cos[:, 0:n].rearrange("p (m h d) -> p m h d", m=m, h=2)
                s4 = rope_sin[:, 0:n].rearrange("p (m h d) -> p m h d", m=m, h=2)
                v2 = src[:, 0:n].rearrange("p (m d) -> p m d", d=32)
                o4 = rot[:, t, 0:n].rearrange("p (m h d) -> p m h d", m=m, h=2)
                for dst, which in ((rope_cos, 0), (rope_sin, 1)):
                    ins = dve.tensor_tensor(dst[:, 0:n].rearrange("p (m d) -> p m d", d=32), v2,
                                            rope[:, t, which, :].unsqueeze(1).broadcast_to([P, 2 * m, 32]), ALU.mult)
                    link(ins)
                dve.tensor_tensor(o4[:, :, 0, :], c4[:, :, 0, :], s4[:, :, 1, :], ALU.subtract).then_inc(sem("rot"), 1)
                dve.tensor_tensor(o4[:, :, 1, :], s4[:, :, 0, :], c4[:, :, 1, :], ALU.add).then_inc(sem("rot"), 1)

            plan = [((s_used, 2), 0, 512, 0), ((s_used, 4), 2, 256, 2), ((sem("in_lat"), 1), 0, 512, 4),
                    ((sem("in_lat"), 2), 0, 256, 8)]
            def take(c):
                event, b, n, free = plan[c]
                dve.wait_ge(*event)
                if free:
                    dve.wait_ge(sem("turn"), free)
                for t in range(NT):
                    if c or t:
                        dve.wait_ge(sem("rot"), 4 * c + 2 * t)
                    rotate(bank[b + t], t, n)
                    if c == 1:
                        dve.tensor_copy(f_tok[:, t, :], bank[b + t][:, 256:512]).then_inc(sem("f_tok"), 1)
                    if c == 3:
                        dve.tensor_copy(v_tok[:, NT + t, 0:256], bank[b + t][:, 256:512]).then_inc(sem("v_lat"), 1)

            split_lo(2)
            norm_stats("n_ctx", ctx_x, ctx_x)
            split_lo(3)
            take(0)
            split_lo(4)
            full_lo("n_ctx", ctx_full, ctxT_hi, ctxT_lo, bank[4:8], lambda k: b_col[:, k:k + 1],
                    lambda k: mcol_ctx[:, k:k + 1], whole=True)
            split_lo(5)
            take(1)
            job_units(0, range(1))
            split_lo(6)
            take(2)
            job_units(0, (1,))
            split_lo(7)
            job_units(0, (2,))
            split_lo(8)
            job_units(0, (3,))
            take(3)
            job_cols(0)
            job_units(1, (0,))
            softplus_lambda()
            split_lo(9)
            job_units(1, (1,))
            split_lo(10)
            job_units(1, (2, 3))
            job_cols(1)
            job_units(2, (0,))
            split_lo(11)
            job_units(2, range(1, 4))
            row_max(0)
            for f in range(2):
                dve.wait_ge(sem("four_hi"), 2)
                dve.tensor_tensor(xT_lo[:, HEADS + f, :], bank[6][:, 256 * f:256 * f + 256],
                                  xT_hi[:, HEADS + f, :].bitcast(F32), ALU.subtract).then_inc(sem("four_lo"), 1)

            job_cols(2)

            def head_square(n):
                h, t = ITS[n]
                dve.wait_ge(sem("d_o"), n + 1)
                o = o_tok[:, t, h * P:h * P + P]
                if n >= 2:
                    dve.wait_ge(*seen("ss", "sub", n - 1))
                dve.tensor_tensor_reduce(sq_junk[:, n % 2, :], o, o, 1.0, 0.0, ALU.mult, ALU.add,
                                         ss[:, t * HEADS + h:t * HEADS + h + 1]).then_inc(sem("ss"), 1)

            for n, (h, t) in enumerate(ITS):
                b = n % 2
                if n + 1 < len(ITS):
                    row_max(n + 1)
                dve.wait_ge(sem("d_exp"), 2 * n + 2)
                if n >= 2:
                    dve.wait_ge(sem("d_o"), n - 1)
                link(dve.reciprocal(rsum[:, b, :], esum[:, b, :]))
                link(dve.tensor_scalar(rsum[:, b, 1:2], rsum[:, b, 1:2], esum[:, b, 0:1], lam_tmp[:, 5:6], ALU.mult, ALU.mult))
                if n >= 2:
                    dve.wait_ge(sem("d_turn"), n - 1)
                dve.scalar_tensor_tensor(out=diff[:, b, :], in0=prob[:, b, 1, :], scalar=rsum[:, b, 1:2],
                                         in1=prob[:, b, 0, :], op0=ALU.mult, op1=ALU.add).then_inc(sem("d_diff"), 1)
                if n >= 2:
                    head_square(n - 2)
            for n in (len(ITS) - 2, len(ITS) - 1):
                head_square(n)
            norm_stats("sub", None, None, 12, P)
            for t in range(NT):
                o = o_tok[:, t, :].rearrange("p (h e) -> p h e", h=HEADS)
                dve.tensor_tensor(o, o, rstd[:, t * HEADS:t * HEADS + HEADS].unsqueeze(2).broadcast_to([P, HEADS, P]),
                                  ALU.mult).then_inc(sem("xn"), 1)
            link(dve.tensor_scalar(a_col[:, 0:1], pc("ev_subln_g"), SUB_SCALE, None, ALU.mult))
            full_lo("sub", o_full, xT_hi, xT_lo, bank[2:5], lambda k: a_col[:, 0:1], None, range(HEADS), 12)
            gate_diag("out", mc(2))

            def dense_residual(stage, bias=None):
                for c in range(2):
                    split_lo(BASE[stage] + 2 * c + 2)
                    split_lo(BASE[stage] + 2 * c + 3)
                    if stage == "out":
                        job_units(3, [(0, 1), (2,)][c])
                    if c == 0:
                        dve.wait_ge(*seen("gate", stage if bias is None else "pw2b", 2))
                    if c == 0 and bias is not None:
                        for n in range(2 * NT):
                            part = x[:, n // 2, 512 * (n % 2):512 * (n % 2) + 512]
                            dve.tensor_tensor(part, part, bias[:, 512 * (n % 2):512 * (n % 2) + 512],
                                              ALU.add).then_inc(sem("x_bias"), 1)
                        dve.wait_ge(sem("x_bias"), 2 * NT)
                    residual(stage, c, bank[2 * c:2 * c + 2],
                             (seen("part", stage, c + 1), (s_used, BASE[stage] + 2 * c + 2)))

            dense_residual("out")

            def ffn(layer, loops, first_job):
                base = BASE[f"ffn{layer}"]
                off = layer * FCH
                norm_stats(f"n_ffn{layer}", x, xn)
                mod_cols(pc("ffn_norm_g", layer * KT, KT), 0, 6 * layer + 4)
                full_lo(f"n_ffn{layer}", xfull, xT_hi, xT_lo, bank[2:6], lambda k: a_col[:, k:k + 1],
                        lambda k: mc(6 * layer + 3, k, 1))

                def hidden(c, i=None):
                    for t in range(NT):
                        dve.wait_ge(sem("silu_g"), at(2 * (off + c) + t + 1, i, 4))
                        dve.tensor_tensor(hid[:, t, :], silu_g[:, t, :], bank[t][:, 256:512], ALU.mult).then_inc(sem("hid"), 1)

                def hidden_lo(c, i=None):
                    dve.wait_ge(sem("hT_hi"), at(off + c + 1, i, 2))
                    dve.tensor_tensor(hT_lo[:, :, :].rearrange("p k s -> p (k s)"), bank[6][:, :],
                                      hT_hi[:, :, :].rearrange("p k s -> p (k s)").bitcast(F32),
                                      ALU.subtract).then_inc(sem("hT_lo"), 1)

                split_lo(base + 2)
                if layer == 0:
                    job_units(3, (3,))
                hidden(0)
                if layer == 0:
                    job_cols(3)
                    dve.wait_ge(s_cols, 4)
                gate_diag(f"ffn{layer}", mc(6 * layer + 5))
                if layer == 1:
                    gate_diag("final", pc("final_g", 0, KT), bias_gate)
                split_lo(base + 3)
                hidden_lo(0)
                job_units(first_job, range(2))
                done = 0
                for q, n in loops:
                    with dve.Fori(0, n) as i:
                        for b in range(2):
                            u = base + 2 + 6 * done + 3 * b
                            c = 1 + 2 * done + b
                            split_lo(u + 2, i)
                            split_lo(u + 3, i)
                            hidden(c, i)
                            if b == 0:
                                job_units(q, (2,), i)
                                split_lo(u + 4, i)
                                hidden_lo(c, i)
                                job_units(q, (3,), i)
                            else:
                                split_lo(u + 4, i)
                                job_units(q + 1, (0,), i)
                                hidden_lo(c, i)
                                job_cols(q, i)
                                job_units(q + 1, (1,), i)
                    done += n
                split_lo(base + 3 * FCH + 1)
                job_units(first_job + 5, range(2, 4))
                dve.wait_ge(*seen("gate", f"ffn{layer}", 2))
                for c in range(2):
                    name = f"ffn{layer}"
                    last = (s_used, base + 3 * FCH) if c == 1 else seen("part", name, 2)
                    residual(name, c, bank[2 + 2 * c:4 + 2 * c], (seen("part", name, 2 * c + 1), last))

            ffn(0, [(4, 5)], 4)
            job_cols(9)

            norm_stats("n_pw1", x, xn)
            mod_cols(pc("mix_norm_g", KT, KT), 0, 7)
            full_lo("n_pw1", xfull, xT_hi, xT_lo, bank[2:6], lambda k: a_col[:, k:k + 1], lambda k: mc(6, k, 1))
            dve.wait_ge(sem("u_zero"), 2)
            steps = [0]
            last_step = {}

            def conv_step(k, ins):
                ins.then_inc(sem("conv"), 1)
                steps[0] += 1
                last_step[k] = steps[0]

            def conv_taps(c):
                dve.wait_ge(sem("pw1_glu"), 2 * c + 2)
                for tap in range(CONV - PE_TAPS):
                    for k in (2 * c, 2 * c + 1):
                        src = u_pad[:, k, tap:tap + S]
                        w = pcol[:, COL["od_dw_w_a"] + tap * KT + k:][:, 0:1]
                        if tap == 0:
                            conv_step(k, dve.tensor_scalar(conv[:, k, :], src, w, pc("od_dw_b", k), ALU.mult, ALU.add))
                        else:
                            dve.wait_ge(sem("conv"), last_step[k])
                            conv_step(k, dve.scalar_tensor_tensor(out=conv[:, k, :], in0=src, scalar=w,
                                                                  in1=conv[:, k, :], op0=ALU.mult, op1=ALU.add))
                    if tap == (None, 12, 12, 0)[c]:
                        conv_whole(c - 1)

            def conv_whole(c):
                dve.wait_ge(sem("conv_pe"), c + 1)
                for k in (2 * c, 2 * c + 1):
                    dve.wait_ge(sem("conv"), last_step[k])
                    dve.tensor_tensor(conv[:, k, :], conv[:, k, :], bank[6][:, 256 * (k % 2):256 * (k % 2) + 256],
                                      ALU.add).then_inc(sem("conv_whole"), 1)

            for c in range(4):
                split_lo(BASE["pw1"] + 2 * c + 2)
                split_lo(BASE["pw1"] + 2 * c + 3)
                for e in range(2):
                    k = 2 * c + e
                    dve.wait_ge(sem("pw1_sig"), k + 1)
                    dve.scalar_tensor_tensor(out=u_pad[:, k, PAD:PAD + S], in0=bank[4][:, 256 * e:256 * e + 256],
                                             scalar=pc("od_pw1_b", k), in1=sig[:, e, :], op0=ALU.add,
                                             op1=ALU.mult).then_inc(sem("pw1_glu"), 1)
                conv_taps(c)
            conv_whole(3)
            dve.wait_ge(sem("ln_mean_mm"), 1)
            link(dve.tensor_scalar(mean[:, :], bank[4][:, 0:S], 1.0 / D, None, ALU.mult))
            for k in range(KT):
                dve.wait_ge(sem("conv_whole"), k + 1)
                dve.tensor_tensor(conv[:, k, :], conv[:, k, :], mean[:, :], ALU.subtract).then_inc(sem("ln_xc"), 1)
            dve.wait_ge(sem("ln_var_mm"), 1)
            dve.tensor_copy(rln[:, :], bank[5][:, 0:S]).then_inc(sem("ln_var"), 1)
            dve.wait_ge(sem("ln_var_tr"), 1)
            dve.tensor_scalar(ms[:, 0:NT], bank[4][:, 0:S].rearrange("p (t s) -> p t s", t=NT)[:, :, 0], 1.0 / D, EPS,
                              ALU.mult, ALU.add).then_inc(sem("ms"), 1)
            dve.wait_ge(*seen("rstd", "ln", 1))
            for t in range(NT):
                dve.tensor_scalar(rln[:, t * P:t * P + P], ident[:, :], rstd[:, t:t + 1], None, ALU.mult).then_inc(sem("ln_diag"), 1)
            dve.wait_ge(sem("ln_row_mm"), 1)
            for k in range(KT):
                dve.wait_ge(sem("ln_xc"), k + 1)
                dve.tensor_tensor(csq[:, k, :], conv[:, k, :], bank[5][:, 0:S], ALU.mult).then_inc(sem("ln_norm"), 1)
            for k in range(KT):
                dve.wait_ge(*seen("hi", "ln", k + 1))
                dve.tensor_tensor(xT_lo[:, k, :], xfull[:, k, :], xT_hi[:, k, :].bitcast(F32),
                                  ALU.subtract).then_inc(sem("lo"), 1)
            gate_diag("pw2", mc(8))
            link(dve.tensor_tensor(b_col[:, :], mc(8), pc("od_pw2_b", 0, KT), ALU.mult))
            bg = bias_gate[:, :].rearrange("p (k f) -> p k f", k=KT)
            dve.tensor_tensor(bg, ident[:, :].unsqueeze(1).broadcast_to([P, KT, P]),
                              b_col[:, :].unsqueeze(2).broadcast_to([P, KT, P]), ALU.mult).then_inc(sem("diag"), 1)
            dense_residual("pw2", bias_gate)
            ffn(1, [(10, 5)], 10)
            job_cols(15)

            norm_stats("n_final", x, xn)
            dve.wait_ge(*seen("gate", "final", 2))
            dve.wait_ge(*seen("xn", "n_final", 2))
            for t in range(NT):
                dve.tensor_tensor(x[:, t, :], xn[:, t, :], bias_gate[:, :], ALU.mult).then_inc(sem("x_final"), 1)

            norm_stats("n_rg", x, xn)
            mod_cols(pc("norm_g_2", 0, KT), 0, V_MOD0 + 1)
            full_lo("n_rg", xfull, xT_hi, xT_lo, bank[2:6], lambda k: a_col[:, k:k + 1], lambda k: mc(V_MOD0, k, 1))
            dve.wait_ge(sem("ru_zero"), 1)
            base = BASE["rg_in"]

            def rg_scan(k):
                dve.wait_ge(sem("rg_b"), k + 1)
                dve.tensor_tensor_scan(uc[:, k, :], r_gate[:, k, :], i_gate[:, k, :], 0.0, ALU.mult,
                                       ALU.add).then_inc(sem("rg_h"), 1)

            for c in range(2):
                split_lo(base + 2 * c + 2)
                split_lo(base + 2 * c + 3)
                dve.wait_ge(sem("rg_turned"), 2 * c + 2)
                for tap in range(RG_CONV):
                    w = COL["rg_conv_w_2"] + tap * KT
                    for e in range(4):
                        k = 4 * c + e
                        src = ru_pad[:, k, tap:tap + S]
                        if tap == 0:
                            ins = dve.tensor_scalar(uc[:, k, :], src, pcol[:, w + k:w + k + 1], pc("rg_conv_b_2", k),
                                                    ALU.mult, ALU.add)
                        else:
                            dve.wait_ge(sem("rg_conv"), 4 * (RG_CONV * c + tap - 1) + e + 1)
                            ins = dve.scalar_tensor_tensor(out=uc[:, k, :], in0=src, scalar=pcol[:, w + k:w + k + 1],
                                                           in1=uc[:, k, :], op0=ALU.mult, op1=ALU.add)
                        ins.then_inc(sem("rg_conv"), 1)
            split_lo(base + 6)
            split_lo(base + 7)
            for k in range(KT):
                if k % 2 == 0:
                    dve.wait_ge(sem("rg_a2"), k // 2 + 1)
                else:
                    dve.wait_ge(sem("rg_a"), k + 1)
                    link(dve.tensor_tensor(y_full[:, k, :], r_gate[:, k, :], r_gate[:, k, :], ALU.mult))
                dve.scalar_tensor_tensor(out=b_seq[:, k, :], in0=y_full[:, k, :], scalar=1.0, in1=b_seq[:, k, :],
                                         op0=ALU.add, op1=ALU.mult).then_inc(sem("rg_m"), 1)
            dve.wait_ge(sem("rg_iu"), KT)
            for k in range(KT):
                dve.wait_ge(sem("rg_sqrt"), k + 1)
                dve.tensor_tensor(i_gate[:, k, :], i_gate[:, k, :], b_seq[:, k, :], ALU.mult).then_inc(sem("rg_b"), 1)
                if k >= 1:
                    rg_scan(k - 1)
            rg_scan(KT - 1)
            split_lo(base + 8)

            def rg_low(k):
                dve.wait_ge(*seen("hi", "rg", k + 1))
                dve.tensor_tensor(xT_lo[:, k, :], y_full[:, k, :], xT_hi[:, k, :].bitcast(F32),
                                  ALU.subtract).then_inc(sem("lo"), 1)

            for k in range(KT):
                dve.wait_ge(sem("rg_h"), k + 1)
                dve.wait_ge(*((sem("rg_g"), k // 2 + 1) if k < 4 else (sem("rg_turned"), 7 + (k - 4) // 2)))
                dve.tensor_tensor(y_full[:, k, :], uc[:, k, :], gT[:, k, :], ALU.mult).then_inc(sem("full"), 1)
                if k >= 1:
                    rg_low(k - 1)
            rg_low(KT - 1)
            split_lo(base + 9)
            gate_diag("rg_out", mc(V_MOD0 + 2))
            dense_residual("rg_out")

            norm_stats("n_kv", x, xn)
            mod_cols(pc("kv_norm_g_2", 0, KT), 0, V_KV + 1)
            full_lo("n_kv", kv_full, xT_hi, xT_lo, bank[2:6], lambda k: a_col[:, k:k + 1], lambda k: mc(V_KV, k, 1))
            for stage in ("kv", "att_in"):
                if stage == "att_in":
                    job_cols(16)
                    dve.wait_ge(s_cols, 17)
                    mod_cols(pc("norm_g_2", KT, KT), 0, V_MOD1 + 1)
                    dve.wait_ge(s_used, BASE["att_in"])
                    full_lo("n_att", kv_full, xT_hi, xT_lo, bank[2:6], lambda k: a_col[:, k:k + 1],
                            lambda k: mc(V_MOD1, k, 1))
                for c in range(4 if stage == "kv" else 2):
                    split_lo(BASE[stage] + 2 * c + 2)
                    if stage == "kv" and c == 3:
                        job_units(17, (2,))
                    split_lo(BASE[stage] + 2 * c + 3)
                    if stage == "kv" and c < 3:
                        job_units(16 + c // 2, [(0, 1), (2, 3)][c % 2])
                    elif stage == "att_in" and c == 0:
                        job_units(17, (3,))
                    elif stage == "att_in":
                        job_cols(17)

            A_ITS = [(h, t) for h in range(A_HEADS) for t in range(NT)]

            def a_max(n):
                h, t = A_ITS[n]
                b = n % 2
                keys = (t + 1) * P
                dve.wait_ge(sem("a_s"), n + 1)
                link(dve.reduce_max(mx[:, b, 0:1], bank[2 + b][:, 0:keys], AX_X))
                dve.tensor_scalar(nb[:, b, 0:1], mx[:, b, 0:1], -float(P) ** -0.5, None, ALU.mult).then_inc(sem("a_nb"), 1)

            def a_out(n):
                h, t = A_ITS[n]
                b = n % 2
                dve.wait_ge(sem("a_pv"), n + 1)
                dve.tensor_scalar(ao[:, t, h * P:h * P + P], bank[6 + b][:, 0:P], rsum[:, b, 0:1], None,
                                  ALU.mult).then_inc(sem("a_o"), 1)

            split_lo(BASE["att_in"] + 6)
            a_max(0)
            for n in range(len(A_ITS)):
                if n + 1 < len(A_ITS):
                    a_max(n + 1)
                dve.wait_ge(sem("a_exp"), n + 1)
                if n >= 2:
                    dve.wait_ge(sem("a_o"), n - 1)
                link(dve.reciprocal(rsum[:, n % 2, 0:1], esum[:, n % 2, 0:1]))
                if n >= 1:
                    a_out(n - 1)
                if n in (2, 6, 10):
                    split_lo(BASE["att_in"] + {2: 7, 6: 8, 10: 9}[n])
            a_out(len(A_ITS) - 1)
            dve.wait_ge(sem("a_o"), len(A_ITS))
            for c in range(2):
                for t in range(NT):
                    cols = slice(512 * c, 512 * c + 512)
                    dve.wait_ge(sem("ag_silu"), 2 * c + t + 1)
                    dve.tensor_tensor(ao[:, t, cols], ao[:, t, cols], ag[:, t, cols], ALU.mult).then_inc(sem("ao_gated"), 1)
            for k in range(KT):
                dve.wait_ge(*seen("hi", "ao", k + 1))
                dve.tensor_tensor(xT_lo[:, k, :], bank[4 + k // 2][:, 256 * (k % 2):256 * (k % 2) + 256],
                                  xT_hi[:, k, :].bitcast(F32), ALU.subtract).then_inc(sem("lo"), 1)
            gate_diag("att_out", mc(V_MOD1 + 2))
            gate_diag("last", pc("final_norm_g_2", 0, KT), last_gate)
            dense_residual("att_out")
            norm_stats("n_last", x, xn)
            dve.wait_ge(*seen("gate", "last", 2))
            dve.wait_ge(*seen("xn", "n_last", 2))
            for t in range(NT):
                dve.tensor_tensor(xn[:, t, :], xn[:, t, :], last_gate[:, :], ALU.mult).then_inc(sem("result"), 1)

        @block.tensor
        def _(pe):
            def three(dst, hi, lo, whi, wlo, start, stop):
                pe.matmul(dst, hi, whi, start=start, stop=False)
                pe.matmul(dst, hi, wlo, start=False, stop=False)
                return pe.matmul(dst, lo, whi, start=False, stop=stop)

            def unit_wait(u, i=None):
                pe.wait_ge(s_lo, at(u + 1, i, 6))

            def half(u, j, hi, lo, banks, last=None, ready=None, ts=range(NT), ks=range(4), part=False):
                wh = w_hi[u % N_SPLIT][:, :].rearrange("p (k n) -> p k n", k=4)
                wl = w_lo[u % N_SPLIT][:, :].rearrange("p (k n) -> p k n", k=4)
                for t in ts:
                    for k in ks:
                        if ready is not None and t == 0:
                            n = min(4 * j + k + 1, dict(STEPS)[ready]["lo"])
                            pe.wait_ge(*seen("lo", ready, n))
                        kt = 4 * j + k
                        ins = three(banks[t][:, :], hi[:, kt, t * P:t * P + P], lo[:, kt, t * P:t * P + P],
                                    wh[:, k, :], wl[:, k, :], kt == 0, kt == KT - 1)
                    if part and j == 1 and t == 0:
                        ins.then_inc(sem("part"), 1)
                if last is not None:
                    ins.then_inc(last, 1)
                return ins

            def turn_norm(stage, src, banks, wait=None):
                pe.wait_ge(*seen("xn", stage, NT))
                for k in range(KT):
                    for t in range(NT):
                        pe.transpose(banks[k // 2][:, 256 * (k % 2) + t * P:256 * (k % 2) + t * P + P],
                                     src[:, t, k * P:k * P + P], ident[:, :]).then_inc(sem("tr"), 1)

            def gate_mm(stage, src=None, b=4):
                src = gate if src is None else src
                pe.wait_ge(*seen("diag", stage, 1))
                for h in range(2):
                    ins = pe.matmul(bank[b + h][:, :], ones[:, :], src[:, 512 * h:512 * h + 512], start=True, stop=True)
                ins.then_inc(sem("gmm"), 1)

            def gate_after(stage):
                def after(c):
                    if c == 0:
                        gate_mm(stage)
                        if stage == "pw2":
                            gate_mm("pw2b", bias_gate, 6)
                        if stage == "att_out":
                            gate_mm("last", last_gate, 6)
                return after

            def job_reduce(q, i=None):
                pe.wait_ge(s_step, at(8 * q + 8, i, 8))
                if q >= 1:
                    pe.wait_ge(s_cols, at(q, i, 1))
                for k in range(KT):
                    ins = pe.matmul(COLS[:, k:k + 1], job_sum[:, k * P:k * P + P], ones[:, 0:1], start=True, stop=True)
                ins.then_inc(s_red, 1)

            pe.wait_ge(sem("ident_in"), 16)
            pe.wait_ge(sem("ones"), 2)

            def turn_rows(g):
                pe.wait_ge(sem(f"prow{g}"), 16 * len(ROW_GROUPS[g]))
                n = sum(k for _, k in ROW_GROUPS[g])
                if g == 4:
                    pe.wait_ge(sem("cols_in"), 1)
                pe.transpose(bank[4 + g % 4][:, 0:n], prow[0:n, g, :], ident[0:n, 0:n]).then_inc(sem("prow_tr"), 1)

            turn_rows(0)
            pe.wait_ge(sem("silu_c"), 1)
            for n in range(ADA0):
                pe.wait_ge(landed[n % N_LAND], 32 * (n // N_LAND + 1))
                w = w_land[n % N_LAND][:, :].rearrange("p (k n) -> p k n", k=2)
                for e in range(2):
                    kt = 2 * (n % 4) + e
                    for h in range(2):
                        ins = pe.matmul(bank[2 * (n // 4) + h][0:2, :], silu_c[:, 0:2, kt],
                                        w[:, e, 512 * h:512 * h + 512], start=kt == 0, stop=kt == KT - 1)
                ins.then_inc(sem("ada0_used"), 1)
                if n == 5:
                    for g in range(1, 5):
                        turn_rows(g)
                if n == 6:
                    pe.wait_ge(sem("cols_in"), 5)
                    turn_norm("n_x", xn, bank[4:8])
            pe.wait_ge(sem("ada0_rows"), 4)
            for n in range(2 * KT):
                pe.transpose(bank[0][:, 2 * n:2 * n + 2], ada_rows[0:2, n * P:n * P + P], ident[0:2, 0:2]).then_inc(sem("ada0_tr"), 1)

            def turn_heads(c):
                nh = 4 if c % 2 == 0 else 2
                rot_need = {0: 4, 1: 8, 2: 12, 3: 16}[c]
                for src in range(1 if c < 2 else 2):
                    for t in range(NT):
                        n = turned[0]
                        turned[0] += 1
                        if src == 0:
                            pe.wait_ge(sem("rot"), rot_need - 2 * (1 - t))
                        else:
                            pe.wait_ge(sem("in_act"), {2: t + 1, 3: 2 + 2 * t + 1}[c])
                        if n >= 2:
                            pe.wait_ge(sem("turn_out"), n - 1)
                        buf = rot if src == 0 else k_ctx
                        for h in range(nh):
                            ins = pe.transpose(bank[(4, 6)[n % 2]][:, h * P:h * P + P], buf[:, t, h * P:h * P + P], ident[:, :])
                        ins.then_inc(sem("turn"), 1)

            turned = [0]
            bank_read = [[("ada0_cols", 2)], [], [("rot", 4)], [("rot", 8), ("f_tok", 2)], [("rot", 12)],
                         [("in_act", 2)], [("rot", 16), ("v_lat", 2)], [("in_act", 6)]]
            events = [[(0, 0)], [(1, 2)], [(2, 0), (3, 2)], [(4, 0), (5, 2)], [(6, 0), (7, 2)]]
            for c in range(5):
                for side, (event, b) in enumerate(events[c]):
                    for name, n in bank_read[event]:
                        pe.wait_ge(sem(name), n)
                    for j in range(2):
                        u = 2 * c + j
                        if side == 0:
                            unit_wait(u)
                        hi, lo = (xT_hi, xT_lo) if side == 0 else (ctxT_hi, ctxT_lo)
                        if c == 2 and side == 1 and j == 0:
                            pe.wait_ge(*seen("lo", "n_ctx", KT))
                        last = s_used if side == len(events[c]) - 1 else None
                        ins = half(u, j, hi, lo, bank[b:b + 2], last, "n_x" if c == 0 else None)
                    if last is None:
                        ins.then_inc(sem("in_lat"), 1)
                    if c == 1:
                        pe.wait_ge(*seen("full", "n_ctx", KT))
                    if c >= 1 and side == 0:
                        turn_heads(c - 1)
                    if c >= 3 and side == 0:
                        job_reduce(c - 3)
                if c == 0:
                    pe.wait_ge(sem("four_in"), 16 * 5)
                    for m in range(2):
                        for f in range(2):
                            ins = pe.matmul(bank[2][:, 256 * m + P * f:256 * m + P * f + P], four_c[:, m, :], four_w[:, f, :],
                                            start=True, stop=True)
                    ins.then_inc(sem("four_gmm"), 1)
                    turn_norm("n_ctx", ctx_x, bank[4:8])
                    pe.wait_ge(sem("four_gs"), 1)

            pe.wait_ge(sem("dft_in"), 16)
            pe.wait_ge(sem("f_tok"), 2)
            pe.wait_ge(sem("turn_out"), 12)
            for f in range(2):
                for t in range(NT):
                    ins = pe.matmul(bank[4 + f][:, :], f_tok[:, t, f * P:f * P + P], dft[:, t, :], start=t == 0, stop=t == NT - 1)
                ins.then_inc(sem("four_ft"), 1)

            ITS = [(h, t) for h in range(HEADS) for t in range(NT)]

            def scores(n):
                h, t = ITS[n]
                b = n % 2
                if n >= 2:
                    pe.wait_ge(sem("d_exp"), 2 * (n - 1))
                for c in range(2):
                    pe.matmul(bank[2 * b + c][:, :], qT[64 * c:64 * c + 64, h, t * P:t * P + P],
                              kT[64 * c:64 * c + 64, h, :], start=True, stop=True).then_inc(sem("d_s"), 1)

            def turn_diff(n):
                pe.wait_ge(sem("d_diff"), n + 1)
                if n >= 2:
                    pe.wait_ge(sem("d_diffT"), n - 1)
                for k in range(4):
                    ins = pe.transpose(bank[4 + n % 2][:, k * P:k * P + P], diff[:, n % 2, k * P:k * P + P], ident[:, :])
                ins.then_inc(sem("d_turn"), 1)

            def diff_v(n):
                h, t = ITS[n]
                pe.wait_ge(sem("d_diffT"), n + 1)
                if n >= 2:
                    pe.wait_ge(sem("d_o"), n - 1)
                for k in range(4):
                    ins = pe.matmul(bank[6 + n % 2][:, 0:P], diffT[:, n % 2, k, :], v_tok[:, k, h * P:h * P + P],
                                    start=k == 0, stop=k == 3)
                ins.then_inc(sem("d_pv"), 1)

            pe.wait_ge(sem("in_act"), 10)
            pe.wait_ge(sem("v_lat"), 2)
            scores(0)
            scores(1)
            pe.wait_ge(sem("four_fts"), 2)
            for f in range(2):
                for n in range(2):
                    ins = pe.matmul(bank[6][:, 256 * f:256 * f + 256], four_g[:, n, f, :],
                                    ftT[:, f, 256 * n:256 * n + 256], start=n == 0, stop=n == 1)
            ins.then_inc(sem("four_y"), 1)
            job_reduce(2)
            for n in range(len(ITS)):
                if n + 2 < len(ITS):
                    scores(n + 2)
                turn_diff(n)
                if n == 1:
                    pe.wait_ge(sem("four_lo"), 2)
                if n == 2:
                    pe.wait_ge(s_cols, 3)
                if n >= 1:
                    diff_v(n - 1)
            diff_v(len(ITS) - 1)
            pe.wait_ge(*seen("xn", "sub", NT))
            for h in range(HEADS):
                for t in range(NT):
                    pe.transpose(bank[2 + h // 2][:, 256 * (h % 2) + t * P:256 * (h % 2) + t * P + P],
                                 o_tok[:, t, h * P:h * P + P], ident[:, :]).then_inc(sem("tr"), 1)

            def dense(stage, n_chunks, ready=None, after=None, before=None, parts=True, job=()):
                for c in range(n_chunks):
                    if before is not None:
                        before(c)
                    for j in range(2):
                        u = BASE[stage] + 2 * c + j
                        unit_wait(u)
                        half(u, j, xT_hi, xT_lo, bank[2 * (c % 2):2 * (c % 2) + 2], s_used,
                             ready if c == 0 else None, part=parts and n_chunks == 2)
                        if (c, j) == job[:2]:
                            job_reduce(job[2])
                    if after is not None:
                        after(c)

            dense("out", 2, "sub", gate_after("out"))

            def ffn(layer, loops, first_job):
                base = BASE[f"ffn{layer}"]
                off = layer * FCH
                turn_norm(f"n_ffn{layer}", xn, bank[2:6])

                def up(c, u, i=None, ready=None):
                    for j in range(2):
                        unit_wait(u + j, i)
                        half(u + j, j, xT_hi, xT_lo, bank[0:2], s_used, ready)

                def down(c, u, i=None, last=False):
                    unit_wait(u, i)
                    pe.wait_ge(sem("hT_lo"), at(off + c + 1, i, 2))
                    wh = w_hi[u % N_SPLIT][:, :].rearrange("p (k n) -> p k n", k=2)
                    wl = w_lo[u % N_SPLIT][:, :].rearrange("p (k n) -> p k n", k=2)
                    order = [(k, h, t) for k in range(2) for h in range(2) for t in range(NT)]
                    if last:
                        order = [(k, h, t) for h in range(2) for t in range(NT) for k in range(2)]
                    for n, (k, h, t) in enumerate(order):
                        ins = three(bank[2 + 2 * h + t][:, :], hT_hi[:, k, t * P:t * P + P],
                                    hT_lo[:, k, t * P:t * P + P], wh[:, k, 512 * h:512 * h + 512],
                                    wl[:, k, 512 * h:512 * h + 512], False, last and k == 1)
                        if last and n in (1, 3, 5):
                            ins.then_inc(sem("part"), 1)
                    ins.then_inc(s_used, 1)

                def turn_hidden(c, i=None):
                    pe.wait_ge(sem("hid"), at(2 * (off + c) + 2, i, 4))
                    if c >= 1 or layer:
                        pe.wait_ge(sem("hT_lo"), at(off + c, i, 2))
                    for t in range(NT):
                        for k in range(2):
                            ins = pe.transpose(bank[6][:, 256 * k + t * P:256 * k + t * P + P],
                                               hid[:, t, k * P:k * P + P], ident[:, :])
                    ins.then_inc(sem("h_turn"), 1)

                up(0, base, None, f"n_ffn{layer}")
                if layer == 0:
                    job_reduce(3)
                turn_hidden(0)
                gate_mm(f"ffn{layer}")
                pe.wait_ge(*seen("gate", f"ffn{layer}", 2))
                if layer == 1:
                    gate_mm("final", bias_gate)
                    pe.wait_ge(*seen("gate", "final", 2))
                pe.wait_ge(sem("zeros"), layer + 1)
                for n in range(4):
                    pe.matmul(bank[2 + n][:, :], zeros[0:1, 0:P], zeros[0:1, :], start=True, stop=False)
                done = 0
                for q, n in loops:
                    with pe.Fori(0, n) as i:
                        for b in range(2):
                            u = base + 2 + 6 * done + 3 * b
                            c = 1 + 2 * done + b
                            up(c, u, i)
                            if b == 1:
                                job_reduce(q, i)
                            down(c - 1, u + 2, i)
                            turn_hidden(c, i)
                    done += n
                down(FCH - 1, base + 3 * FCH - 1, None, True)
                job_reduce(first_job + 5)

            ffn(0, [(4, 5)], 4)
            turn_norm("n_pw1", xn, bank[2:6])

            def turn_pair(stage, src, free):
                def after(c):
                    pe.wait_ge(sem(f"{stage}_tok"), 2 * c + 2)
                    if c >= 1:
                        free(c)
                    for g in range(2):
                        for k in range(2):
                            for t in range(NT):
                                ins = pe.transpose(bank[4 + g][:, 256 * k + t * P:256 * k + t * P + P],
                                                   src[:, t, 256 * g + k * P:256 * g + k * P + P], ident[:, :])
                    ins.then_inc(sem(f"{stage}_turn"), 1)
                return after

            def pw1_free(c):
                pe.wait_ge(sem("pw1_glu"), 2 * c)

            def pw1_after(c):
                turn_pair("pw1", ag_tok, pw1_free)(c)
                if c >= 1:
                    conv_diag(c - 1)

            def conv_diag(c):
                pe.wait_ge(sem("pw1_glu"), 2 * c + 2)
                if c >= 1:
                    pe.wait_ge(sem("conv_whole"), 2 * c)
                for e in range(2):
                    for n in range(PE_TAPS):
                        pe.wait_ge(sem("tap_diag"), (2 * c + e) * PE_TAPS + n + 1)
                        tap = CONV - PE_TAPS + n
                        ins = pe.matmul(bank[6][:, 256 * e:256 * e + 256], tap_diag[e][:, n, :],
                                        u_pad[:, 2 * c + e, tap:tap + S], start=n == 0, stop=n == PE_TAPS - 1)
                ins.then_inc(sem("conv_pe"), 1)

            dense("pw1", 4, "n_pw1", pw1_after)
            conv_diag(3)
            for k in range(KT):
                pe.wait_ge(sem("conv_whole"), k + 1)
                if k == 0:
                    pe.wait_ge(sem("pw1_glu"), KT)
                ins = pe.matmul(bank[4][:, 0:S], ones[:, :], conv[:, k, :], start=k == 0, stop=k == KT - 1)
            ins.then_inc(sem("ln_mean_mm"), 1)
            for k in range(KT):
                pe.wait_ge(sem("ln_sq"), k + 1)
                ins = pe.matmul(bank[5][:, 0:S], ones[:, :], csq[:, k, :], start=k == 0, stop=k == KT - 1)
            ins.then_inc(sem("ln_var_mm"), 1)
            pe.wait_ge(sem("ln_var"), 1)
            for t in range(NT):
                ins = pe.transpose(bank[4][:, t * P:t * P + P], rln[:, t * P:t * P + P], ident[:, :])
            ins.then_inc(sem("ln_var_tr"), 1)
            pe.wait_ge(sem("ln_diag"), 2)
            pe.matmul(bank[5][:, 0:S], ones[:, :], rln[:, :], start=True, stop=True).then_inc(sem("ln_row_mm"), 1)
            dense("pw2", 2, "ln", gate_after("pw2"))
            ffn(1, [(10, 5)], 10)

            turn_norm("n_rg", xn, bank[2:6])

            def rg_gate_mm(g):
                n, h = RG_GROUPS[g]
                if g < 2:
                    pe.wait_ge(sem(f"rg_w{g}"), 16)
                else:
                    pe.wait_ge(sem("rg_sig"), 2 * (g - 1))
                pe.wait_ge(sem("rg_conv"), RG_CONV * 4 * (h // 2 + 1))
                for e in range(2):
                    for k in range(2):
                        ins = pe.matmul(bank[6 + g % 2][:, 256 * e:256 * e + 256], rg_w[n][:, h, k, P * e:P * e + P],
                                        uc[:, 2 * h + k, :], start=k == 0, stop=k == 1)
                ins.then_inc(sem("rg_gates"), 1)

            def rg_free(c):
                pe.wait_ge(sem("rg_turned"), 2 * c)

            pe.wait_ge(s_cols, 16)
            for c in range(4):
                for j in range(2):
                    u = BASE["rg_in"] + 2 * c + j
                    unit_wait(u)
                    for t in range(NT):
                        half(u, j, xT_hi, xT_lo, bank[2 * (c % 2):2 * (c % 2) + 2], s_used if t == 1 else None,
                             "n_rg" if c == 0 else None, (t,))
                        for g in {(2, 0, 1): (2, 3), (2, 1, 0): (4, 5), (2, 1, 1): (6, 7)}.get((c, j, t), ()):
                            rg_gate_mm(g)
                turn_pair("rg_in", rg_tok, rg_free)(c)
                if c == 1:
                    rg_gate_mm(0)
                    rg_gate_mm(1)
            pe.wait_ge(sem("rg_in_tok"), 8)
            pe.wait_ge(sem("rg_turned"), 8)
            pe.wait_ge(sem("rg_sig"), 2 * KT)
            dense("rg_out", 2, "rg", gate_after("rg_out"))

            turn_norm("n_kv", xn, bank[2:6])

            def attn_after(stage):
                def after(c):
                    if c >= 2:
                        return
                    for t in range(NT):
                        n = 2 * c + t
                        pe.wait_ge(sem(f"{stage}_tok"), n + 1)
                        if n >= 2:
                            pe.wait_ge(sem(f"{stage}_turned"), n - 1)
                        for h in range(4):
                            ins = pe.transpose(bank[4 + n % 2][:, h * P:h * P + P], a_tok[:, t, h * P:h * P + P], ident[:, :])
                        ins.then_inc(sem(f"{stage}_turn"), 1)
                return after

            def rows_read(stage):
                def before(c):
                    if c == 2:
                        pe.wait_ge(sem(f"{stage}_tok"), 2)
                    if c == 3:
                        pe.wait_ge(sem(f"{stage}_tok"), 4)
                return before

            dense("kv", 4, "n_kv", attn_after("kv"), rows_read("kv"), job=(2, 0, 16))
            pe.wait_ge(sem("kv_turned"), 4)
            pe.wait_ge(sem("kv_rows"), 4)
            for k in range(KT):
                for t in range(NT):
                    pe.transpose(bank[2 + k // 2][:, 256 * (k % 2) + t * P:256 * (k % 2) + t * P + P],
                                 xn[:, t, k * P:k * P + P], ident[:, :]).then_inc(sem("tr"), 1)
            dense("att_in", 2, "n_att", attn_after("att_in"), parts=False, job=(1, 0, 17))

            A_ITS = [(h, t) for h in range(A_HEADS) for t in range(NT)]

            def a_scores(n):
                h, t = A_ITS[n]
                if n == 0:
                    pe.wait_ge(sem("mask_in"), 16)
                if n >= 2:
                    pe.wait_ge(sem("a_exp"), n - 1)
                s_bank = bank[2 + n % 2]
                pe.matmul(s_bank[:, 0:(t + 1) * P], aqT[:, h, t * P:t * P + P], akT[:, h, 0:(t + 1) * P],
                          start=True, stop=False)
                pe.matmul(s_bank[:, t * P:(t + 1) * P], ident[:, :], mask[:, :], start=False, stop=True).then_inc(sem("a_s"), 1)

            def a_turn(n):
                h, t = A_ITS[n]
                pe.wait_ge(sem("a_exp"), n + 1)
                if n >= 2:
                    pe.wait_ge(sem("a_apT"), n - 1)
                for k in range(t + 1):
                    ins = pe.transpose(bank[4 + n % 2][:, k * P:k * P + P], ap_[:, n % 2, k * P:k * P + P], ident[:, :])
                ins.then_inc(sem("a_turn"), 1)

            def a_v(n):
                h, t = A_ITS[n]
                pe.wait_ge(sem("a_apT"), n + 1)
                if n >= 2:
                    pe.wait_ge(sem("a_o"), n - 1)
                for k in range(t + 1):
                    ins = pe.matmul(bank[6 + n % 2][:, 0:P], apT[:, n % 2, k, :], av[:, k, h * P:h * P + P],
                                    start=k == 0, stop=k == t)
                ins.then_inc(sem("a_pv"), 1)

            def gate_group(g):
                c, j, t, e = 2 + g // 8, g // 4 % 2, g // 2 % 2, g % 2
                u = BASE["att_in"] + 2 * c + j
                if g == 0:
                    pe.wait_ge(sem("att_in_tok"), 2)
                if g == 8:
                    pe.wait_ge(sem("att_in_rows"), 2)
                if g % 4 == 0:
                    unit_wait(u)
                half(u, j, xT_hi, xT_lo, bank[0:2], s_used if g % 4 == 3 else None, None, (t,), (2 * e, 2 * e + 1))

            def attend(n):
                if n + 2 < len(A_ITS):
                    a_scores(n + 2)
                a_turn(n)
                if n >= 1:
                    a_v(n - 1)

            gate_group(0)
            gate_group(1)
            pe.wait_ge(sem("att_in_turned"), 4)
            pe.wait_ge(s_cols, 18)
            a_scores(0)
            a_scores(1)
            for g in range(2, 16):
                gate_group(g)
                attend(g - 2)
            attend(14)
            attend(15)
            a_v(len(A_ITS) - 1)
            pe.wait_ge(sem("a_o"), len(A_ITS))
            for k in range(KT):
                pe.wait_ge(sem("ao_gated"), 2 * (k // 4) + 2)
                for t in range(NT):
                    pe.transpose(bank[4 + k // 2][:, 256 * (k % 2) + t * P:256 * (k % 2) + t * P + P],
                                 ao[:, t, k * P:k * P + P], ident[:, :]).then_inc(sem("tr"), 1)
            pe.wait_ge(sem("att_in_rows"), 4)
            dense("att_out", 2, "ao", gate_after("att_out"))


CONSTS = ("k_ident", "k_rope", "k_dft", "k_dft64", "k_mask")


def constants():
    import numpy as np

    ident = np.eye(P, dtype=np.float32)
    grid_w = 64
    inv = np.float32(10000.0) ** (-np.arange(0, 32, 2, dtype=np.float32) / np.float32(32))
    row = np.repeat(np.arange(S // grid_w, dtype=np.float32), grid_w)
    col = np.tile(np.arange(grid_w, dtype=np.float32), S // grid_w)
    ang = np.concatenate([row[:, None] * inv, col[:, None] * inv], axis=-1).astype(np.float32)
    rope = np.stack([np.cos(ang), np.sin(ang)], axis=1).astype(np.float32)
    n = np.arange(S)
    a = 2 * np.pi * ((n[:, None] * n[None, :]) % S) / S
    dft = np.concatenate([np.cos(a), np.sin(a)], axis=1).astype(np.float32)
    m = np.arange(64)
    b = 2 * np.pi * ((m[:, None] * m[None, :]) % 64) / 64
    norm = 1.0 / np.sqrt(S * 64)
    d64 = np.zeros((2, P, P), np.float32)
    for g in range(2):
        r = slice(64 * g, 64 * g + 64)
        d64[0, r, r] = np.cos(b) * norm
        d64[1, r, r] = -np.sin(b) * norm
    mask = np.where(np.arange(P)[None, :] <= np.arange(P)[:, None], 0.0, NEG).astype(np.float32)
    return {"k_ident": ident, "k_rope": rope, "k_dft": dft, "k_dft64": d64, "k_mask": mask}


def kernel(**inputs):
    import numpy as np
    import concourse.bacc as bacc
    from concourse.bass_utils import run_bass_kernel_spmd

    nc = bacc.Bacc("TRN2", target_bir_lowering=False, num_devices=1)
    arrays, tensors = {}, {}
    for name, a in {**inputs, **constants()}.items():
        a = np.ascontiguousarray(a)
        arrays[name + "_dram"] = a
        tensors[name] = nc.dram_tensor(name + "_dram", a.shape, mybir.dt.from_np(a.dtype), kind="ExternalInput").ap()
    out = nc.dram_tensor("out_dram", (1, S, D), F32, kind="ExternalOutput").ap()
    build(nc, tensors, out)
    return run_bass_kernel_spmd(nc, [arrays], core_ids=[0]).results[0]["out_dram"]
```

```python
from contextlib import ExitStack

import concourse.bass as bass
from concourse import mybir

F32 = mybir.dt.float32
R32 = mybir.dt.float32r
BF16 = mybir.dt.bfloat16
ALU = mybir.AluOpType
ACT = mybir.ActivationFunctionType
AX_X = mybir.AxisListType.X

P = 128
D = 1024
KT = D // P
S = 256
NT = S // P
EPS = 1e-6
D_FF = 2816
DIFF_W = 768
HEADS = DIFF_W // P
KEYS = 2 * S
SUB_SCALE = 1.0 - 0.2
CONV = 31
PAD = CONV // 2
PE_TAPS = 11
RG_CONV = 4
RG_C = 8.0
A_HEADS = 8

UNIT = 2048
N_LAND = 6
N_SPLIT = 3
N_ALAND = 2
ADA0 = 8
FCH = D_FF // 256
NEG = -1e30

V_MOD0, V_KV, V_MOD1 = 12, 15, 17
JOBS = list(range(2, 20))

STAGES = [("in", 10), ("out", 4), ("ffn0", 3 * FCH), ("pw1", 8), ("pw2", 4), ("ffn1", 3 * FCH),
          ("rg_in", 8), ("rg_out", 4), ("kv", 8), ("att_in", 8), ("att_out", 4)]
BASE = {}
_n = 0
for _name, _count in STAGES:
    BASE[_name] = _n
    _n += _count
UNITS = _n

ROW_GROUPS = [
    [("ada_b", 96), ("c", 8), ("c_ctx", 8), ("c_2", 8), ("final_g", 8)],
    [("mod_b_2_0", 24), ("kv_mod_b_2", 16), ("mod_b_2_1", 24), ("mix_norm_g", 16), ("ffn_norm_g", 16), ("norm_g_2", 16),
     ("kv_norm_g_2", 8), ("final_norm_g_2", 8)],
    [("od_pw1_b", 16), ("od_dw_b", 8), ("od_ln_g", 8), ("od_ln_b", 8), ("od_pw2_b", 8),
     ("rg_conv_b_2", 8), ("rg_b_a_2", 8), ("rg_b_x_2", 8), ("rg_lambda_2", 8), ("rg_conv_w_2", 32),
     ("ev_subln_g", 1)],
    [("od_dw_w_a", 16 * 8)],
    [("od_dw_w_b", 15 * 8)],
]
COL = {}
for _g, _rows in enumerate(ROW_GROUPS):
    _r = 0
    for _name, _count in _rows:
        COL[_name] = _g * P + _r
        _r += _count

WHOLE = {"ss": NT, "ms": 1, "rstd": 1, "xn": NT, "tr": 2 * KT, "full": KT, "hi": KT, "lo": KT}
SPLIT = {"full": KT, "hi": KT, "lo": KT}
TILED = {"ss": 2 * NT, "ms": NT, "rstd": NT, "xn": NT, "tr": NT * KT, "full": NT * KT, "hi": NT * KT, "lo": NT * KT}
RESCALED = {"ss": 2 * NT, "ms": NT, "rstd": NT, "xn": NT}
GATED = {"diag": 1, "gmm": 1, "gate": 2}
PRODUCT = {**GATED, "part": 2}
STEPS = [("n_x", WHOLE), ("n_ctx", WHOLE),
         ("sub", {"ss": 12, "ms": 1, "rstd": 1, "xn": NT, "tr": 2 * HEADS, "full": HEADS, "hi": HEADS, "lo": HEADS}),
         ("out", PRODUCT), ("n_ffn0", TILED), ("ffn0", {**GATED, "part": 3}), ("n_pw1", TILED),
         ("ln", {"ms": 1, "rstd": 1, **SPLIT}), ("pw2", PRODUCT),
         ("pw2b", GATED), ("n_ffn1", TILED), ("ffn1", {**GATED, "part": 3}), ("n_final", RESCALED), ("final", GATED),
         ("n_rg", {**TILED, "ss": NT}), ("rg", SPLIT), ("rg_out", PRODUCT), ("n_kv", TILED), ("n_att", {"tr": 2 * KT, **SPLIT}),
         ("ao", {"tr": 2 * KT, "hi": KT, "lo": KT}), ("att_out", PRODUCT), ("n_last", RESCALED), ("last", GATED)]
STEPS_BEFORE = {}
_seen = {}
for _stage, _adds in STEPS:
    for _kind, _count in _adds.items():
        STEPS_BEFORE[_kind, _stage] = _seen.get(_kind, 0)
        _seen[_kind] = _seen.get(_kind, 0) + _count
ADDS = dict(STEPS)

AFTER_DENSE = ((4, 5), (2, 3))
AFTER_FFN = ((2, 4), (3, 5))
RG_GROUPS = [(0, 0), (0, 1), (1, 0), (1, 1), (0, 2), (0, 3), (1, 2), (1, 3)]


def rg_sigs(n, k):
    return 2 * RG_GROUPS.index((n, k // 2)) + k % 2 + 1


def at(base, i=None, step=0):
    return base if i is None else i * step + base


def build(nc, t_in, out):
    with ExitStack() as ctx:
        sems = {}

        def sem(name):
            if name not in sems:
                sems[name] = ctx.enter_context(nc.semaphore(name))
            return sems[name]

        def seen(kind, stage, n):
            return sem(kind), STEPS_BEFORE[kind, stage] + n

        ARENA = 16512

        def place(name, shape, offset, dtype=F32):
            return nc.alloc_sbuf_tensor_at(name, shape, dtype, offset=ARENA + offset)

        KB = 1024
        w_land = [place(f"w_land{i}", [P, UNIT], 8 * KB * i) for i in range(N_LAND)]
        w_hi = [place(f"w_hi{i}", [P, UNIT], (48 + 8 * i) * KB, R32) for i in range(N_SPLIT)]
        w_lo = [place(f"w_lo{i}", [P, UNIT], (72 + 8 * i) * KB, R32) for i in range(N_SPLIT)]
        a_land = [place(f"a_land{i}", [P, UNIT], (96 + 8 * i) * KB) for i in range(N_ALAND)]
        job_sum = place("job_sum", [P, D], 112 * KB)
        BIG = 116 * KB
        xT_hi = place("xT_hi", [P, KT, S], 164 * KB, R32)
        xT_lo = place("xT_lo", [P, KT, S], 172 * KB, R32)
        x = place("x", [P, NT, D], 180 * KB)
        S1 = 188 * KB
        xn = place("xn", [P, NT, D], S1)
        xfull = place("xfull", [P, KT, S], BIG + 40 * KB)
        gate = place("gate", [P, D], 196 * KB)
        SMALL = [200 * KB]

        def small(name, shape):
            size = 4
            for n in shape[1:]:
                size *= n
            offset = SMALL[0]
            SMALL[0] += -(-size // 32) * 32
            assert ARENA + SMALL[0] <= 229344
            return place(name, shape, offset)

        ident = small("ident", [P, P])
        ones = small("ones", [P, P])
        pcol = small("pcol", [P, 5 * P])
        mcol = small("mcol", [P, 20 * KT])
        mcol_ctx = small("mcol_ctx", [P, 2 * KT])
        silu_c = small("silu_c", [P, 3, KT])
        four_g = small("four_g", [P, 2, 2, P])
        rope = small("rope", [P, NT, 2, 32])
        mask = place("mask", [P, P], SMALL[0] - 512)
        a_col = small("a_col", [P, KT])
        b_col = small("b_col", [P, KT])
        ss = small("ss", [P, 12])
        ms = small("ms", [P, 12])
        rstd = small("rstd", [P, 12])
        neg_half = small("neg_half", [P, 12])
        lam_tmp = small("lam_tmp", [P, 8])
        mx = small("mx", [P, 2, 2])
        nb = small("nb", [P, 2, 2])
        esum = small("esum", [P, 2, 2])
        rsum = small("rsum", [P, 2, 2])
        sp_c = small("sp_c", [P, 8, KT])
        prow = place("prow", [P, 5, P], 112 * KB)
        ctx_x = place("ctx_x", [P, NT, D], BIG)
        ctx_full = place("ctx_full", [P, KT, S], BIG)
        ada_rows = place("ada_rows", [2, 2 * D], BIG + 8 * KB)
        ctx_junk = place("ctx_junk", [P, NT, D], BIG + 18 * KB)
        lam_in = place("lam_in", [P, 4, 64], BIG + 16 * KB)
        lam_junk = place("lam_junk", [P, 2, 64], BIG + 17 * KB)
        ctxT_hi = place("ctxT_hi", [P, KT, S], BIG + 32 * KB, R32)
        ctxT_lo = place("ctxT_lo", [P, KT, S], BIG + 40 * KB, R32)
        qT = place("qT", [P, HEADS, S], BIG)
        kT = place("kT", [P, HEADS, KEYS], BIG + 6 * KB)
        v_tok = place("v_tok", [P, 4, DIFF_W], BIG + 18 * KB)
        f_tok = place("f_tok", [P, NT, S], BIG + 30 * KB)
        rope_cos = place("rope_cos", [P, 512], 196 * KB)
        rope_sin = place("rope_sin", [P, 512], 198 * KB)
        rot = place("rot", [P, 2, 512], S1)
        k_ctx = place("k_ctx", [P, 2, 512], S1 + 4 * KB)
        prob = place("prob", [P, 2, 2, 512], BIG + 32 * KB)
        diff = place("diff", [P, 2, 512], BIG + 40 * KB)
        diffT = place("diffT", [P, 2, 4, P], BIG + 44 * KB)
        o_tok = place("o_tok", [P, NT, DIFF_W], S1)
        o_full = place("o_full", [P, HEADS, S], BIG + 40 * KB)
        dft = place("dft", [P, NT, 512], 196 * KB)
        ftT = place("ftT", [P, 2, 512], S1 + 4 * KB)
        four_c = place("four_c", [P, 2, P], BIG + 26 * KB)
        four_w = place("four_w", [P, 2, P], BIG + 27 * KB)
        sq_junk = place("sq_junk", [P, 2, P], S1 + 6 * KB)
        silu_g = place("silu_g", [P, NT, 256], BIG)
        hid = place("hid", [P, NT, 256], BIG + 2 * KB)
        hT_hi = place("hT_hi", [P, 2, S], BIG + 4 * KB, R32)
        hT_lo = place("hT_lo", [P, 2, S], BIG + 6 * KB, R32)
        zeros = place("zeros", [P, 512], BIG + 8 * KB, BF16)
        UP = S + 2 * PAD
        u_pad = place("u_pad", [P, KT, UP], BIG)
        conv = place("conv", [P, KT, S], BIG + 9 * KB)
        ag_tok = place("ag_tok", [P, NT, 512], BIG + 17 * KB)
        sig = place("sig", [P, 2, S], BIG + 21 * KB)
        csq = place("csq", [P, KT, S], BIG + 23 * KB)
        mean = place("mean", [P, S], BIG + 31 * KB)
        rln = place("rln", [P, S], BIG + 32 * KB)
        tap_diag = [place("tap_diag0", [P, PE_TAPS, P], BIG + 23 * KB), place("tap_diag1", [P, PE_TAPS, P], BIG + 38 * KB)]
        bias_gate = place("bias_gate", [P, D], BIG + 34 * KB)
        RUP = S + RG_CONV - 1
        ru_pad = place("ru_pad", [P, KT, RUP], BIG)
        gT = place("gT", [P, KT, S], BIG + 9 * KB)
        rg_tok = place("rg_tok", [P, NT, 512], BIG + 17 * KB)
        uc = place("uc", [P, KT, S], BIG + 21 * KB)
        r_gate = place("r_gate", [P, KT, S], BIG + 29 * KB)
        i_gate = place("i_gate", [P, KT, S], BIG + 37 * KB)
        b_seq = place("b_seq", [P, KT, S], BIG)
        y_full = place("y_full", [P, KT, S], S1)
        rg_w = [place(f"rg_w{n}", [P, 4, 2, S], (96 + 8 * n) * KB) for n in range(2)]
        akT = place("akT", [P, KT, S], BIG)
        aqT = place("aqT", [P, KT, S], BIG + 8 * KB)
        av = place("av", [P, NT, D], BIG + 16 * KB)
        ag = place("ag", [P, NT, D], BIG + 24 * KB)
        a_tok = place("a_tok", [P, NT, 512], BIG + 32 * KB)
        ap_ = place("ap_", [P, 2, S], BIG + 36 * KB)
        apT = place("apT", [P, 2, NT, P], BIG + 38 * KB)
        ao = place("ao", [P, NT, D], BIG + 40 * KB)
        kv_full = place("kv_full", [P, KT, S], BIG + 40 * KB)
        last_gate = place("last_gate", [P, D], BIG)
        tmp = place("tmp", [P, 2, 512], BIG + 9 * KB)
        sq_half = place("sq_half", [P, 2, 512], BIG + 13 * KB)

        bank = [ctx.enter_context(nc.psum_tensor(f"bank{i}", [P, 512], F32)) for i in range(8)]
        COLS = bank[7]

        landed = [sem(f"w_landed{i}") for i in range(N_LAND)]
        a_landed = [sem(f"a_landed{i}") for i in range(N_ALAND)]
        s_hi, s_lo, s_used = sem("w_hi"), sem("w_lo"), sem("w_used")
        s_step, s_red, s_cols = sem("job_step"), sem("job_reduced"), sem("job_cols")

        def kview(w, n=None):
            return w.rearrange("(k p) n -> p k n", p=P)

        def pc(name, k=0, n=1):
            return pcol[:, COL[name] + k:COL[name] + k + n]

        def mc(v, k=0, n=KT):
            return mcol[:, v * KT + k:v * KT + k + n]

        block = ctx.enter_context(nc.Block())

        @block.sync
        def _(sp):
            def load_unit(u, parts, i=None):
                n = u + ADA0
                if n >= N_LAND:
                    if n - N_LAND < ADA0:
                        sp.wait_ge(sem("ada0_used"), n - N_LAND + 1)
                    else:
                        sp.wait_ge(s_lo, at(n - N_LAND - ADA0 + 1, i, 6))
                slot = n % N_LAND
                for view, src in parts(w_land[slot]):
                    sp.dma_start(view, src).then_inc(landed[slot], 16)

            def cols_half(w, col, j):
                def parts(land):
                    v = land[:, :].rearrange("p (k n) -> p k n", k=4)
                    return [(v[:, 2 * h:2 * h + 2, :],
                             kview(w)[:, 4 * j + 2 * h:4 * j + 2 * h + 2, bass.ds(col, 512)]) for h in range(2)]
                return parts

            def cols_pair(wa, ca, wb, cb, j):
                def parts(land):
                    v = land[:, :].rearrange("p (k n) -> p k n", k=4)
                    return [(v[:, :, 256 * h:256 * h + 256], kview(w)[:, 4 * j:4 * j + 4, bass.ds(c, 256)])
                            for h, (w, c) in enumerate(((wa, ca), (wb, cb)))]
                return parts

            def rows_pair(w, row, col=0):
                def parts(land):
                    v = land[:, :].rearrange("p (k n) -> p k n", k=2)
                    return [(v[:, h, :], w[bass.ds(row + h * P, P), col:col + D]) for h in range(2)]
                return parts

            ada = t_in["ada_w"]
            w_in = t_in["ev_w_in"][0]

            def rows(name, src, n, g, r):
                sp.dma_start(prow[r:r + n, g, :], src).then_inc(sem(f"prow{g}"), 16)

            def as_rows(name):
                h = t_in[name]
                if len(h.shape) == 1:
                    return h.rearrange("(r p) -> r p", p=P)
                if len(h.shape) == 3:
                    h = h[0]
                return h.rearrange("a (r p) -> (a r) p", p=P)

            def load_rows(g):
                r = 0
                for name, n in ROW_GROUPS[g]:
                    if name == "od_dw_w_a":
                        src = as_rows("od_dw_w")[0:n, :]
                    elif name == "od_dw_w_b":
                        src = as_rows("od_dw_w")[P:P + n, :]
                    elif name in ("mod_b_2_0", "mod_b_2_1"):
                        layer = int(name[-1])
                        src = as_rows("mod_b_2")[n * layer:n * layer + n, :]
                    else:
                        src = as_rows(name)
                    rows(name, src, n, g, r)
                    r += n

            sp.dma_start(ident[:, :], t_in["k_ident"]).then_inc(sem("ident_in"), 16)
            load_rows(0)
            sp.dma_start(x[:, :, :], t_in["x"][0].rearrange("(t p) d -> p t d", p=P)).then_inc(sem("x_in"), 16)
            for n in range(4):
                load_unit(n - ADA0, rows_pair(ada[0], n * 256))
            load_rows(1)
            for n in range(4, 6):
                load_unit(n - ADA0, rows_pair(ada[0], (n - 4) * 256, D))
            for g in (2, 3, 4):
                load_rows(g)
            sp.dma_start(rope[:, :, :, :], t_in["k_rope"].rearrange("(t p) c d -> p t c d", p=P)).then_inc(sem("rope_in"), 16)
            for n, name in enumerate(("ev_lambda_q1", "ev_lambda_k1", "ev_lambda_q2", "ev_lambda_k2")):
                sp.dma_start(lam_in[:, n, :], t_in[name][0:1, :].broadcast_to([P, 64])).then_inc(sem("lam_in"), 16)
            for n in range(6, ADA0):
                load_unit(n - ADA0, rows_pair(ada[0], (n - 4) * 256, D))

            in_cols = [lambda j: cols_half(w_in, 0, j), lambda j: cols_pair(w_in, 512, w_in, 3 * DIFF_W, j),
                       lambda j: cols_half(w_in, 768, j), lambda j: cols_half(w_in, 1280, j),
                       lambda j: cols_half(w_in, 1792, j)]
            for c in range(5):
                for j in range(2):
                    load_unit(2 * c + j, in_cols[c](j))
                if c == 0:
                    sp.dma_start(ctx_x[:, :, :], t_in["ctx"][0].rearrange("(t p) d -> p t d", p=P)).then_inc(sem("ctx_in"), 16)
                    sp.dma_start(four_c[:, :, :], t_in["k_dft64"].rearrange("c p n -> p c n")).then_inc(sem("four_in"), 16)
                    sp.wait_ge(sem("four_zero"), 1)
                    for g in range(4):
                        r = 64 * (g % 2)
                        sp.dma_start(four_w[r:r + 64, g // 2, r:r + 64], t_in["ev_fourier_w"][0, g]).then_inc(sem("four_in"), 16)

            def load_dense(stage, w, n_cols):
                for c in range(n_cols // 512):
                    for j in range(2):
                        load_unit(BASE[stage] + 2 * c + j, cols_half(w, 512 * c, j))

            def load_ffn(layer, loops):
                w1, w3, w2 = (t_in[n][layer] for n in ("ffn_w1", "ffn_w3", "ffn_w2"))
                base = BASE[f"ffn{layer}"]
                for j in range(2):
                    load_unit(base + j, cols_pair(w1, 0, w3, 0, j))
                done = 0
                for n in loops:
                    with sp.Fori(0, n) as i:
                        for b in range(2):
                            u = base + 2 + 6 * done + 3 * b
                            c = 1 + 2 * done + b
                            for j in range(2):
                                load_unit(u + j, cols_pair(w1, i * 512 + 256 * c, w3, i * 512 + 256 * c, j), i)
                            load_unit(u + 2, rows_pair(w2, i * 512 + 256 * (c - 1)), i)
                    done += n
                load_unit(base + 3 * FCH - 1, rows_pair(w2, 256 * (FCH - 1)))

            load_dense("out", t_in["ev_w_out"][0], D)
            load_ffn(0, (5,))

            def load_pairs(stage, w):
                for c in range(4):
                    for j in range(2):
                        load_unit(BASE[stage] + 2 * c + j, cols_pair(w, 256 * c, w, D + 256 * c, j))

            load_pairs("pw1", t_in["od_pw1_w"][0])
            load_dense("pw2", t_in["od_pw2_w"][0], D)
            load_ffn(1, (5,))
            load_dense("rg_in", t_in["rg_w_in_2"][0], 2 * D)
            load_dense("rg_out", t_in["rg_w_out_2"][0], D)
            load_dense("kv", t_in["w_kv_2"], 2 * D)
            load_dense("att_in", t_in["att_w_in_2"][0], 2 * D)
            load_dense("att_out", t_in["att_w_out_2"][0], D)
            for t in range(NT):
                sp.wait_ge(sem("result"), t + 1)
                sp.dma_start(out[0, t * P:(t + 1) * P, :], xn[:, t, :]).then_inc(sem("stored"), 16)
            sp.wait_ge(sem("stored"), 16 * NT)

        @block.gpsimd
        def _(pool):
            pool.memset(ones[:, :], 1.0).then_inc(sem("ones"), 1)
            pool.memset(neg_half[:, :], -0.5).then_inc(sem("ones"), 1)
            pool.memset(four_w[:, :, :], 0.0).then_inc(sem("four_zero"), 1)
            pool.wait_ge(sem("ones"), 2)

            def pow_half(stage, n):
                pool.wait_ge(*seen("ms", stage, 1))
                pool.tensor_tensor(rstd[:, 0:n], ms[:, 0:n], neg_half[:, 0:n], ALU.pow).then_inc(sem("rstd"), 1)

            def pow_tiles(stage):
                for t in range(NT):
                    pool.wait_ge(*seen("ms", stage, t + 1))
                    pool.tensor_tensor(rstd[:, t:t + 1], ms[:, t:t + 1], neg_half[:, t:t + 1], ALU.pow).then_inc(sem("rstd"), 1)

            def load_job(q, w, col, units=range(4), i=None):
                for j in units:
                    a = 4 * q + j
                    if a >= N_ALAND:
                        pool.wait_ge(s_step, at(2 * (a - N_ALAND) + 2, i, 8))
                    pool.dma_start(a_land[j % 2][:, :].rearrange("p (k n) -> p k n", k=2),
                                   kview(w)[:, 2 * j:2 * j + 2, bass.ds(col, D)]).then_inc(a_landed[j % 2], 16)

            ada = [t_in["ada_w"][n] for n in range(2)]
            mod = [t_in["mod_w_2"][n] for n in range(2)]

            pow_half("n_x", NT)
            pow_half("n_ctx", NT)
            for q in range(3):
                load_job(q, ada[0], (q + 2) * D, range(2))
                if q == 2:
                    pool.wait_ge(sem("rot"), 16)
                    pool.dma_start(dft[:, :, :], t_in["k_dft"].rearrange("(t p) n -> p t n", p=P)).then_inc(sem("dft_in"), 16)
                load_job(q, ada[0], (q + 2) * D, range(2, 4))
            load_job(3, ada[0], 5 * D, range(2))
            pool.wait_ge(sem("rot"), 16)
            pool.dma_start(mask[:, :], t_in["k_mask"]).then_inc(sem("mask_in"), 16)
            pow_half("sub", 12)
            load_job(3, ada[0], 5 * D, range(2, 4))

            def zero_ffn():
                pool.memset(zeros[:, :], 0.0).then_inc(sem("zeros"), 1)

            pow_tiles("n_ffn0")
            load_job(4, ada[1], 0, range(2))
            zero_ffn()
            with pool.Fori(0, 5) as i:
                load_job(4, ada[1], i * D, range(2, 4), i)
                load_job(5, ada[1], i * D + D, range(2), i)
            load_job(9, ada[1], 5 * D, range(2, 4))
            pow_tiles("n_pw1")
            pool.wait_ge(sem("xres"), 8)
            pool.memset(u_pad[:, :, 0:PAD], 0.0).then_inc(sem("u_zero"), 1)
            pool.memset(u_pad[:, :, PAD + S:UP], 0.0).then_inc(sem("u_zero"), 1)
            pow_half("ln", NT)
            pool.wait_ge(*seen("gate", "pw2b", 2))
            for n in range(2 * NT):
                t, cols = n // 2, slice(512 * (n % 2), 512 * (n % 2) + 512)
                pool.tensor_tensor(x[:, t, cols], x[:, t, cols], bias_gate[:, cols], ALU.add).then_inc(sem("x_bias"), 1)
            load_job(10, mod[0], 0, range(2))
            pow_tiles("n_ffn1")
            zero_ffn()
            with pool.Fori(0, 2) as i:
                load_job(10, mod[0], i * D, range(2, 4), i)
                load_job(11, mod[0], i * D + D, range(2), i)
            load_job(12, mod[0], 2 * D, range(2, 4))
            for q in (13, 14):
                load_job(q, t_in["kv_mod_w_2"], (q - 13) * D)
            load_job(15, mod[1], 0)
            pow_tiles("n_final")
            pow_tiles("n_rg")
            pool.wait_ge(sem("xres"), 16)
            pool.memset(ru_pad[:, :, 0:RG_CONV - 1], 0.0).then_inc(sem("ru_zero"), 1)
            for n, name in enumerate(("rg_w_a_2", "rg_w_x_2")):
                pool.wait_ge(s_step, 8 * 16 - 2 + 2 * n)
                pool.dma_start(rg_w[n][:, :, :, :], t_in[name][0].rearrange("h (k p) j -> p h k j", p=P)).then_inc(sem(f"rg_w{n}"), 16)
            for k in range(KT):
                pool.wait_ge(sem("rg_sig"), rg_sigs(1, k))
                pool.tensor_tensor(i_gate[:, k, :], i_gate[:, k, :], uc[:, k, :], ALU.mult).then_inc(sem("rg_iu"), 1)
            for k in range(0, KT, 2):
                pool.wait_ge(sem("rg_a"), k + 1)
                pool.tensor_tensor(y_full[:, k, :], r_gate[:, k, :], r_gate[:, k, :], ALU.mult).then_inc(sem("rg_a2"), 1)
            pool.wait_ge(sem("rg_gates"), len(RG_GROUPS))
            load_job(16, mod[1], D, range(2))
            pow_tiles("n_kv")
            load_job(16, mod[1], D, range(2, 4))
            load_job(17, mod[1], 2 * D)
            pow_tiles("n_last")

        @block.scalar
        def _(act):
            def split_hi(u, i=None):
                if u >= UNITS:
                    return
                n = u + ADA0
                act.wait_ge(landed[n % N_LAND], at(32 * (n // N_LAND + 1), i, 32))
                if u >= N_SPLIT:
                    act.wait_ge(s_used, at(u - N_SPLIT + 1, i, 6))
                act.activation(w_hi[u % N_SPLIT][:, :], w_land[n % N_LAND][:, :], ACT.Copy).then_inc(s_hi, 1)

            def norm_square(stage, src, junk):
                for t in range(NT):
                    act.activation(junk[:, t, :], src[:, t, :], ACT.Square,
                                   accum_out=ss[:, t:t + 1]).then_inc(sem("ss"), 1)

            def half_squares(stage, residual_steps, ns=range(2 * NT), tiles_first=False):
                for n in ns:
                    t, c = (n // 2, n % 2) if tiles_first else (n % 2, n // 2)
                    act.wait_ge(sem("xres"), residual_steps + n + 1)
                    if n >= 2:
                        act.wait_ge(*seen("ss", stage, n - 1))
                    act.activation(sq_half[:, n % 2, :], x[:, t, 512 * c:512 * c + 512], ACT.Square,
                                   accum_out=ss[:, 2 * t + c:2 * t + c + 1]).then_inc(sem("ss"), 1)

            def full_hi(stage, full, hi, ks=range(KT)):
                for n, k in enumerate(ks):
                    act.wait_ge(*seen("full", stage, n + 1))
                    act.activation(hi[:, k, :], full[:, k, :], ACT.Copy).then_inc(sem("hi"), 1)

            def tile_hi(stage, full, hi, unit, residual_steps=None):
                for n in range(NT * KT):
                    t, k = n // KT, n % KT
                    if n == 4 and residual_steps is not None:
                        half_squares(stage, residual_steps, (3,))
                    if n == KT:
                        split_hi(unit)
                    act.wait_ge(*seen("full", stage, n + 1))
                    act.activation(hi[:, k, t * P:t * P + P], full[:, k, t * P:t * P + P], ACT.Copy).then_inc(sem("hi"), 1)

            def gate_copy(stage, dst=None, b=4):
                dst = gate if dst is None else dst
                act.wait_ge(*seen("gmm", stage, 1))
                for h in range(2):
                    act.activation(dst[:, 512 * h:512 * h + 512], bank[b + h][:, :], ACT.Copy).then_inc(sem("gate"), 1)

            act.wait_ge(sem("cols_in"), 1)
            act.activation(silu_c[:, :, :], pcol[:, COL["c"]:COL["c"] + 24].rearrange("p (c k) -> p c k", c=3),
                           ACT.Silu).then_inc(sem("silu_c"), 1)
            act.wait_ge(sem("x_in"), 16)
            norm_square("n_x", x, xn)
            split_hi(0)
            split_hi(1)
            act.wait_ge(sem("ada0_used"), ADA0)
            for n in range(4):
                act.activation(ada_rows[:, 512 * n:512 * n + 512], bank[n][0:2, :], ACT.Copy).then_inc(sem("ada0_rows"), 1)
            act.wait_ge(sem("lam_dot"), 2)
            act.activation(lam_tmp[:, 2:4], lam_tmp[:, 0:2], ACT.Exp).then_inc(sem("lam_exp"), 1)
            act.wait_ge(sem("sp_abs"), 1)
            act.activation(sp_c[:, 1, :], sp_c[:, 0, :], ACT.Exp, scale=-1.0).then_inc(sem("sp_exp"), 1)
            full_hi("n_x", xfull, xT_hi)

            turned = [0]

            def turn_copy(dst, h0, nh, tok):
                n = turned[0]
                turned[0] += 1
                act.wait_ge(sem("turn"), n + 1)
                act.activation(dst[:, h0:h0 + nh, tok:tok + P],
                               bank[(4, 6)[n % 2]][:, 0:nh * P].rearrange("p (h s) -> p h s", h=nh),
                               ACT.Copy).then_inc(sem("turn_out"), 1)

            def turns(c):
                if c in (0, 1):
                    for t in range(NT):
                        turn_copy(qT, 4 * c, 4 - 2 * c, t * P)
                if c in (2, 3):
                    for src in range(2):
                        for t in range(NT):
                            turn_copy(kT, 4 * (c - 2), 4 - 2 * (c - 2), (S if src == 0 else 0) + t * P)

            for c in range(5):
                split_hi(2 * c + 2)
                if c == 0:
                    act.wait_ge(sem("ctx_in"), 16)
                    act.wait_ge(*seen("rstd", "n_x", 1))
                    norm_square("n_ctx", ctx_x, ctx_junk)
                if c == 1:
                    act.wait_ge(sem("four_gmm"), 1)
                    act.activation(four_g[:, :, :, :].rearrange("p c f n -> p (c f n)"), bank[2][:, :], ACT.Copy).then_inc(sem("four_gs"), 1)
                    full_hi("n_ctx", ctx_full, ctxT_hi)
                if c < 2:
                    split_hi(2 * c + 3)
                if c == 1:
                    act.wait_ge(*seen("lo", "n_ctx", KT))
                if c >= 1:
                    turns(c - 1)
                if c >= 2:
                    split_hi(2 * c + 3)
                if c == 2:
                    act.wait_ge(s_used, 6)
                    for t in range(NT):
                        act.activation(k_ctx[:, t, :], bank[2 + t][:, :], ACT.Copy).then_inc(sem("in_act"), 1)
                if c == 3:
                    act.wait_ge(s_used, 8)
                    act.wait_ge(sem("turn"), 8)
                    for t in range(NT):
                        act.activation(k_ctx[:, t, 0:256], bank[2 + t][:, 0:256], ACT.Copy).then_inc(sem("in_act"), 1)
                        act.activation(v_tok[:, t, 0:256], bank[2 + t][:, 256:512], ACT.Copy).then_inc(sem("in_act"), 1)
                if c == 4:
                    for src, tile in ((0, NT), (1, 0)):
                        act.wait_ge(*((sem("in_lat"), 3) if src == 0 else (s_used, 10)))
                        for t in range(NT):
                            act.activation(v_tok[:, tile + t, 256:768], bank[2 * src + t][:, :], ACT.Copy).then_inc(sem("in_act"), 1)

            for f in range(2):
                act.wait_ge(sem("four_ft"), f + 1)
                act.activation(ftT[:, f, :], bank[4 + f][:, :], ACT.Copy).then_inc(sem("four_fts"), 1)
            ITS = [(h, t) for h in range(HEADS) for t in range(NT)]

            def exps(n):
                for c in range(2):
                    act.wait_ge(sem("d_nb"), n + 1)
                    if n >= 2:
                        act.wait_ge(sem("d_diff"), n - 1)
                    act.activation(prob[:, n % 2, c, :], bank[2 * (n % 2) + c][:, :], ACT.Exp, scale=0.125,
                                   bias=nb[:, n % 2, c:c + 1], accum_out=esum[:, n % 2, c:c + 1]).then_inc(sem("d_exp"), 1)

            def head_out(n):
                h, t = ITS[n]
                act.wait_ge(sem("d_pv"), n + 1)
                act.activation(o_tok[:, t, h * P:h * P + P], bank[6 + n % 2][:, 0:P], ACT.Copy,
                               scale=rsum[:, n % 2, 0:1]).then_inc(sem("d_o"), 1)

            exps(0)
            act.wait_ge(sem("four_y"), 1)
            for f in range(2):
                act.activation(xT_hi[:, HEADS + f, :], bank[6][:, 256 * f:256 * f + 256], ACT.Copy).then_inc(sem("four_hi"), 1)

            for n in range(len(ITS)):
                if n + 1 < len(ITS):
                    exps(n + 1)
                act.wait_ge(sem("d_turn"), n + 1)
                if n >= 2:
                    act.wait_ge(sem("d_pv"), n - 1)
                act.activation(diffT[:, n % 2, :, :].rearrange("p k s -> p (k s)"), bank[4 + n % 2][:, :], ACT.Copy).then_inc(sem("d_diffT"), 1)
                if n >= 1:
                    head_out(n - 1)
            head_out(len(ITS) - 1)
            full_hi("sub", o_full, xT_hi, range(HEADS))

            def dense_out(stage, after, residual_steps):
                split_hi(BASE[stage] + 2)
                split_hi(BASE[stage] + 3)
                gate_copy(stage)
                if stage == "pw2":
                    gate_copy("pw2b", bias_gate, 6)
                if stage == "att_out":
                    gate_copy("last", last_gate, 6)
                split_hi(BASE[stage] + 4)
                half_squares(after, residual_steps, (0, 1, 2))
                split_hi(BASE[stage] + 5)
                if stage == "att_out":
                    half_squares(after, residual_steps, (3,))

            dense_out("out", "n_ffn0", 0)

            def ffn(layer, loops):
                base = BASE[f"ffn{layer}"]
                off = layer * FCH
                tile_hi(f"n_ffn{layer}", xfull, xT_hi, base + 2, 8 * layer)

                def silu(c, u, i=None):
                    act.wait_ge(s_used, at(u + 2, i, 6))
                    for t in range(NT):
                        act.activation(silu_g[:, t, :], bank[t][:, 0:256], ACT.Silu).then_inc(sem("silu_g"), 1)

                def hidden_hi(c, i=None):
                    act.wait_ge(sem("h_turn"), at(off + c + 1, i, 2))
                    act.activation(hT_hi[:, :, :].rearrange("p k s -> p (k s)"), bank[6][:, :], ACT.Copy).then_inc(sem("hT_hi"), 1)

                silu(0, base)
                split_hi(base + 3)
                hidden_hi(0)
                done = 0
                for n in loops:
                    with act.Fori(0, n) as i:
                        for b in range(2):
                            u = base + 2 + 6 * done + 3 * b
                            c = 1 + 2 * done + b
                            split_hi(u + 2, i)
                            split_hi(u + 3, i)
                            silu(c, u, i)
                            split_hi(u + 4, i)
                            hidden_hi(c, i)
                    done += n
                split_hi(base + 3 * FCH + 1)
                gate_copy(f"ffn{layer}", b=0)
                after, steps = ("n_pw1", "n_final")[layer], 4 + 8 * layer
                half_squares(after, steps, (0, 1), tiles_first=True)
                if layer == 1:
                    gate_copy("final", bias_gate, 0)
                half_squares(after, steps, (2, 3)[:1 + layer], tiles_first=True)

            ffn(0, (5,))

            def rows_out(stage, dst, chunks):
                for c in chunks:
                    if c > 0:
                        split_hi(BASE[stage] + 2 * c + 2)
                    split_hi(BASE[stage] + 2 * c + 3)
                    act.wait_ge(s_used, BASE[stage] + 2 * c + 2)
                    if c >= 1:
                        act.wait_ge(sem(f"{stage}_turn"), c)
                    for t in range(NT):
                        act.activation(dst[:, t, :], bank[2 * (c % 2) + t][:, :], ACT.Copy).then_inc(sem(f"{stage}_tok"), 1)
                    yield c

            tile_hi("n_pw1", xfull, xT_hi, BASE["pw1"] + 2, 4)
            for c in rows_out("pw1", ag_tok, range(4)):
                act.wait_ge(sem("pw1_turn"), c + 1)
                if c >= 1:
                    act.wait_ge(sem("pw1_glu"), 2 * c)
                for e in range(2):
                    act.activation(sig[:, e, :], bank[5][:, 256 * e:256 * e + 256], ACT.Sigmoid,
                                   bias=pc("od_pw1_b", KT + 2 * c + e)).then_inc(sem("pw1_sig"), 1)
                if c >= 1:
                    act.wait_ge(sem("conv_pe"), c)
                for e in range(2):
                    for n in range(PE_TAPS):
                        w = COL["od_dw_w_a"] + (CONV - PE_TAPS + n) * KT + 2 * c + e
                        act.activation(tap_diag[e][:, n, :], ident[:, :], ACT.Copy, scale=pcol[:, w:w + 1]).then_inc(sem("tap_diag"), 1)
            for k in range(KT):
                act.wait_ge(sem("ln_xc"), k + 1)
                act.activation(csq[:, k, :], conv[:, k, :], ACT.Square).then_inc(sem("ln_sq"), 1)
            for k in range(KT):
                act.wait_ge(sem("ln_norm"), k + 1)
                act.activation(xfull[:, k, :], csq[:, k, :], ACT.Silu, scale=pc("od_ln_g", k),
                               bias=pc("od_ln_b", k)).then_inc(sem("full"), 1)
                act.wait_ge(*seen("full", "ln", k + 1))
                act.activation(xT_hi[:, k, :], xfull[:, k, :], ACT.Copy).then_inc(sem("hi"), 1)
            dense_out("pw2", "n_ffn1", 8)
            ffn(1, (3, 2))

            act.wait_ge(*seen("ss", "n_final", 2 * NT))
            for t in range(NT):
                act.wait_ge(sem("x_final"), t + 1)
                if t == 1:
                    act.wait_ge(*seen("ss", "n_rg", 1))
                act.activation(sq_half[:, :, :].rearrange("p c n -> p (c n)"), x[:, t, :], ACT.Square,
                               accum_out=ss[:, t:t + 1]).then_inc(sem("ss"), 1)
            tile_hi("n_rg", xfull, xT_hi, BASE["rg_in"] + 2)
            base = BASE["rg_in"]

            def rg_rows(c):
                act.wait_ge(s_used, base + 2 * c + 2)
                if c >= 1:
                    act.wait_ge(sem("rg_in_turn"), c)
                for t in range(NT):
                    act.activation(rg_tok[:, t, :], bank[2 * (c % 2) + t][:, :], ACT.Copy).then_inc(sem("rg_in_tok"), 1)

            def rg_turned(c, func=ACT.Copy):
                act.wait_ge(sem("rg_in_turn"), c + 1)
                for g in range(2):
                    k = 4 * (c % 2) + 2 * g
                    dst = ru_pad[:, k:k + 2, RG_CONV - 1:RUP] if c < 2 else gT[:, k:k + 2, :]
                    act.activation(dst, bank[4 + g][:, :].rearrange("p (k s) -> p k s", k=2), func).then_inc(sem("rg_turned"), 1)

            def rg_sigmoids(g):
                n, h = RG_GROUPS[g]
                act.wait_ge(sem("rg_gates"), g + 1)
                for e in range(2):
                    k = 2 * h + e
                    dst, b = ((r_gate, "rg_b_a_2"), (i_gate, "rg_b_x_2"))[n]
                    act.activation(dst[:, k, :], bank[6 + g % 2][:, 256 * e:256 * e + 256], ACT.Sigmoid,
                                   bias=pc(b, k)).then_inc(sem("rg_sig"), 1)
                if n == 0:
                    act.wait_ge(sem("rg_conv"), RG_CONV * 4 * (h // 2 + 1))
                    for k in (2 * h, 2 * h + 1):
                        act.wait_ge(sem("rg_sig"), rg_sigs(0, k))
                        act.activation(b_seq[:, k, :], r_gate[:, k, :], ACT.Tanh, scale=sp_c[:, 7, k:k + 1]).then_inc(sem("rg_th"), 1)

            split_hi(base + 3)
            rg_rows(0)
            act.wait_ge(sem("ru_zero"), 1)
            rg_turned(0)
            split_hi(base + 4)
            split_hi(base + 5)
            rg_rows(1)
            rg_turned(1)
            split_hi(base + 6)
            act.wait_ge(sem("sp_done"), 1)
            rg_sigmoids(0)
            rg_sigmoids(1)
            split_hi(base + 7)
            for g in range(2, 6):
                rg_sigmoids(g)
            rg_rows(2)
            rg_sigmoids(6)
            rg_sigmoids(7)
            rg_turned(2)
            for k in range(KT):
                act.wait_ge(sem("rg_th"), k + 1)
                act.activation(r_gate[:, k, :], r_gate[:, k, :], ACT.Exp, scale=sp_c[:, 7, k:k + 1]).then_inc(sem("rg_a"), 1)
            split_hi(base + 8)
            for k in range(KT):
                act.wait_ge(sem("rg_m"), k + 1)
                act.activation(b_seq[:, k, :], b_seq[:, k, :], ACT.Sqrt, scale=-1.0).then_inc(sem("rg_sqrt"), 1)
            rg_rows(3)
            act.wait_ge(sem("rg_turned"), 6)
            for k in range(0, 4, 2):
                act.activation(gT[:, k:k + 2, :], gT[:, k:k + 2, :], ACT.Silu).then_inc(sem("rg_g"), 1)
            rg_turned(3, ACT.Silu)
            split_hi(base + 9)
            full_hi("rg", y_full, xT_hi)
            dense_out("rg_out", "n_kv", 16)

            tile_hi("n_kv", kv_full, xT_hi, BASE["kv"] + 2, 16)

            def copies(stage, c, dst):
                if c > 0 or stage == "att_in":
                    split_hi(BASE[stage] + 2 * c + 2)
                split_hi(BASE[stage] + 2 * c + 3)
                act.wait_ge(s_used, BASE[stage] + 2 * c + 2)
                for t in range(NT):
                    if c < 2:
                        if c == 1:
                            act.wait_ge(sem(f"{stage}_turn"), t + 1)
                        act.activation(a_tok[:, t, :], bank[2 * (c % 2) + t][:, :], ACT.Copy).then_inc(sem(f"{stage}_tok"), 1)
                    else:
                        func = ACT.Copy if stage == "kv" else ACT.Silu
                        act.activation(dst[:, t, 512 * (c - 2):512 * (c - 2) + 512], bank[2 * (c % 2) + t][:, :],
                                       func).then_inc(sem(f"{stage}_rows"), 1)

            for stage, dst, turned_dst in (("kv", av, akT), ("att_in", ag, aqT)):
                if stage == "att_in":
                    full_hi("n_att", kv_full, xT_hi)
                for c in range(4 if stage == "kv" else 2):
                    copies(stage, c, dst)
                    if c < 2:
                        for t in range(NT):
                            n = 2 * c + t
                            act.wait_ge(sem(f"{stage}_turn"), n + 1)
                            act.activation(turned_dst[:, 4 * c:4 * c + 4, t * P:t * P + P],
                                           bank[4 + n % 2][:, :].rearrange("p (h s) -> p h s", h=4),
                                           ACT.Copy).then_inc(sem(f"{stage}_turned"), 1)

            A_ITS = [(h, t) for h in range(A_HEADS) for t in range(NT)]
            base = BASE["att_in"]

            def a_exp(n):
                h, t = A_ITS[n]
                keys = (t + 1) * P
                act.wait_ge(sem("a_nb"), n + 1)
                if n >= 2:
                    act.wait_ge(sem("a_turn"), n - 1)
                act.activation(ap_[:, n % 2, 0:keys], bank[2 + n % 2][:, 0:keys], ACT.Exp, scale=float(P) ** -0.5,
                               bias=nb[:, n % 2, 0:1], accum_out=esum[:, n % 2, 0:1]).then_inc(sem("a_exp"), 1)

            def gate_rows(c):
                act.wait_ge(s_used, base + 2 * c + 2)
                for t in range(NT):
                    act.activation(ag[:, t, 512 * (c - 2):512 * (c - 2) + 512], bank[t][:, :], ACT.Copy).then_inc(sem("att_in_rows"), 1)

            split_hi(base + 6)
            a_exp(0)
            for n, (h, t) in enumerate(A_ITS):
                if n + 1 < len(A_ITS):
                    a_exp(n + 1)
                act.wait_ge(sem("a_turn"), n + 1)
                if n >= 2:
                    act.wait_ge(sem("a_pv"), n - 1)
                act.activation(apT[:, n % 2, 0:t + 1, :].rearrange("p k s -> p (k s)"),
                               bank[4 + n % 2][:, 0:(t + 1) * P], ACT.Copy).then_inc(sem("a_apT"), 1)
                if n == 2:
                    split_hi(base + 7)
                if n == 4:
                    gate_rows(2)
                if n == 6:
                    split_hi(base + 8)
                if n == 10:
                    split_hi(base + 9)
                if n == 13:
                    gate_rows(3)
            act.wait_ge(sem("att_in_rows"), 4)
            for c in range(2):
                for t in range(NT):
                    part = ag[:, t, 512 * c:512 * c + 512]
                    act.activation(part, part, ACT.Silu).then_inc(sem("ag_silu"), 1)
            for k in range(KT):
                act.wait_ge(*seen("tr", "ao", 4 * (k // 2) + 4))
                act.activation(xT_hi[:, k, :], bank[4 + k // 2][:, 256 * (k % 2):256 * (k % 2) + 256], ACT.Copy).then_inc(sem("hi"), 1)
                act.wait_ge(*seen("lo", "ao", k + 1))
            dense_out("att_out", "n_last", 20)

        @block.vector
        def _(dve):
            count = [0]

            def link(ins):
                count[0] += 1
                ins.then_inc(sem("dve_chain"), 1)
                dve.wait_ge(sem("dve_chain"), count[0])

            def split_lo(u, i=None):
                if u >= UNITS:
                    return
                n = u + ADA0
                dve.wait_ge(s_hi, at(u + 1, i, 6))
                dve.tensor_tensor(w_lo[u % N_SPLIT][:, :], w_land[n % N_LAND][:, :],
                                  w_hi[u % N_SPLIT][:, :].bitcast(F32), ALU.subtract).then_inc(s_lo, 1)

            def job_units(q, units, i=None):
                c = 0 if JOBS[q] < V_MOD0 else 2
                for j in units:
                    dve.wait_ge(a_landed[j % 2], at(16 * (2 * q + j // 2 + 1), i, 32))
                    for e in range(2):
                        n = 2 * j + e
                        w = a_land[j % 2][:, e * D:e * D + D]
                        if n == 0:
                            if q >= 1:
                                dve.wait_ge(s_red, at(q, i, 1))
                            ins = dve.tensor_scalar(job_sum[:, :], w, silu_c[:, c, n:n + 1], None, ALU.mult)
                        else:
                            dve.wait_ge(s_step, at(8 * q + n, i, 8))
                            ins = dve.scalar_tensor_tensor(out=job_sum[:, :], in0=w, scalar=silu_c[:, c, n:n + 1],
                                                           in1=job_sum[:, :], op0=ALU.mult, op1=ALU.add)
                        ins.then_inc(s_step, 1)

            def job_cols(q, i=None):
                v = JOBS[q]
                dve.wait_ge(s_red, at(q + 1, i, 1))
                if i is None:
                    dst, bias = mcol[:, v * KT:v * KT + KT], pcol[:, v * KT + (32 if v >= V_MOD0 else 0):][:, 0:KT]
                else:
                    dst = mcol[:, bass.ds(i * KT + v * KT, KT)]
                    bias = pcol[:, bass.ds(i * KT + (v * KT + (32 if v >= V_MOD0 else 0)), KT)]
                dve.tensor_tensor(dst, COLS[:, 0:KT], bias, ALU.add).then_inc(s_cols, 1)

            def norm_stats(stage, src, dst, n=NT, width=D):
                dve.wait_ge(*seen("ss", stage, n))
                dve.tensor_scalar(ms[:, 0:n], ss[:, 0:n], 1.0 / width, EPS, ALU.mult, ALU.add).then_inc(sem("ms"), 1)
                dve.wait_ge(*seen("rstd", stage, 1))
                if dst is not None:
                    for t in range(NT):
                        dve.tensor_scalar(dst[:, t, :], src[:, t, :], rstd[:, t:t + 1], None, ALU.mult).then_inc(sem("xn"), 1)

            def mod_cols(g, v_scale):
                link(dve.scalar_tensor_tensor(out=a_col[:, :], in0=mc(v_scale), scalar=1.0, in1=g, op0=ALU.add, op1=ALU.mult))

            def full_lo(stage, full, hi, lo, banks, a, b, ks=range(KT), turns=2 * KT, whole=False):
                if whole:
                    dve.wait_ge(*seen("tr", stage, turns))

                def low(n):
                    dve.wait_ge(*seen("hi", stage, n + 1))
                    dve.tensor_tensor(lo[:, ks[n], :], full[:, ks[n], :], hi[:, ks[n], :].bitcast(F32),
                                      ALU.subtract).then_inc(sem("lo"), 1)

                for n, k in enumerate(ks):
                    if not whole and k % 2 == 0:
                        dve.wait_ge(*seen("tr", stage, 2 * k + 4))
                    src = banks[k // 2][:, 256 * (k % 2):256 * (k % 2) + 256]
                    if b is None:
                        ins = dve.tensor_scalar(full[:, k, :], src, a(k), None, ALU.mult)
                    else:
                        ins = dve.tensor_scalar(full[:, k, :], src, a(k), b(k), ALU.mult, ALU.add)
                    ins.then_inc(sem("full"), 1)
                    if n >= 1:
                        low(n - 1)
                low(len(ks) - 1)

            def gate_diag(stage, col, dst=None):
                g = (gate if dst is None else dst)[:, :].rearrange("p (k f) -> p k f", k=KT)
                dve.tensor_tensor(g, ident[:, :].unsqueeze(1).broadcast_to([P, KT, P]),
                                  col.unsqueeze(2).broadcast_to([P, KT, P]), ALU.mult).then_inc(sem("diag"), 1)

            parts_done = [0]

            def residual(c, t, b, wait):
                cols = slice(512 * c, 512 * c + 512)
                part = tmp[:, parts_done[0] % 2, :]
                parts_done[0] += 1
                dve.wait_ge(*wait)
                link(dve.tensor_tensor(part, bank[b][:, :], gate[:, cols], ALU.mult))
                dve.tensor_tensor(x[:, t, cols], x[:, t, cols], part, ALU.add).then_inc(sem("xres"), 1)

            def tile_mean(stage, t, squares):
                dve.wait_ge(*seen("ss", stage, squares))
                mean_sq = ms[:, t:t + 1]
                if stage == "n_rg":
                    dve.tensor_scalar(mean_sq, ss[:, t:t + 1], 1.0 / D, EPS, ALU.mult, ALU.add).then_inc(sem("ms"), 1)
                else:
                    link(dve.tensor_tensor(mean_sq, ss[:, 2 * t:2 * t + 1], ss[:, 2 * t + 1:2 * t + 2], ALU.add))
                    dve.tensor_scalar(mean_sq, mean_sq, 1.0 / D, EPS, ALU.mult, ALU.add).then_inc(sem("ms"), 1)

            def tile_normed(stage, t):
                dve.wait_ge(*seen("rstd", stage, t + 1))
                dve.tensor_scalar(xn[:, t, :], x[:, t, :], rstd[:, t:t + 1], None, ALU.mult).then_inc(sem("xn"), 1)

            def tile_operand(stage, full, hi, lo, shift, banks, between, unit, squares=2 * NT):
                def low(n):
                    t, k = n // KT, n % KT
                    cols = slice(t * P, t * P + P)
                    dve.wait_ge(*seen("hi", stage, n + 1))
                    dve.tensor_tensor(lo[:, k, cols], full[:, k, cols], hi[:, k, cols].bitcast(F32),
                                      ALU.subtract).then_inc(sem("lo"), 1)

                for n in range(NT * KT):
                    t, k = n // KT, n % KT
                    if n == 4:
                        for step in between:
                            residual(*step)
                    if n == 6:
                        tile_mean(stage, 1, squares)
                    if n == KT:
                        low(n - 1)
                        tile_normed(stage, 1)
                        split_lo(unit)
                    if n % 4 == 0:
                        dve.wait_ge(*seen("tr", stage, n + 4))
                    dve.tensor_scalar(full[:, k, t * P:t * P + P], bank[banks[t][k // 4]][:, P * (k % 4):P * (k % 4) + P],
                                      a_col[:, k:k + 1], mc(shift, k, 1), ALU.mult, ALU.add).then_inc(sem("full"), 1)
                    if k >= 1:
                        low(n - 1)
                low(NT * KT - 1)

            for g in range(5):
                dve.wait_ge(sem("prow_tr"), g + 1)
                n = sum(k for _, k in ROW_GROUPS[g])
                dve.tensor_copy(pcol[:, g * P:g * P + n], bank[4 + g % 4][:, 0:n]).then_inc(sem("cols_in"), 1)
                if g == 0:
                    norm_stats("n_x", x, xn)
            split_lo(0)
            split_lo(1)
            dve.wait_ge(sem("lam_in"), 64)
            dve.wait_ge(sem("cols_in"), 5)
            for n in range(2):
                dve.tensor_tensor_reduce(lam_junk[:, n, :], lam_in[:, 2 * n, :], lam_in[:, 2 * n + 1, :], 1.0, 0.0,
                                         ALU.mult, ALU.add, lam_tmp[:, n:n + 1]).then_inc(sem("lam_dot"), 1)
            lam = pc("rg_lambda_2", 0, KT)
            link(dve.tensor_scalar(sp_c[:, 2, :], lam, -1.0, 0.0, ALU.mult, ALU.max))
            dve.scalar_tensor_tensor(out=sp_c[:, 0, :], in0=sp_c[:, 2, :], scalar=2.0, in1=lam,
                                     op0=ALU.mult, op1=ALU.add).then_inc(sem("sp_abs"), 1)
            dve.wait_ge(sem("lam_exp"), 1)
            link(dve.tensor_tensor(lam_tmp[:, 4:5], lam_tmp[:, 3:4], lam_tmp[:, 2:3], ALU.subtract))
            link(dve.tensor_scalar(lam_tmp[:, 5:6], lam_tmp[:, 4:5], -(1.0 - SUB_SCALE), None, ALU.add))

            dve.wait_ge(sem("ada0_tr"), 16)
            turned = bank[0][:, 0:32].rearrange("p (v c) -> p v c", c=2)
            dve.tensor_tensor(mcol[:, 0:2 * KT], turned[:, :, 0], pcol[:, 0:2 * KT], ALU.add).then_inc(sem("ada0_cols"), 1)
            dve.tensor_tensor(mcol_ctx[:, :], turned[:, :, 1], pcol[:, 0:2 * KT], ALU.add).then_inc(sem("ada0_cols"), 1)
            dve.wait_ge(sem("ada0_cols"), 2)
            mod_cols(pc("mix_norm_g", 0, KT), 1)
            link(dve.scalar_tensor_tensor(out=b_col[:, :], in0=mcol_ctx[:, KT:2 * KT], scalar=1.0,
                                          in1=pc("mix_norm_g", 0, KT), op0=ALU.add, op1=ALU.mult))
            full_lo("n_x", xfull, xT_hi, xT_lo, bank[4:8], lambda k: a_col[:, k:k + 1], lambda k: mc(0, k, 1))

            def softplus_lambda():
                dve.wait_ge(sem("sp_exp"), 1)
                link(dve.tensor_scalar(sp_c[:, 3, :], sp_c[:, 1, :], 2.0, None, ALU.add))
                link(dve.reciprocal(sp_c[:, 4, :], sp_c[:, 3, :]))
                link(dve.tensor_tensor(sp_c[:, 3, :], sp_c[:, 1, :], sp_c[:, 4, :], ALU.mult))
                link(dve.tensor_tensor(sp_c[:, 4, :], sp_c[:, 3, :], sp_c[:, 3, :], ALU.mult))
                link(dve.tensor_scalar(sp_c[:, 5, :], sp_c[:, 4, :], 1.0 / 17, 1.0 / 15, ALU.mult, ALU.add))
                for n in range(13, 0, -2):
                    link(dve.tensor_tensor(sp_c[:, 5, :], sp_c[:, 5, :], sp_c[:, 4, :], ALU.mult))
                    link(dve.tensor_scalar(sp_c[:, 5, :], sp_c[:, 5, :], 1.0 / n, None, ALU.add))
                link(dve.tensor_tensor(sp_c[:, 5, :], sp_c[:, 5, :], sp_c[:, 3, :], ALU.mult))
                link(dve.scalar_tensor_tensor(out=sp_c[:, 5, :], in0=sp_c[:, 5, :], scalar=2.0, in1=sp_c[:, 2, :],
                                              op0=ALU.mult, op1=ALU.add))
                dve.tensor_scalar(sp_c[:, 7, :], sp_c[:, 5, :], -RG_C, None, ALU.mult).then_inc(sem("sp_done"), 1)

            ITS = [(h, t) for h in range(HEADS) for t in range(NT)]

            def row_max(n):
                b = n % 2
                if n >= 2:
                    dve.wait_ge(sem("d_exp"), 2 * (n - 1))
                for c in range(2):
                    dve.wait_ge(sem("d_s"), 2 * n + c + 1)
                    dve.reduce_max(mx[:, b, c:c + 1], bank[2 * b + c][:, :], AX_X).then_inc(sem("d_mx"), 1)
                dve.wait_ge(sem("d_mx"), 2 * n + 2)
                dve.tensor_scalar(nb[:, b, :], mx[:, b, :], -0.125, None, ALU.mult).then_inc(sem("d_nb"), 1)

            dve.wait_ge(sem("rope_in"), 16)

            def rotate(src, t, n):
                m = n // 64
                v = src[:, 0:n].rearrange("p (m h d) -> p m h d", m=m, h=2)
                c4 = rope_cos[:, 0:n].rearrange("p (m h d) -> p m h d", m=m, h=2)
                s4 = rope_sin[:, 0:n].rearrange("p (m h d) -> p m h d", m=m, h=2)
                v2 = src[:, 0:n].rearrange("p (m d) -> p m d", d=32)
                o4 = rot[:, t, 0:n].rearrange("p (m h d) -> p m h d", m=m, h=2)
                for dst, which in ((rope_cos, 0), (rope_sin, 1)):
                    ins = dve.tensor_tensor(dst[:, 0:n].rearrange("p (m d) -> p m d", d=32), v2,
                                            rope[:, t, which, :].unsqueeze(1).broadcast_to([P, 2 * m, 32]), ALU.mult)
                    link(ins)
                dve.tensor_tensor(o4[:, :, 0, :], c4[:, :, 0, :], s4[:, :, 1, :], ALU.subtract).then_inc(sem("rot"), 1)
                dve.tensor_tensor(o4[:, :, 1, :], s4[:, :, 0, :], c4[:, :, 1, :], ALU.add).then_inc(sem("rot"), 1)

            plan = [((s_used, 2), 0, 512, 0), ((s_used, 4), 2, 256, 2), ((sem("in_lat"), 1), 0, 512, 4),
                    ((sem("in_lat"), 2), 0, 256, 8)]
            def take(c):
                event, b, n, free = plan[c]
                dve.wait_ge(*event)
                if free:
                    dve.wait_ge(sem("turn"), free)
                for t in range(NT):
                    if c or t:
                        dve.wait_ge(sem("rot"), 4 * c + 2 * t)
                    rotate(bank[b + t], t, n)
                    if c == 1:
                        dve.tensor_copy(f_tok[:, t, :], bank[b + t][:, 256:512]).then_inc(sem("f_tok"), 1)
                    if c == 3:
                        dve.tensor_copy(v_tok[:, NT + t, 0:256], bank[b + t][:, 256:512]).then_inc(sem("v_lat"), 1)

            split_lo(2)
            norm_stats("n_ctx", ctx_x, ctx_x)
            split_lo(3)
            take(0)
            split_lo(4)
            full_lo("n_ctx", ctx_full, ctxT_hi, ctxT_lo, bank[4:8], lambda k: b_col[:, k:k + 1],
                    lambda k: mcol_ctx[:, k:k + 1], whole=True)
            split_lo(5)
            take(1)
            job_units(0, range(1))
            split_lo(6)
            take(2)
            job_units(0, (1,))
            split_lo(7)
            job_units(0, (2,))
            split_lo(8)
            job_units(0, (3,))
            take(3)
            job_cols(0)
            job_units(1, (0,))
            softplus_lambda()
            split_lo(9)
            job_units(1, (1,))
            split_lo(10)
            job_units(1, (2, 3))
            job_cols(1)
            job_units(2, (0,))
            split_lo(11)
            job_units(2, range(1, 4))
            row_max(0)
            for f in range(2):
                dve.wait_ge(sem("four_hi"), 2)
                dve.tensor_tensor(xT_lo[:, HEADS + f, :], bank[6][:, 256 * f:256 * f + 256],
                                  xT_hi[:, HEADS + f, :].bitcast(F32), ALU.subtract).then_inc(sem("four_lo"), 1)

            job_cols(2)

            def head_square(n):
                h, t = ITS[n]
                dve.wait_ge(sem("d_o"), n + 1)
                o = o_tok[:, t, h * P:h * P + P]
                if n >= 2:
                    dve.wait_ge(*seen("ss", "sub", n - 1))
                dve.tensor_tensor_reduce(sq_junk[:, n % 2, :], o, o, 1.0, 0.0, ALU.mult, ALU.add,
                                         ss[:, t * HEADS + h:t * HEADS + h + 1]).then_inc(sem("ss"), 1)

            for n, (h, t) in enumerate(ITS):
                b = n % 2
                if n + 1 < len(ITS):
                    row_max(n + 1)
                dve.wait_ge(sem("d_exp"), 2 * n + 2)
                if n >= 2:
                    dve.wait_ge(sem("d_o"), n - 1)
                link(dve.reciprocal(rsum[:, b, :], esum[:, b, :]))
                link(dve.tensor_scalar(rsum[:, b, 1:2], rsum[:, b, 1:2], esum[:, b, 0:1], lam_tmp[:, 5:6], ALU.mult, ALU.mult))
                if n >= 2:
                    dve.wait_ge(sem("d_turn"), n - 1)
                dve.scalar_tensor_tensor(out=diff[:, b, :], in0=prob[:, b, 1, :], scalar=rsum[:, b, 1:2],
                                         in1=prob[:, b, 0, :], op0=ALU.mult, op1=ALU.add).then_inc(sem("d_diff"), 1)
                if n >= 2:
                    head_square(n - 2)
            for n in (len(ITS) - 2, len(ITS) - 1):
                head_square(n)
            norm_stats("sub", None, None, 12, P)
            for t in range(NT):
                o = o_tok[:, t, :].rearrange("p (h e) -> p h e", h=HEADS)
                dve.tensor_tensor(o, o, rstd[:, t * HEADS:t * HEADS + HEADS].unsqueeze(2).broadcast_to([P, HEADS, P]),
                                  ALU.mult).then_inc(sem("xn"), 1)
            link(dve.tensor_scalar(a_col[:, 0:1], pc("ev_subln_g"), SUB_SCALE, None, ALU.mult))
            full_lo("sub", o_full, xT_hi, xT_lo, bank[2:5], lambda k: a_col[:, 0:1], None, range(HEADS), 12)
            gate_diag("out", mc(2))

            def dense_residual(stage, after):
                split_lo(BASE[stage] + 2)
                split_lo(BASE[stage] + 3)
                if stage == "out":
                    job_units(3, (0, 1))
                if stage == "pw2":
                    job_units(9, (2, 3))
                dve.wait_ge(*seen("gate", stage, 2))
                if stage == "pw2":
                    dve.wait_ge(sem("x_bias"), 2 * NT)
                residual(0, 0, 0, seen("part", stage, 1))
                residual(0, 1, 1, (s_used, BASE[stage] + 2))
                split_lo(BASE[stage] + 4)
                if stage == "out":
                    job_units(3, (2,))
                residual(1, 0, 2, seen("part", stage, 2))
                tile_mean(after, 0, 3)
                tile_normed(after, 0)
                split_lo(BASE[stage] + 5)
                return [(1, 1, 3, (s_used, BASE[stage] + 4))]

            mod_cols(pc("ffn_norm_g", 0, KT), 4)
            left = dense_residual("out", "n_ffn0")

            def ffn(layer, loops, first_job, left):
                base = BASE[f"ffn{layer}"]
                off = layer * FCH
                tile_operand(f"n_ffn{layer}", xfull, xT_hi, xT_lo, 6 * layer + 3, AFTER_DENSE, left, base + 2)

                def hidden(c, i=None):
                    for t in range(NT):
                        dve.wait_ge(sem("silu_g"), at(2 * (off + c) + t + 1, i, 4))
                        dve.tensor_tensor(hid[:, t, :], silu_g[:, t, :], bank[t][:, 256:512], ALU.mult).then_inc(sem("hid"), 1)

                def hidden_lo(c, i=None):
                    dve.wait_ge(sem("hT_hi"), at(off + c + 1, i, 2))
                    dve.tensor_tensor(hT_lo[:, :, :].rearrange("p k s -> p (k s)"), bank[6][:, :],
                                      hT_hi[:, :, :].rearrange("p k s -> p (k s)").bitcast(F32),
                                      ALU.subtract).then_inc(sem("hT_lo"), 1)

                if layer == 0:
                    job_units(3, (3,))
                hidden(0)
                job_cols(first_job - 1)
                split_lo(base + 3)
                hidden_lo(0)
                dve.wait_ge(s_cols, first_job)
                gate_diag(f"ffn{layer}", mc(6 * layer + 5))
                if layer == 1:
                    gate_diag("final", pc("final_g", 0, KT), bias_gate)
                job_units(first_job, range(2))
                done = 0
                for q, n in loops:
                    with dve.Fori(0, n) as i:
                        for b in range(2):
                            u = base + 2 + 6 * done + 3 * b
                            c = 1 + 2 * done + b
                            split_lo(u + 2, i)
                            split_lo(u + 3, i)
                            hidden(c, i)
                            if b == 0:
                                job_units(q, (2,), i)
                                split_lo(u + 4, i)
                                hidden_lo(c, i)
                                job_units(q, (3,), i)
                            else:
                                split_lo(u + 4, i)
                                job_units(q + 1, (0,), i)
                                hidden_lo(c, i)
                                job_cols(q, i)
                                job_units(q + 1, (1,), i)
                    done += n
                split_lo(base + 3 * FCH + 1)
                name = f"ffn{layer}"
                dve.wait_ge(*seen("gate", name, 2))
                steps = [(c, t, 2 + 2 * c + t, seen("part", name, 2 * t + c + 1) if (t, c) != (1, 1) else (s_used, base + 3 * FCH))
                         for t in range(NT) for c in range(2)]
                residual(*steps[0])
                residual(*steps[1])
                tile_mean(("n_pw1", "n_final")[layer], 0, 2)
                if layer == 0:
                    tile_normed("n_pw1", 0)
                residual(*steps[2])
                return [steps[3]]

            left = ffn(0, [(4, 5)], 4, left)

            mod_cols(pc("mix_norm_g", KT, KT), 7)
            tile_operand("n_pw1", xfull, xT_hi, xT_lo, 6, AFTER_FFN, left, BASE["pw1"] + 2)
            dve.wait_ge(sem("u_zero"), 2)
            steps = [0]
            last_step = {}

            def conv_step(k, ins):
                ins.then_inc(sem("conv"), 1)
                steps[0] += 1
                last_step[k] = steps[0]

            def conv_taps(c):
                dve.wait_ge(sem("pw1_glu"), 2 * c + 2)
                for tap in range(CONV - PE_TAPS):
                    for k in (2 * c, 2 * c + 1):
                        src = u_pad[:, k, tap:tap + S]
                        w = pcol[:, COL["od_dw_w_a"] + tap * KT + k:][:, 0:1]
                        if tap == 0:
                            conv_step(k, dve.tensor_scalar(conv[:, k, :], src, w, pc("od_dw_b", k), ALU.mult, ALU.add))
                        else:
                            dve.wait_ge(sem("conv"), last_step[k])
                            conv_step(k, dve.scalar_tensor_tensor(out=conv[:, k, :], in0=src, scalar=w,
                                                                  in1=conv[:, k, :], op0=ALU.mult, op1=ALU.add))
                    if tap == (None, 12, 12, 4)[c]:
                        conv_whole(c - 1)

            def conv_whole(c):
                dve.wait_ge(sem("conv_pe"), c + 1)
                for k in (2 * c, 2 * c + 1):
                    dve.wait_ge(sem("conv"), last_step[k])
                    dve.tensor_tensor(conv[:, k, :], conv[:, k, :], bank[6][:, 256 * (k % 2):256 * (k % 2) + 256],
                                      ALU.add).then_inc(sem("conv_whole"), 1)

            for c in range(4):
                if c > 0:
                    split_lo(BASE["pw1"] + 2 * c + 2)
                split_lo(BASE["pw1"] + 2 * c + 3)
                for e in range(2):
                    k = 2 * c + e
                    dve.wait_ge(sem("pw1_sig"), k + 1)
                    dve.scalar_tensor_tensor(out=u_pad[:, k, PAD:PAD + S], in0=bank[4][:, 256 * e:256 * e + 256],
                                             scalar=pc("od_pw1_b", k), in1=sig[:, e, :], op0=ALU.add,
                                             op1=ALU.mult).then_inc(sem("pw1_glu"), 1)
                conv_taps(c)
            conv_whole(3)
            dve.wait_ge(sem("ln_mean_mm"), 1)
            link(dve.tensor_scalar(mean[:, :], bank[4][:, 0:S], 1.0 / D, None, ALU.mult))
            for k in range(KT):
                dve.wait_ge(sem("conv_whole"), k + 1)
                dve.tensor_tensor(conv[:, k, :], conv[:, k, :], mean[:, :], ALU.subtract).then_inc(sem("ln_xc"), 1)
            dve.wait_ge(sem("ln_var_mm"), 1)
            dve.tensor_copy(rln[:, :], bank[5][:, 0:S]).then_inc(sem("ln_var"), 1)
            dve.wait_ge(sem("ln_var_tr"), 1)
            dve.tensor_scalar(ms[:, 0:NT], bank[4][:, 0:S].rearrange("p (t s) -> p t s", t=NT)[:, :, 0], 1.0 / D, EPS,
                              ALU.mult, ALU.add).then_inc(sem("ms"), 1)
            dve.wait_ge(*seen("rstd", "ln", 1))
            for t in range(NT):
                dve.tensor_scalar(rln[:, t * P:t * P + P], ident[:, :], rstd[:, t:t + 1], None, ALU.mult).then_inc(sem("ln_diag"), 1)
            dve.wait_ge(sem("ln_row_mm"), 1)
            for k in range(KT):
                dve.wait_ge(sem("ln_xc"), k + 1)
                dve.tensor_tensor(csq[:, k, :], conv[:, k, :], bank[5][:, 0:S], ALU.mult).then_inc(sem("ln_norm"), 1)
            for k in range(KT):
                dve.wait_ge(*seen("hi", "ln", k + 1))
                dve.tensor_tensor(xT_lo[:, k, :], xfull[:, k, :], xT_hi[:, k, :].bitcast(F32),
                                  ALU.subtract).then_inc(sem("lo"), 1)
            gate_diag("pw2", mc(8))
            link(dve.tensor_tensor(b_col[:, :], mc(8), pc("od_pw2_b", 0, KT), ALU.mult))
            bg = bias_gate[:, :].rearrange("p (k f) -> p k f", k=KT)
            dve.tensor_tensor(bg, ident[:, :].unsqueeze(1).broadcast_to([P, KT, P]),
                              b_col[:, :].unsqueeze(2).broadcast_to([P, KT, P]), ALU.mult).then_inc(sem("diag"), 1)
            mod_cols(pc("ffn_norm_g", KT, KT), 10)
            left = dense_residual("pw2", "n_ffn1")
            left = ffn(1, [(10, 5)], 10, left)

            dve.wait_ge(*seen("gate", "final", 2))
            for t in range(NT):
                if t == 1:
                    residual(*left[0])
                    tile_mean("n_final", 1, 4)
                tile_normed("n_final", t)
                dve.wait_ge(*seen("xn", "n_final", t + 1))
                dve.tensor_tensor(x[:, t, :], xn[:, t, :], bias_gate[:, :], ALU.mult).then_inc(sem("x_final"), 1)
            tile_mean("n_rg", 0, 1)
            dve.wait_ge(sem("x_final"), NT)
            tile_normed("n_rg", 0)
            mod_cols(pc("norm_g_2", 0, KT), V_MOD0 + 1)
            tile_operand("n_rg", xfull, xT_hi, xT_lo, V_MOD0, AFTER_FFN, (), BASE["rg_in"] + 2, NT)
            dve.wait_ge(sem("ru_zero"), 1)
            base = BASE["rg_in"]

            def rg_scan(k):
                dve.wait_ge(sem("rg_b"), k + 1)
                dve.tensor_tensor_scan(uc[:, k, :], r_gate[:, k, :], i_gate[:, k, :], 0.0, ALU.mult,
                                       ALU.add).then_inc(sem("rg_h"), 1)

            for c in range(2):
                if c == 1:
                    split_lo(base + 4)
                job_units(15, (2 + c,))
                split_lo(base + 2 * c + 3)
                if c == 1:
                    job_cols(15)
                dve.wait_ge(sem("rg_turned"), 2 * c + 2)
                for tap in range(RG_CONV):
                    w = COL["rg_conv_w_2"] + tap * KT
                    for e in range(4):
                        k = 4 * c + e
                        src = ru_pad[:, k, tap:tap + S]
                        if tap == 0:
                            ins = dve.tensor_scalar(uc[:, k, :], src, pcol[:, w + k:w + k + 1], pc("rg_conv_b_2", k),
                                                    ALU.mult, ALU.add)
                        else:
                            dve.wait_ge(sem("rg_conv"), 4 * (RG_CONV * c + tap - 1) + e + 1)
                            ins = dve.scalar_tensor_tensor(out=uc[:, k, :], in0=src, scalar=pcol[:, w + k:w + k + 1],
                                                           in1=uc[:, k, :], op0=ALU.mult, op1=ALU.add)
                        ins.then_inc(sem("rg_conv"), 1)
            split_lo(base + 6)
            split_lo(base + 7)
            for k in range(KT):
                if k % 2 == 0:
                    dve.wait_ge(sem("rg_a2"), k // 2 + 1)
                else:
                    dve.wait_ge(sem("rg_a"), k + 1)
                    link(dve.tensor_tensor(y_full[:, k, :], r_gate[:, k, :], r_gate[:, k, :], ALU.mult))
                dve.scalar_tensor_tensor(out=b_seq[:, k, :], in0=y_full[:, k, :], scalar=1.0, in1=b_seq[:, k, :],
                                         op0=ALU.add, op1=ALU.mult).then_inc(sem("rg_m"), 1)
            split_lo(base + 8)
            dve.wait_ge(sem("rg_iu"), KT)
            for k in range(KT):
                dve.wait_ge(sem("rg_sqrt"), k + 1)
                dve.tensor_tensor(i_gate[:, k, :], i_gate[:, k, :], b_seq[:, k, :], ALU.mult).then_inc(sem("rg_b"), 1)
                if k >= 1:
                    rg_scan(k - 1)
            rg_scan(KT - 1)

            def rg_low(k):
                dve.wait_ge(*seen("hi", "rg", k + 1))
                dve.tensor_tensor(xT_lo[:, k, :], y_full[:, k, :], xT_hi[:, k, :].bitcast(F32),
                                  ALU.subtract).then_inc(sem("lo"), 1)

            for k in range(KT):
                dve.wait_ge(sem("rg_h"), k + 1)
                dve.wait_ge(*((sem("rg_g"), k // 2 + 1) if k < 4 else (sem("rg_turned"), 7 + (k - 4) // 2)))
                dve.tensor_tensor(y_full[:, k, :], uc[:, k, :], gT[:, k, :], ALU.mult).then_inc(sem("full"), 1)
                if k >= 1:
                    rg_low(k - 1)
            rg_low(KT - 1)
            split_lo(base + 9)
            gate_diag("rg_out", mc(V_MOD0 + 2))
            mod_cols(pc("kv_norm_g_2", 0, KT), V_KV + 1)
            left = dense_residual("rg_out", "n_kv")

            tile_operand("n_kv", kv_full, xT_hi, xT_lo, V_KV, AFTER_DENSE, left, BASE["kv"] + 2)
            for stage in ("kv", "att_in"):
                if stage == "att_in":
                    job_cols(16)
                    dve.wait_ge(s_cols, 17)
                    mod_cols(pc("norm_g_2", KT, KT), V_MOD1 + 1)
                    dve.wait_ge(s_used, BASE["att_in"])
                    full_lo("n_att", kv_full, xT_hi, xT_lo, bank[2:6], lambda k: a_col[:, k:k + 1],
                            lambda k: mc(V_MOD1, k, 1))
                for c in range(4 if stage == "kv" else 2):
                    if c > 0 or stage == "att_in":
                        split_lo(BASE[stage] + 2 * c + 2)
                    if stage == "kv" and c == 3:
                        job_units(17, (2,))
                    split_lo(BASE[stage] + 2 * c + 3)
                    if stage == "kv" and c < 3:
                        job_units(16 + c // 2, [(0, 1), (2, 3)][c % 2])
                    elif stage == "att_in" and c == 0:
                        job_units(17, (3,))
                    elif stage == "att_in":
                        job_cols(17)

            A_ITS = [(h, t) for h in range(A_HEADS) for t in range(NT)]

            def a_max(n):
                h, t = A_ITS[n]
                b = n % 2
                keys = (t + 1) * P
                dve.wait_ge(sem("a_s"), n + 1)
                link(dve.reduce_max(mx[:, b, 0:1], bank[2 + b][:, 0:keys], AX_X))
                dve.tensor_scalar(nb[:, b, 0:1], mx[:, b, 0:1], -float(P) ** -0.5, None, ALU.mult).then_inc(sem("a_nb"), 1)

            def a_out(n):
                h, t = A_ITS[n]
                b = n % 2
                dve.wait_ge(sem("a_pv"), n + 1)
                dve.tensor_scalar(ao[:, t, h * P:h * P + P], bank[6 + b][:, 0:P], rsum[:, b, 0:1], None,
                                  ALU.mult).then_inc(sem("a_o"), 1)

            split_lo(BASE["att_in"] + 6)
            a_max(0)
            for n in range(len(A_ITS)):
                if n + 1 < len(A_ITS):
                    a_max(n + 1)
                dve.wait_ge(sem("a_exp"), n + 1)
                if n >= 2:
                    dve.wait_ge(sem("a_o"), n - 1)
                link(dve.reciprocal(rsum[:, n % 2, 0:1], esum[:, n % 2, 0:1]))
                if n >= 1:
                    a_out(n - 1)
                if n in (2, 6, 10):
                    split_lo(BASE["att_in"] + {2: 7, 6: 8, 10: 9}[n])
            a_out(len(A_ITS) - 1)
            dve.wait_ge(sem("a_o"), len(A_ITS))
            for c in range(2):
                for t in range(NT):
                    cols = slice(512 * c, 512 * c + 512)
                    dve.wait_ge(sem("ag_silu"), 2 * c + t + 1)
                    dve.tensor_tensor(ao[:, t, cols], ao[:, t, cols], ag[:, t, cols], ALU.mult).then_inc(sem("ao_gated"), 1)
            for k in range(KT):
                dve.wait_ge(*seen("hi", "ao", k + 1))
                dve.tensor_tensor(xT_lo[:, k, :], bank[4 + k // 2][:, 256 * (k % 2):256 * (k % 2) + 256],
                                  xT_hi[:, k, :].bitcast(F32), ALU.subtract).then_inc(sem("lo"), 1)
            gate_diag("att_out", mc(V_MOD1 + 2))
            gate_diag("last", pc("final_norm_g_2", 0, KT), last_gate)
            left = dense_residual("att_out", "n_last")
            residual(*left[0])
            tile_mean("n_last", 1, 4)
            dve.wait_ge(*seen("gate", "last", 2))
            for t in range(NT):
                if t == 1:
                    tile_normed("n_last", 1)
                dve.wait_ge(*seen("xn", "n_last", t + 1))
                dve.tensor_tensor(xn[:, t, :], xn[:, t, :], last_gate[:, :], ALU.mult).then_inc(sem("result"), 1)

        @block.tensor
        def _(pe):
            def three(dst, hi, lo, whi, wlo, start, stop):
                pe.matmul(dst, hi, whi, start=start, stop=False)
                pe.matmul(dst, hi, wlo, start=False, stop=False)
                return pe.matmul(dst, lo, whi, start=False, stop=stop)

            def unit_wait(u, i=None):
                pe.wait_ge(s_lo, at(u + 1, i, 6))

            def half(u, j, hi, lo, banks, last=None, ready=None, ts=range(NT), ks=range(4), part=False):
                wh = w_hi[u % N_SPLIT][:, :].rearrange("p (k n) -> p k n", k=4)
                wl = w_lo[u % N_SPLIT][:, :].rearrange("p (k n) -> p k n", k=4)
                for t in ts:
                    for k in ks:
                        if ready is not None and ADDS[ready]["lo"] == NT * KT:
                            pe.wait_ge(*seen("lo", ready, KT * t + 4 * j + k + 1))
                        elif ready is not None and t == 0:
                            pe.wait_ge(*seen("lo", ready, min(4 * j + k + 1, ADDS[ready]["lo"])))
                        kt = 4 * j + k
                        ins = three(banks[t][:, :], hi[:, kt, t * P:t * P + P], lo[:, kt, t * P:t * P + P],
                                    wh[:, k, :], wl[:, k, :], kt == 0, kt == KT - 1)
                    if part and j == 1 and t == 0:
                        ins.then_inc(sem("part"), 1)
                if last is not None:
                    ins.then_inc(last, 1)
                return ins

            def turn_norm(stage, src, banks):
                pe.wait_ge(*seen("xn", stage, NT))
                for k in range(KT):
                    for t in range(NT):
                        pe.transpose(banks[k // 2][:, 256 * (k % 2) + t * P:256 * (k % 2) + t * P + P],
                                     src[:, t, k * P:k * P + P], ident[:, :]).then_inc(sem("tr"), 1)

            def turn_tile(stage, t, banks):
                pe.wait_ge(*seen("xn", stage, t + 1))
                for k in range(KT):
                    pe.transpose(bank[banks[t][k // 4]][:, P * (k % 4):P * (k % 4) + P],
                                 xn[:, t, k * P:k * P + P], ident[:, :]).then_inc(sem("tr"), 1)

            def first_chunk(stage, u, banks, turned=False):
                if not turned:
                    turn_tile(stage, 0, banks)
                for j in range(2):
                    unit_wait(u + j)
                    half(u + j, j, xT_hi, xT_lo, bank[0:2], None, stage, (0,))
                turn_tile(stage, 1, banks)
                for j in range(2):
                    half(u + j, j, xT_hi, xT_lo, bank[0:2], s_used, stage, (1,))

            def gate_mm(stage, src=None, b=4):
                src = gate if src is None else src
                pe.wait_ge(*seen("diag", stage, 1))
                for h in range(2):
                    ins = pe.matmul(bank[b + h][:, :], ones[:, :], src[:, 512 * h:512 * h + 512], start=True, stop=True)
                ins.then_inc(sem("gmm"), 1)

            def gate_mid(stage):
                def mid():
                    gate_mm(stage)
                    if stage == "pw2":
                        gate_mm("pw2b", bias_gate, 6)
                    if stage == "att_out":
                        gate_mm("last", last_gate, 6)
                return mid

            def job_reduce(q, i=None):
                pe.wait_ge(s_step, at(8 * q + 8, i, 8))
                if q >= 1:
                    pe.wait_ge(s_cols, at(q, i, 1))
                for k in range(KT):
                    ins = pe.matmul(COLS[:, k:k + 1], job_sum[:, k * P:k * P + P], ones[:, 0:1], start=True, stop=True)
                ins.then_inc(s_red, 1)

            pe.wait_ge(sem("ident_in"), 16)
            pe.wait_ge(sem("ones"), 2)

            def turn_rows(g):
                pe.wait_ge(sem(f"prow{g}"), 16 * len(ROW_GROUPS[g]))
                n = sum(k for _, k in ROW_GROUPS[g])
                if g == 4:
                    pe.wait_ge(sem("cols_in"), 1)
                pe.transpose(bank[4 + g % 4][:, 0:n], prow[0:n, g, :], ident[0:n, 0:n]).then_inc(sem("prow_tr"), 1)

            turn_rows(0)
            pe.wait_ge(sem("silu_c"), 1)
            for n in range(ADA0):
                pe.wait_ge(landed[n % N_LAND], 32 * (n // N_LAND + 1))
                w = w_land[n % N_LAND][:, :].rearrange("p (k n) -> p k n", k=2)
                for e in range(2):
                    kt = 2 * (n % 4) + e
                    for h in range(2):
                        ins = pe.matmul(bank[2 * (n // 4) + h][0:2, :], silu_c[:, 0:2, kt],
                                        w[:, e, 512 * h:512 * h + 512], start=kt == 0, stop=kt == KT - 1)
                ins.then_inc(sem("ada0_used"), 1)
                if n == 5:
                    for g in range(1, 5):
                        turn_rows(g)
                if n == 6:
                    pe.wait_ge(sem("cols_in"), 5)
                    turn_norm("n_x", xn, bank[4:8])
            pe.wait_ge(sem("ada0_rows"), 4)
            for n in range(2 * KT):
                pe.transpose(bank[0][:, 2 * n:2 * n + 2], ada_rows[0:2, n * P:n * P + P], ident[0:2, 0:2]).then_inc(sem("ada0_tr"), 1)

            def turn_heads(c):
                nh = 4 if c % 2 == 0 else 2
                rot_need = {0: 4, 1: 8, 2: 12, 3: 16}[c]
                for src in range(1 if c < 2 else 2):
                    for t in range(NT):
                        n = turned[0]
                        turned[0] += 1
                        if src == 0:
                            pe.wait_ge(sem("rot"), rot_need - 2 * (1 - t))
                        else:
                            pe.wait_ge(sem("in_act"), {2: t + 1, 3: 2 + 2 * t + 1}[c])
                        if n >= 2:
                            pe.wait_ge(sem("turn_out"), n - 1)
                        buf = rot if src == 0 else k_ctx
                        for h in range(nh):
                            ins = pe.transpose(bank[(4, 6)[n % 2]][:, h * P:h * P + P], buf[:, t, h * P:h * P + P], ident[:, :])
                        ins.then_inc(sem("turn"), 1)

            turned = [0]
            bank_read = [[("ada0_cols", 2)], [], [("rot", 4)], [("rot", 8), ("f_tok", 2)], [("rot", 12)],
                         [("in_act", 2)], [("rot", 16), ("v_lat", 2)], [("in_act", 6)]]
            events = [[(0, 0)], [(1, 2)], [(2, 0), (3, 2)], [(4, 0), (5, 2)], [(6, 0), (7, 2)]]
            for c in range(5):
                for side, (event, b) in enumerate(events[c]):
                    for name, n in bank_read[event]:
                        pe.wait_ge(sem(name), n)
                    for j in range(2):
                        u = 2 * c + j
                        if side == 0:
                            unit_wait(u)
                        hi, lo = (xT_hi, xT_lo) if side == 0 else (ctxT_hi, ctxT_lo)
                        if c == 2 and side == 1 and j == 0:
                            pe.wait_ge(*seen("lo", "n_ctx", KT))
                        last = s_used if side == len(events[c]) - 1 else None
                        ins = half(u, j, hi, lo, bank[b:b + 2], last, "n_x" if c == 0 else None)
                    if last is None:
                        ins.then_inc(sem("in_lat"), 1)
                    if c == 1:
                        pe.wait_ge(*seen("full", "n_ctx", KT))
                    if c >= 1 and side == 0:
                        turn_heads(c - 1)
                    if c >= 3 and side == 0:
                        job_reduce(c - 3)
                if c == 0:
                    pe.wait_ge(sem("four_in"), 16 * 5)
                    for m in range(2):
                        for f in range(2):
                            ins = pe.matmul(bank[2][:, 256 * m + P * f:256 * m + P * f + P], four_c[:, m, :], four_w[:, f, :],
                                            start=True, stop=True)
                    ins.then_inc(sem("four_gmm"), 1)
                    turn_norm("n_ctx", ctx_x, bank[4:8])
                    pe.wait_ge(sem("four_gs"), 1)

            pe.wait_ge(sem("dft_in"), 16)
            pe.wait_ge(sem("f_tok"), 2)
            pe.wait_ge(sem("turn_out"), 12)
            for f in range(2):
                for t in range(NT):
                    ins = pe.matmul(bank[4 + f][:, :], f_tok[:, t, f * P:f * P + P], dft[:, t, :], start=t == 0, stop=t == NT - 1)
                ins.then_inc(sem("four_ft"), 1)

            ITS = [(h, t) for h in range(HEADS) for t in range(NT)]

            def scores(n):
                h, t = ITS[n]
                b = n % 2
                if n >= 2:
                    pe.wait_ge(sem("d_exp"), 2 * (n - 1))
                for c in range(2):
                    pe.matmul(bank[2 * b + c][:, :], qT[64 * c:64 * c + 64, h, t * P:t * P + P],
                              kT[64 * c:64 * c + 64, h, :], start=True, stop=True).then_inc(sem("d_s"), 1)

            def turn_diff(n):
                pe.wait_ge(sem("d_diff"), n + 1)
                if n >= 2:
                    pe.wait_ge(sem("d_diffT"), n - 1)
                for k in range(4):
                    ins = pe.transpose(bank[4 + n % 2][:, k * P:k * P + P], diff[:, n % 2, k * P:k * P + P], ident[:, :])
                ins.then_inc(sem("d_turn"), 1)

            def diff_v(n):
                h, t = ITS[n]
                pe.wait_ge(sem("d_diffT"), n + 1)
                if n >= 2:
                    pe.wait_ge(sem("d_o"), n - 1)
                for k in range(4):
                    ins = pe.matmul(bank[6 + n % 2][:, 0:P], diffT[:, n % 2, k, :], v_tok[:, k, h * P:h * P + P],
                                    start=k == 0, stop=k == 3)
                ins.then_inc(sem("d_pv"), 1)

            pe.wait_ge(sem("in_act"), 10)
            pe.wait_ge(sem("v_lat"), 2)
            scores(0)
            scores(1)
            pe.wait_ge(sem("four_fts"), 2)
            for f in range(2):
                for n in range(2):
                    ins = pe.matmul(bank[6][:, 256 * f:256 * f + 256], four_g[:, n, f, :],
                                    ftT[:, f, 256 * n:256 * n + 256], start=n == 0, stop=n == 1)
            ins.then_inc(sem("four_y"), 1)
            job_reduce(2)
            for n in range(len(ITS)):
                if n + 2 < len(ITS):
                    scores(n + 2)
                turn_diff(n)
                if n == 1:
                    pe.wait_ge(sem("four_lo"), 2)
                if n == 2:
                    pe.wait_ge(s_cols, 3)
                if n >= 1:
                    diff_v(n - 1)
            diff_v(len(ITS) - 1)
            pe.wait_ge(*seen("xn", "sub", NT))
            for h in range(HEADS):
                for t in range(NT):
                    pe.transpose(bank[2 + h // 2][:, 256 * (h % 2) + t * P:256 * (h % 2) + t * P + P],
                                 o_tok[:, t, h * P:h * P + P], ident[:, :]).then_inc(sem("tr"), 1)

            def dense(stage, n_chunks, ready=None, after=None, before=None, parts=True, job=(), turn_banks=None,
                      norm_after=None, mid=None):
                for c in range(n_chunks):
                    if before is not None:
                        before(c)
                    u = BASE[stage] + 2 * c
                    banks = bank[2 * (c % 2):2 * (c % 2) + 2]
                    if c == 0 and turn_banks is not None:
                        first_chunk(ready, u, turn_banks, turn_banks == AFTER_DENSE)
                    elif c == 1 and parts and n_chunks == 2:
                        for t in range(NT):
                            for j in range(2):
                                if t == 0:
                                    unit_wait(u + j)
                                last = s_used if t == 1 else None
                                if (t, j) != (1, 1) or norm_after is None:
                                    half(u + j, j, xT_hi, xT_lo, banks, last, None, (t,), part=True)
                                else:
                                    half(u + 1, 1, xT_hi, xT_lo, banks, None, None, (1,), (0, 1))
                                    turn_tile(norm_after, 0, AFTER_DENSE)
                                    half(u + 1, 1, xT_hi, xT_lo, banks, last, None, (1,), (2, 3))
                    else:
                        for j in range(2):
                            unit_wait(u + j)
                            half(u + j, j, xT_hi, xT_lo, banks, s_used, ready if c == 0 else None,
                                 part=parts and n_chunks == 2)
                            if (c, j) == (0, 0) and mid is not None:
                                mid()
                            if (c, j) == job[:2]:
                                job_reduce(job[2])
                    if after is not None:
                        after(c)

            dense("out", 2, "sub", mid=gate_mid("out"), norm_after="n_ffn0")

            def ffn(layer, loops, first_job):
                base = BASE[f"ffn{layer}"]
                off = layer * FCH

                def up(c, u, i=None):
                    for j in range(2):
                        unit_wait(u + j, i)
                        half(u + j, j, xT_hi, xT_lo, bank[0:2], s_used)

                def down(c, u, i=None, last=False):
                    unit_wait(u, i)
                    pe.wait_ge(sem("hT_lo"), at(off + c + 1, i, 2))
                    wh = w_hi[u % N_SPLIT][:, :].rearrange("p (k n) -> p k n", k=2)
                    wl = w_lo[u % N_SPLIT][:, :].rearrange("p (k n) -> p k n", k=2)
                    order = [(k, h, t) for k in range(2) for h in range(2) for t in range(NT)]
                    if last:
                        order = [(k, h, t) for t in range(NT) for h in range(2) for k in range(2)]
                    for n, (k, h, t) in enumerate(order):
                        ins = three(bank[2 + 2 * h + t][:, :], hT_hi[:, k, t * P:t * P + P],
                                    hT_lo[:, k, t * P:t * P + P], wh[:, k, 512 * h:512 * h + 512],
                                    wl[:, k, 512 * h:512 * h + 512], False, last and k == 1)
                        if last and n in (1, 3, 5):
                            ins.then_inc(sem("part"), 1)
                    ins.then_inc(s_used, 1)

                def turn_hidden(c, i=None):
                    pe.wait_ge(sem("hid"), at(2 * (off + c) + 2, i, 4))
                    if c >= 1 or layer:
                        pe.wait_ge(sem("hT_lo"), at(off + c, i, 2))
                    for t in range(NT):
                        for k in range(2):
                            ins = pe.transpose(bank[6][:, 256 * k + t * P:256 * k + t * P + P],
                                               hid[:, t, k * P:k * P + P], ident[:, :])
                    ins.then_inc(sem("h_turn"), 1)

                first_chunk(f"n_ffn{layer}", base, AFTER_DENSE, True)
                job_reduce(first_job - 1)
                turn_hidden(0)
                pe.wait_ge(sem("zeros"), layer + 1)
                for n in range(4):
                    pe.matmul(bank[2 + n][:, :], zeros[0:1, 0:P], zeros[0:1, :], start=True, stop=False)
                done = 0
                for q, n in loops:
                    with pe.Fori(0, n) as i:
                        for b in range(2):
                            u = base + 2 + 6 * done + 3 * b
                            c = 1 + 2 * done + b
                            up(c, u, i)
                            if b == 1:
                                job_reduce(q, i)
                            down(c - 1, u + 2, i)
                            turn_hidden(c, i)
                    done += n
                pe.wait_ge(sem("hid"), 2 * (off + FCH))
                gate_mm(f"ffn{layer}", b=0)
                down(FCH - 1, base + 3 * FCH - 1, None, True)
                if layer == 1:
                    pe.wait_ge(*seen("gate", "ffn1", 2))
                    gate_mm("final", bias_gate, 0)

            ffn(0, [(4, 5)], 4)

            def turn_pair(stage, src, free):
                def after(c):
                    pe.wait_ge(sem(f"{stage}_tok"), 2 * c + 2)
                    if c >= 1:
                        free(c)
                    for g in range(2):
                        for k in range(2):
                            for t in range(NT):
                                ins = pe.transpose(bank[4 + g][:, 256 * k + t * P:256 * k + t * P + P],
                                                   src[:, t, 256 * g + k * P:256 * g + k * P + P], ident[:, :])
                    ins.then_inc(sem(f"{stage}_turn"), 1)
                return after

            def pw1_free(c):
                pe.wait_ge(sem("pw1_glu"), 2 * c)

            def pw1_after(c):
                turn_pair("pw1", ag_tok, pw1_free)(c)
                if c >= 1:
                    conv_diag(c - 1)

            def conv_diag(c):
                pe.wait_ge(sem("pw1_glu"), 2 * c + 2)
                if c >= 1:
                    pe.wait_ge(sem("conv_whole"), 2 * c)
                for e in range(2):
                    for n in range(PE_TAPS):
                        pe.wait_ge(sem("tap_diag"), (2 * c + e) * PE_TAPS + n + 1)
                        tap = CONV - PE_TAPS + n
                        ins = pe.matmul(bank[6][:, 256 * e:256 * e + 256], tap_diag[e][:, n, :],
                                        u_pad[:, 2 * c + e, tap:tap + S], start=n == 0, stop=n == PE_TAPS - 1)
                ins.then_inc(sem("conv_pe"), 1)

            dense("pw1", 4, "n_pw1", pw1_after, turn_banks=AFTER_FFN)
            conv_diag(3)
            for k in range(KT):
                pe.wait_ge(sem("conv_whole"), k + 1)
                if k == 0:
                    pe.wait_ge(sem("pw1_glu"), KT)
                ins = pe.matmul(bank[4][:, 0:S], ones[:, :], conv[:, k, :], start=k == 0, stop=k == KT - 1)
            ins.then_inc(sem("ln_mean_mm"), 1)
            for k in range(KT):
                pe.wait_ge(sem("ln_sq"), k + 1)
                ins = pe.matmul(bank[5][:, 0:S], ones[:, :], csq[:, k, :], start=k == 0, stop=k == KT - 1)
            ins.then_inc(sem("ln_var_mm"), 1)
            pe.wait_ge(sem("ln_var"), 1)
            for t in range(NT):
                ins = pe.transpose(bank[4][:, t * P:t * P + P], rln[:, t * P:t * P + P], ident[:, :])
            ins.then_inc(sem("ln_var_tr"), 1)
            pe.wait_ge(sem("ln_diag"), 2)
            pe.matmul(bank[5][:, 0:S], ones[:, :], rln[:, :], start=True, stop=True).then_inc(sem("ln_row_mm"), 1)
            dense("pw2", 2, "ln", mid=gate_mid("pw2"), norm_after="n_ffn1")
            ffn(1, [(10, 5)], 10)


            def rg_gate_mm(g):
                n, h = RG_GROUPS[g]
                if g in (0, 2):
                    pe.wait_ge(sem(f"rg_w{n}"), 16)
                if g >= 2:
                    pe.wait_ge(sem("rg_sig"), 2 * (g - 1))
                pe.wait_ge(sem("rg_conv"), RG_CONV * 4 * (h // 2 + 1))
                for e in range(2):
                    for k in range(2):
                        ins = pe.matmul(bank[6 + g % 2][:, 256 * e:256 * e + 256], rg_w[n][:, h, k, P * e:P * e + P],
                                        uc[:, 2 * h + k, :], start=k == 0, stop=k == 1)
                ins.then_inc(sem("rg_gates"), 1)

            def rg_free(c):
                pe.wait_ge(sem("rg_turned"), 2 * c)

            for c in range(4):
                if c == 0:
                    first_chunk("n_rg", BASE["rg_in"], AFTER_FFN)
                for j in range(2 if c else 0):
                    u = BASE["rg_in"] + 2 * c + j
                    unit_wait(u)
                    for t in range(NT):
                        half(u, j, xT_hi, xT_lo, bank[2 * (c % 2):2 * (c % 2) + 2], s_used if t == 1 else None,
                             None, (t,))
                        for g in {(2, 0, 1): (2, 3), (2, 1, 0): (4, 5), (2, 1, 1): (6, 7)}.get((c, j, t), ()):
                            rg_gate_mm(g)
                    if (c, j) == (1, 1):
                        job_reduce(15)
                turn_pair("rg_in", rg_tok, rg_free)(c)
                if c == 1:
                    pe.wait_ge(s_cols, 16)
                    rg_gate_mm(0)
                    rg_gate_mm(1)
            pe.wait_ge(sem("rg_in_tok"), 8)
            pe.wait_ge(sem("rg_turned"), 8)
            pe.wait_ge(sem("rg_sig"), 2 * KT)
            dense("rg_out", 2, "rg", mid=gate_mid("rg_out"), norm_after="n_kv")


            def attn_after(stage):
                def after(c):
                    if c >= 2:
                        return
                    for t in range(NT):
                        n = 2 * c + t
                        pe.wait_ge(sem(f"{stage}_tok"), n + 1)
                        if n >= 2:
                            pe.wait_ge(sem(f"{stage}_turned"), n - 1)
                        for h in range(4):
                            ins = pe.transpose(bank[4 + n % 2][:, h * P:h * P + P], a_tok[:, t, h * P:h * P + P], ident[:, :])
                        ins.then_inc(sem(f"{stage}_turn"), 1)
                return after

            def rows_read(stage):
                def before(c):
                    if c == 2:
                        pe.wait_ge(sem(f"{stage}_tok"), 2)
                    if c == 3:
                        pe.wait_ge(sem(f"{stage}_tok"), 4)
                return before

            dense("kv", 4, "n_kv", attn_after("kv"), rows_read("kv"), job=(2, 0, 16), turn_banks=AFTER_DENSE)
            pe.wait_ge(sem("kv_turned"), 4)
            pe.wait_ge(sem("kv_rows"), 4)
            for k in range(KT):
                for t in range(NT):
                    pe.transpose(bank[2 + k // 2][:, 256 * (k % 2) + t * P:256 * (k % 2) + t * P + P],
                                 xn[:, t, k * P:k * P + P], ident[:, :]).then_inc(sem("tr"), 1)
            dense("att_in", 2, "n_att", attn_after("att_in"), parts=False, job=(1, 0, 17))

            A_ITS = [(h, t) for h in range(A_HEADS) for t in range(NT)]

            def a_scores(n):
                h, t = A_ITS[n]
                if n == 0:
                    pe.wait_ge(sem("mask_in"), 16)
                if n >= 2:
                    pe.wait_ge(sem("a_exp"), n - 1)
                s_bank = bank[2 + n % 2]
                pe.matmul(s_bank[:, 0:(t + 1) * P], aqT[:, h, t * P:t * P + P], akT[:, h, 0:(t + 1) * P],
                          start=True, stop=False)
                pe.matmul(s_bank[:, t * P:(t + 1) * P], ident[:, :], mask[:, :], start=False, stop=True).then_inc(sem("a_s"), 1)

            def a_turn(n):
                h, t = A_ITS[n]
                pe.wait_ge(sem("a_exp"), n + 1)
                if n >= 2:
                    pe.wait_ge(sem("a_apT"), n - 1)
                for k in range(t + 1):
                    ins = pe.transpose(bank[4 + n % 2][:, k * P:k * P + P], ap_[:, n % 2, k * P:k * P + P], ident[:, :])
                ins.then_inc(sem("a_turn"), 1)

            def a_v(n):
                h, t = A_ITS[n]
                pe.wait_ge(sem("a_apT"), n + 1)
                if n >= 2:
                    pe.wait_ge(sem("a_o"), n - 1)
                for k in range(t + 1):
                    ins = pe.matmul(bank[6 + n % 2][:, 0:P], apT[:, n % 2, k, :], av[:, k, h * P:h * P + P],
                                    start=k == 0, stop=k == t)
                ins.then_inc(sem("a_pv"), 1)

            def gate_group(g):
                c, j, t, e = 2 + g // 8, g // 4 % 2, g // 2 % 2, g % 2
                u = BASE["att_in"] + 2 * c + j
                if g == 0:
                    pe.wait_ge(sem("att_in_tok"), 2)
                if g == 8:
                    pe.wait_ge(sem("att_in_rows"), 2)
                if g % 4 == 0:
                    unit_wait(u)
                half(u, j, xT_hi, xT_lo, bank[0:2], s_used if g % 4 == 3 else None, None, (t,), (2 * e, 2 * e + 1))

            def attend(n):
                if n + 2 < len(A_ITS):
                    a_scores(n + 2)
                a_turn(n)
                if n >= 1:
                    a_v(n - 1)

            gate_group(0)
            gate_group(1)
            pe.wait_ge(sem("att_in_turned"), 4)
            pe.wait_ge(s_cols, 18)
            a_scores(0)
            a_scores(1)
            for g in range(2, 16):
                gate_group(g)
                attend(g - 2)
            attend(14)
            attend(15)
            a_v(len(A_ITS) - 1)
            pe.wait_ge(sem("a_o"), len(A_ITS))
            for k in range(KT):
                pe.wait_ge(sem("ao_gated"), 2 * (k // 4) + 2)
                for t in range(NT):
                    pe.transpose(bank[4 + k // 2][:, 256 * (k % 2) + t * P:256 * (k % 2) + t * P + P],
                                 ao[:, t, k * P:k * P + P], ident[:, :]).then_inc(sem("tr"), 1)
            pe.wait_ge(sem("att_in_rows"), 4)
            dense("att_out", 2, "ao", mid=gate_mid("att_out"))


CONSTS = ("k_ident", "k_rope", "k_dft", "k_dft64", "k_mask")


def constants():
    import numpy as np

    ident = np.eye(P, dtype=np.float32)
    grid_w = 64
    inv = np.float32(10000.0) ** (-np.arange(0, 32, 2, dtype=np.float32) / np.float32(32))
    row = np.repeat(np.arange(S // grid_w, dtype=np.float32), grid_w)
    col = np.tile(np.arange(grid_w, dtype=np.float32), S // grid_w)
    ang = np.concatenate([row[:, None] * inv, col[:, None] * inv], axis=-1).astype(np.float32)
    rope = np.stack([np.cos(ang), np.sin(ang)], axis=1).astype(np.float32)
    n = np.arange(S)
    a = 2 * np.pi * ((n[:, None] * n[None, :]) % S) / S
    dft = np.concatenate([np.cos(a), np.sin(a)], axis=1).astype(np.float32)
    m = np.arange(64)
    b = 2 * np.pi * ((m[:, None] * m[None, :]) % 64) / 64
    norm = 1.0 / np.sqrt(S * 64)
    d64 = np.zeros((2, P, P), np.float32)
    for g in range(2):
        r = slice(64 * g, 64 * g + 64)
        d64[0, r, r] = np.cos(b) * norm
        d64[1, r, r] = -np.sin(b) * norm
    mask = np.where(np.arange(P)[None, :] <= np.arange(P)[:, None], 0.0, NEG).astype(np.float32)
    return {"k_ident": ident, "k_rope": rope, "k_dft": dft, "k_dft64": d64, "k_mask": mask}


def kernel(**inputs):
    import numpy as np
    import concourse.bacc as bacc
    from concourse.bass_utils import run_bass_kernel_spmd

    nc = bacc.Bacc("TRN2", target_bir_lowering=False, num_devices=1)
    arrays, tensors = {}, {}
    for name, a in {**inputs, **constants()}.items():
        a = np.ascontiguousarray(a)
        arrays[name + "_dram"] = a
        tensors[name] = nc.dram_tensor(name + "_dram", a.shape, mybir.dt.from_np(a.dtype), kind="ExternalInput").ap()
    out = nc.dram_tensor("out_dram", (1, S, D), F32, kind="ExternalOutput").ap()
    build(nc, tensors, out)
    return run_bass_kernel_spmd(nc, [arrays], core_ids=[0]).results[0]["out_dram"]
```
